# Optimizing a Trainium2 kernel written in Bass

```python
import math
import jax, jax.numpy as jnp
from jax import lax
import numpy as np

D_MODEL = 1024
BATCH = 1
SEQ = 512
DEPTH = 1

CHUNK = 64
MIX_WIDTH = D_MODEL
LRU_WIDTH = MIX_WIDTH // 2
ATT_WIDTH = MIX_WIDTH - LRU_WIDTH
LRU_BLOCKS = 8
LRU_BLOCK_W = LRU_WIDTH // LRU_BLOCKS
CONV_W = 4
LRU_C = 8.0
ATT_HEADS = 8
ATT_HEAD_DIM = ATT_WIDTH // ATT_HEADS
Q_BLOCK = 128
D_FF = -(-8 * D_MODEL // (3 * 256)) * 256
IN_COLS = 2 * LRU_WIDTH + 3 * ATT_WIDTH
EPS = 1e-6


def rms_norm(x, g):
    xf = x.astype(jnp.float32)
    xf = xf * lax.rsqrt(jnp.mean(xf * xf, axis=-1, keepdims=True) + EPS)
    return xf.astype(x.dtype) * g

def causal_depthwise_conv(x, w, b):
    s = x.shape[1]
    xp = jnp.pad(x, ((0, 0), (CONV_W - 1, 0), (0, 0)))
    y = b
    for i in range(CONV_W):
        y = y + xp[:, i:i + s, :] * w[i]
    return y

def block_diag_linear(x, w, b):
    bsz, s, _ = x.shape
    xb = x.reshape(bsz, s, LRU_BLOCKS, LRU_BLOCK_W)
    y = jnp.einsum('bsnc,ncd->bsnd', xb, w) + b
    return y.reshape(bsz, s, LRU_WIDTH)

def rg_lru(x, w_rg, b_rg, w_ig, b_ig, lam):
    r = jax.nn.sigmoid(block_diag_linear(x, w_rg, b_rg).astype(jnp.float32))
    i = jax.nn.sigmoid(block_diag_linear(x, w_ig, b_ig).astype(jnp.float32))
    log_a = -LRU_C * r * jax.nn.softplus(-lam.astype(jnp.float32))
    a = jnp.exp(log_a)
    mult = jnp.sqrt(-jnp.expm1(2.0 * log_a))
    bterm = mult * (i * x.astype(jnp.float32))

    def combine(e1, e2):
        a1, b1 = e1
        a2, b2 = e2
        return a1 * a2, a2 * b1 + b2

    _, h = lax.associative_scan(combine, (a, bterm), axis=1)
    return h.astype(x.dtype)

def stick_breaking_attention(q, k, v):
    bsz, s, h, dh = q.shape
    nb = s // Q_BLOCK
    scale = 1.0 / math.sqrt(dh)
    qb = q.reshape(bsz, nb, Q_BLOCK, h, dh).transpose(1, 0, 2, 3, 4)
    key_pos = jnp.arange(s)

    def one_block(args):
        q_blk, blk = args
        z = jnp.einsum('bqhd,bkhd->bhqk', q_blk, k).astype(jnp.float32) * scale
        t = blk * Q_BLOCK + jnp.arange(Q_BLOCK)
        mask = key_pos[None, :] < t[:, None]
        log_beta = jax.nn.log_sigmoid(z)
        log_1mb = jnp.where(mask, jax.nn.log_sigmoid(-z), 0.0)
        suffix = lax.cumsum(log_1mb, axis=3, reverse=True) - log_1mb
        att = jnp.where(mask, jnp.exp(log_beta + suffix), 0.0)
        return jnp.einsum('bhqk,bkhd->bqhd', att.astype(v.dtype), v)

    out = lax.map(one_block, (qb, jnp.arange(nb)))
    return out.transpose(1, 0, 2, 3, 4).reshape(bsz, s, h, dh)

def first_inputs(seed: int = 0) -> dict:
    key = jax.random.key(seed)
    ks = jax.random.split(key, 20)
    f32 = jnp.float32
    nrm = lambda k, shp, sc: jax.random.normal(k, shp, f32) * sc
    gain = lambda k, shp: 1.0 + 0.05 * jax.random.normal(k, shp, f32)
    x = jax.random.normal(ks[0], (BATCH, SEQ, D_MODEL), f32)
    u = jax.random.uniform(ks[9], (DEPTH, LRU_WIDTH), f32, 0.9, 0.999)
    a0 = u ** (1.0 / LRU_C)
    lru_lambda = jnp.log(a0) - jnp.log1p(-a0)
    return {
        "x": x,
        "norm_mix": gain(ks[1], (DEPTH, D_MODEL)),
        "w_in": nrm(ks[2], (DEPTH, D_MODEL, IN_COLS), D_MODEL ** -0.5),
        "conv_w": nrm(ks[3], (DEPTH, CONV_W, LRU_WIDTH), CONV_W ** -0.5),
        "conv_b": nrm(ks[4], (DEPTH, LRU_WIDTH), 0.01),
        "w_rg": nrm(ks[5], (DEPTH, LRU_BLOCKS, LRU_BLOCK_W, LRU_BLOCK_W), LRU_BLOCK_W ** -0.5),
        "b_rg": nrm(ks[6], (DEPTH, LRU_BLOCKS, LRU_BLOCK_W), 0.01),
        "w_ig": nrm(ks[7], (DEPTH, LRU_BLOCKS, LRU_BLOCK_W, LRU_BLOCK_W), LRU_BLOCK_W ** -0.5),
        "b_ig": nrm(ks[8], (DEPTH, LRU_BLOCKS, LRU_BLOCK_W), 0.01),
        "lru_lambda": lru_lambda,
        "norm_lru_out": gain(ks[10], (DEPTH, LRU_WIDTH)),
        "norm_att_out": gain(ks[11], (DEPTH, ATT_WIDTH)),
        "w_out": nrm(ks[12], (DEPTH, MIX_WIDTH, D_MODEL), MIX_WIDTH ** -0.5),
        "norm_ffn": gain(ks[13], (DEPTH, D_MODEL)),
        "w_ffn_in": nrm(ks[14], (DEPTH, D_MODEL, 2 * D_FF), D_MODEL ** -0.5),
        "w_ffn_out": nrm(ks[15], (DEPTH, D_FF, D_MODEL), D_FF ** -0.5),
        "norm_final": gain(ks[16], (D_MODEL,)),
    }

def first_block(x, norm_mix, w_in, conv_w, conv_b, w_rg, b_rg, w_ig, b_ig, lru_lambda,
              norm_lru_out, norm_att_out, w_out, norm_ffn, w_ffn_in, w_ffn_out, norm_final):
    bsz, s, _ = x.shape
    for l in range(DEPTH):
        h = rms_norm(x, norm_mix[l])
        u = jnp.einsum('bsd,de->bse', h, w_in[l])
        o = 0
        lru_x = u[..., o:o + LRU_WIDTH]; o += LRU_WIDTH
        lru_g = u[..., o:o + LRU_WIDTH]; o += LRU_WIDTH
        q = u[..., o:o + ATT_WIDTH].reshape(bsz, s, ATT_HEADS, ATT_HEAD_DIM); o += ATT_WIDTH
        k = u[..., o:o + ATT_WIDTH].reshape(bsz, s, ATT_HEADS, ATT_HEAD_DIM); o += ATT_WIDTH
        v = u[..., o:o + ATT_WIDTH].reshape(bsz, s, ATT_HEADS, ATT_HEAD_DIM)

        xc = causal_depthwise_conv(lru_x, conv_w[l], conv_b[l])
        hl = rg_lru(xc, w_rg[l], b_rg[l], w_ig[l], b_ig[l], lru_lambda[l])
        y_lru = jax.nn.gelu(lru_g) * hl

        y_att = stick_breaking_attention(q, k, v).reshape(bsz, s, ATT_WIDTH)

        y = jnp.concatenate([rms_norm(y_lru, norm_lru_out[l]),
                             rms_norm(y_att, norm_att_out[l])], axis=-1)
        x = x + jnp.einsum('bse,ed->bsd', y, w_out[l])

        h2 = rms_norm(x, norm_ffn[l])
        gu = jnp.einsum('bsd,df->bsf', h2, w_ffn_in[l])
        x = x + jnp.einsum('bsf,fd->bsd', jax.nn.silu(gu[..., :D_FF]) * gu[..., D_FF:], w_ffn_out[l])
    return rms_norm(x, norm_final)


GRID_W = 64
HEAD_DIM = 64
NA_HEADS = 8
NA_KH_MAX = 8
NA_KW = 16
NA_QBLK = 16
NA_BAND = 2 * NA_KW
NA_W = NA_HEADS * HEAD_DIM
GQA_HEADS = 8
GQA_KV_HEADS = 2
GQA_QBLK = 128
ROPE_THETA = 10000.0
GQA_Q_W = GQA_HEADS * HEAD_DIM
GQA_KV_W = GQA_KV_HEADS * HEAD_DIM
MEM_TOKENS = 256
MEM_HEADS = 4
MEM_HEAD_DIM = 128
MEM_W = MEM_HEADS * MEM_HEAD_DIM
N_BRANCH = 3
BRANCH_WIDTH = 512
GATE_W = N_BRANCH * D_MODEL
IN_W = 3 * NA_W + GQA_Q_W + 2 * GQA_KV_W + MEM_W + GATE_W
N_EXPERTS = 16
EC_CAPACITY_FACTOR = 2
D_FF_EXPERT = 1024
LN_EPS = 1e-5
RMS_EPS = 1e-6
DN_ALPHA = (2 * DEPTH) ** 0.25
DN_BETA = (8 * DEPTH) ** -0.25
NEG_INF = -1e30


def _split_points():
    sizes = (NA_W, NA_W, NA_W, GQA_Q_W, GQA_KV_W, GQA_KV_W, MEM_W)
    return tuple(int(v) for v in np.cumsum(sizes))

def layer_norm(x, g, b):
    xf = x.astype(jnp.float32)
    mu = jnp.mean(xf, axis=-1, keepdims=True)
    var = jnp.mean(jnp.square(xf - mu), axis=-1, keepdims=True)
    return ((xf - mu) * lax.rsqrt(var + LN_EPS) * g.astype(jnp.float32) + b.astype(jnp.float32)).astype(x.dtype)

def rms_norm_2(x, g):
    xf = x.astype(jnp.float32)
    ms = jnp.mean(jnp.square(xf), axis=-1, keepdims=True)
    return (xf * lax.rsqrt(ms + RMS_EPS) * g.astype(jnp.float32)).astype(x.dtype)

def axial_rope_tables(seq_len):
    t = jnp.arange(seq_len)
    row = (t // GRID_W).astype(jnp.float32)
    col = (t % GRID_W).astype(jnp.float32)
    half = HEAD_DIM // 2
    inv = ROPE_THETA ** (-jnp.arange(0, half, 2, dtype=jnp.float32) / half)
    ang = jnp.concatenate([row[:, None] * inv, col[:, None] * inv], axis=-1)
    return jnp.cos(ang), jnp.sin(ang)

def apply_rope(x, cos, sin):
    xf = x.astype(jnp.float32)
    x1, x2 = xf[..., 0::2], xf[..., 1::2]
    c, s = cos[None, :, None, :], sin[None, :, None, :]
    out = jnp.stack([x1 * c - x2 * s, x1 * s + x2 * c], axis=-1).reshape(x.shape)
    return out.astype(x.dtype)

def neighbourhood_attention(q, k, v, rpb):
    S, H, dh = q.shape
    rows = S // GRID_W
    kh = min(NA_KH_MAX, rows)
    ncb = GRID_W // NA_QBLK
    qg = q.reshape(rows, ncb, NA_QBLK, H, dh)
    kg = k.reshape(rows, GRID_W, H, dh)
    vg = v.reshape(rows, GRID_W, H, dh)
    r = jnp.arange(rows)
    row_start = jnp.clip(r - kh // 2, 0, rows - kh)
    key_rows = row_start[:, None] + jnp.arange(kh)
    cb = jnp.arange(ncb)
    band_start = jnp.clip(cb * NA_QBLK - NA_KW // 2, 0, GRID_W - NA_BAND)
    key_cols = band_start[:, None] + jnp.arange(NA_BAND)
    ri = key_rows[:, None, :, None]
    ci = key_cols[None, :, None, :]
    k_blk = kg[ri, ci]
    v_blk = vg[ri, ci]
    qcol = cb[:, None] * NA_QBLK + jnp.arange(NA_QBLK)
    col_start = jnp.clip(qcol - NA_KW // 2, 0, GRID_W - NA_KW)
    kc = key_cols[:, None, :]
    in_win = (kc >= col_start[:, :, None]) & (kc < col_start[:, :, None] + NA_KW)
    dr = key_rows - r[:, None]
    dc = jnp.clip(kc - qcol[:, :, None] + NA_KW - 1, 0, 2 * NA_KW - 2)
    bias = rpb[:, (dr + NA_KH_MAX - 1)[:, None, None, :, None], dc[None, :, :, None, :]]
    scores = jnp.einsum('rcqhd,rckwhd->hrcqkw', qg, k_blk,
                        preferred_element_type=jnp.float32) * (1.0 / math.sqrt(dh))
    scores = jnp.where(in_win[None, None, :, :, None, :], scores + bias.astype(jnp.float32), NEG_INF)
    p = jax.nn.softmax(scores, axis=(-2, -1))
    out = jnp.einsum('hrcqkw,rckwhd->rcqhd', p.astype(v.dtype), v_blk)
    return out.reshape(S, H * dh)

def gqa_attention(q, k, v, q_gain, k_gain, cos, sin):
    q = apply_rope(rms_norm_2(q, q_gain), cos, sin)
    k = apply_rope(rms_norm_2(k, k_gain), cos, sin)
    B, S, Hq, dh = q.shape
    hkv = k.shape[2]
    grp = Hq // hkv
    nblk = S // GQA_QBLK
    qb = q.reshape(B, nblk, GQA_QBLK, hkv, grp, dh).transpose(1, 0, 3, 4, 2, 5)
    scale = 1.0 / math.sqrt(dh)

    def block(qi):
        s = jnp.einsum('bkgqd,bskd->bkgqs', qi, k, preferred_element_type=jnp.float32) * scale
        p = jax.nn.softmax(s, axis=-1)
        return jnp.einsum('bkgqs,bskd->bqkgd', p.astype(v.dtype), v)

    out = lax.map(block, qb)
    return out.transpose(1, 0, 2, 3, 4, 5).reshape(B, S, Hq * dh)

def memory_attention(q, mk, mv):
    B, S, H, dm = q.shape
    s = jnp.einsum('bshd,bmhd->bhsm', q, mk, preferred_element_type=jnp.float32) * (1.0 / math.sqrt(dm))
    p = jax.nn.softmax(s, axis=-1)
    return jnp.einsum('bhsm,bmhd->bshd', p.astype(mv.dtype), mv).reshape(B, S, H * dm)

def expert_choice_ffn(x, w_router, w_gate_up, w_down):
    B, T, D = x.shape
    cap = EC_CAPACITY_FACTOR * T // N_EXPERTS
    logits = jnp.einsum('btd,de->bte', x, w_router, preferred_element_type=jnp.float32)
    aff = jax.nn.softmax(logits, axis=-1)
    gate, idx = lax.top_k(jnp.swapaxes(aff, 1, 2), cap)
    bidx = jnp.arange(B)[:, None, None]
    xs = x[bidx, idx]
    h = jnp.einsum('becd,edf->becf', xs, w_gate_up)
    hg, hu = jnp.split(h, 2, axis=-1)
    ye = jnp.einsum('becf,efd->becd', jax.nn.silu(hg) * hu, w_down)
    ye = ye * gate[..., None].astype(ye.dtype)
    return jnp.zeros_like(x).at[bidx, idx].add(ye)

def second_inputs(seed: int = 0) -> dict:
    key = jax.random.key(seed)
    ks = jax.random.split(key, 20)

    def nrm(k, shape, scale):
        return jax.random.normal(k, shape, jnp.float32) * scale

    return {
        "x": nrm(ks[0], (BATCH, SEQ, D_MODEL), 1.0),
        "mem": nrm(ks[1], (BATCH, MEM_TOKENS, D_MODEL), 1.0),
        "w_in": nrm(ks[2], (DEPTH, D_MODEL, IN_W), D_MODEL ** -0.5),
        "b_gate": nrm(ks[3], (DEPTH, GATE_W), 0.1),
        "na_rpb": nrm(ks[4], (DEPTH, NA_HEADS, 2 * NA_KH_MAX - 1, 2 * NA_KW - 1), 0.05),
        "gqa_q_gain": 1.0 + nrm(ks[5], (DEPTH, HEAD_DIM), 0.1),
        "gqa_k_gain": 1.0 + nrm(ks[6], (DEPTH, HEAD_DIM), 0.1),
        "w_mem_kv": nrm(ks[7], (DEPTH, D_MODEL, 2 * MEM_W), D_MODEL ** -0.5),
        "w_branch": nrm(ks[8], (DEPTH, N_BRANCH, BRANCH_WIDTH, D_MODEL), BRANCH_WIDTH ** -0.5),
        "w_out": nrm(ks[9], (DEPTH, D_MODEL, D_MODEL), D_MODEL ** -0.5 * DN_BETA),
        "ln1_g": 1.0 + nrm(ks[10], (DEPTH, D_MODEL), 0.1),
        "ln1_b": nrm(ks[11], (DEPTH, D_MODEL), 0.02),
        "w_router": nrm(ks[12], (DEPTH, D_MODEL, N_EXPERTS), D_MODEL ** -0.5),
        "w_gate_up": nrm(ks[13], (DEPTH, N_EXPERTS, D_MODEL, 2 * D_FF_EXPERT), D_MODEL ** -0.5),
        "w_down": nrm(ks[14], (DEPTH, N_EXPERTS, D_FF_EXPERT, D_MODEL), D_FF_EXPERT ** -0.5 * DN_BETA),
        "ln2_g": 1.0 + nrm(ks[15], (DEPTH, D_MODEL), 0.1),
        "ln2_b": nrm(ks[16], (DEPTH, D_MODEL), 0.02),
    }

def second_block(x, mem, w_in, b_gate, na_rpb, gqa_q_gain, gqa_k_gain, w_mem_kv, w_branch, w_out,
              ln1_g, ln1_b, w_router, w_gate_up, w_down, ln2_g, ln2_b):
    B, S, D = x.shape
    M = mem.shape[1]
    cos, sin = axial_rope_tables(S)
    for l in range(DEPTH):
        z = jnp.einsum('bsd,df->bsf', x, w_in[l])
        q_na, k_na, v_na, q_g, k_g, v_g, q_m, gate_logits = jnp.split(z, _split_points(), axis=-1)
        rpb = na_rpb[l]
        y_na = lax.map(lambda qkv: neighbourhood_attention(qkv[0], qkv[1], qkv[2], rpb),
                       (q_na.reshape(B, S, NA_HEADS, HEAD_DIM),
                        k_na.reshape(B, S, NA_HEADS, HEAD_DIM),
                        v_na.reshape(B, S, NA_HEADS, HEAD_DIM)))
        y_gqa = gqa_attention(q_g.reshape(B, S, GQA_HEADS, HEAD_DIM),
                              k_g.reshape(B, S, GQA_KV_HEADS, HEAD_DIM),
                              v_g.reshape(B, S, GQA_KV_HEADS, HEAD_DIM),
                              gqa_q_gain[l], gqa_k_gain[l], cos, sin)
        mkv = jnp.einsum('bmd,df->bmf', mem, w_mem_kv[l])
        mk, mv = jnp.split(mkv, 2, axis=-1)
        y_mem = memory_attention(q_m.reshape(B, S, MEM_HEADS, MEM_HEAD_DIM),
                                 mk.reshape(B, M, MEM_HEADS, MEM_HEAD_DIM),
                                 mv.reshape(B, M, MEM_HEADS, MEM_HEAD_DIM))
        branches = jnp.stack([y_na, y_gqa, y_mem], axis=2)
        proj = jnp.einsum('bsgk,gkd->bsgd', branches, w_branch[l])
        gates = jax.nn.sigmoid(gate_logits + b_gate[l]).reshape(B, S, N_BRANCH, D)
        merged = jnp.sum(gates * proj, axis=2)
        mix = jnp.einsum('bsd,de->bse', merged, w_out[l])
        x = layer_norm(DN_ALPHA * x + mix, ln1_g[l], ln1_b[l])
        ffn = expert_choice_ffn(x, w_router[l], w_gate_up[l], w_down[l])
        x = layer_norm(DN_ALPHA * x + ffn, ln2_g[l], ln2_b[l])
    return x


def setup_inputs(seed=0):
    out = dict(first_inputs(seed))
    for name, value in second_inputs(seed + 1).items():
        if name != "x":
            out[name + "_2"] = value
    return out


def reference(
    x, norm_mix, w_in, conv_w, conv_b, w_rg, b_rg, w_ig, b_ig, lru_lambda, norm_lru_out,
    norm_att_out, w_out, norm_ffn, w_ffn_in, w_ffn_out, norm_final, mem_2, w_in_2, b_gate_2,
    na_rpb_2, gqa_q_gain_2, gqa_k_gain_2, w_mem_kv_2, w_branch_2, w_out_2, ln1_g_2, ln1_b_2,
    w_router_2, w_gate_up_2, w_down_2, ln2_g_2, ln2_b_2,
):
    x = first_block(
        x, norm_mix, w_in, conv_w, conv_b, w_rg, b_rg, w_ig, b_ig, lru_lambda, norm_lru_out,
        norm_att_out, w_out, norm_ffn, w_ffn_in, w_ffn_out, norm_final,
    )
    return second_block(
        x, mem_2, w_in_2, b_gate_2, na_rpb_2, gqa_q_gain_2, gqa_k_gain_2, w_mem_kv_2,
        w_branch_2, w_out_2, ln1_g_2, ln1_b_2, w_router_2, w_gate_up_2, w_down_2, ln2_g_2,
        ln2_b_2,
    )


_drawn_inputs = setup_inputs


def setup_inputs(seed=0):
    import zlib

    import numpy as np

    out = dict(_drawn_inputs(seed))
    spreads = {}
    factors = {'b_rg': 8.0,
     'b_ig': 8.0,
     'b_gate_2': 8.0,
     'na_rpb_2': 28.167,
     'gqa_q_gain_2': 8.0,
     'gqa_k_gain_2': 8.0,
     'ln2_b_2': 2.751}
    for name, (base, spread) in spreads.items():
        noise = np.random.default_rng([zlib.crc32(name.encode()), seed]).standard_normal(out[name].shape)
        drawn = base * np.exp(spread * noise) if base else spread * noise
        out[name] = __import__('jax').numpy.asarray(drawn.astype(out[name].dtype))
    for name, factor in factors.items():
        out[name] = (out[name] * factor).astype(out[name].dtype)
    return out
```

```python
from contextlib import ExitStack

import numpy as np
import concourse.bass as bass
from concourse import mybir

P = 128
S = 512
D = 1024
KT = D // P
TT = S // P
UC = 256
DFF = 2816
E = 16
CAP = 64
DFE = 1024
M = 256
ALPHA = 2.0 ** 0.25
NEG = -1e30

F32 = mybir.dt.float32
F32R = mybir.dt.float32r
U32 = mybir.dt.uint32
ALU = mybir.AluOpType
ACT = mybir.ActivationFunctionType
AX = mybir.AxisListType.X

C_ID, C_LT, C_NEG, C_NAM, C_ONE, C_TC = 0, 128, 256, 384, 480, 608
C_EPS6, C_EPS5, C_COS, C_SIN, C_IOTA = 612, 613, 614, 742, 870
C_N1 = C_IOTA
C_N = C_IOTA + S
V_GMIX, V_GFFN, V_CW, V_CB, V_BRG, V_BIG, V_LAM, V_GLRU, V_GATT, V_BG, V_GQ = 0, 8, 16, 32, 36, 40, 44, 48, 52, 56, 80
V_N = 80 + 128


class Step:

    def __init__(self, kind, counts, after=None, kw=None, dst=None, src=None,
                 u=None, w=None, c0=0, K=KT, mode=None, evac=None, nt=S, row0=0, who=(), r0=0,
                 dh=None, dl=None, nf=0, T=TT, scale=None, perm=False, f32=False, const=1.0, n0=0,
                 d=0, grow=None, rows=None,
                 att=None, h=0, half=0, n=0, qt=(), nkt=(), a=None):
        self.kind, self.counts, self.after, self.kw, self.dst, self.src = kind, counts, after, kw, dst, src
        self.u, self.w, self.c0, self.K, self.mode, self.evac = u, w, c0, K, mode, evac
        self.nt, self.row0, self.who, self.r0 = nt, row0, who, r0
        self.dh, self.dl, self.nf, self.T, self.scale = dh, dl, nf, T, scale
        self.perm, self.f32, self.const, self.n0 = perm, f32, const, n0
        self.d, self.grow, self.rows = d, grow, rows
        self.att, self.h, self.half, self.n, self.qt, self.nkt, self.a = att, h, half, n, qt, nkt, a
        self.t = self.o = None


def number(plan):
    at = {}
    for st in plan:
        st.at = dict(at)
        for s, n in st.counts.items():
            at[s] = at.get(s, 0) + n
        st.end = dict(at)
    return at


def build(nc, x, w_in, w_out, w_ffn_in, w_ffn_out, mem, w_in2, w_memkv, w_branch, w_out2, w_router,
          w_gu, w_down, w_rg, w_ig, rows, rpb, vecs, consts, out, stop=None):
    ctx = ExitStack()
    base = (nc.sbuf_base + 63) // 64 * 64

    def at(name, kb, shape, dt=F32):
        return nc.alloc_sbuf_tensor_at(name, shape, dt, offset=base + int(kb * 1024), align_bytes=32)

    def sem(name):
        return ctx.enter_context(nc.semaphore(name))

    XH = at("XH", 0, [P, KT, S], F32R)
    XL = at("XL", 16, [P, KT, S], F32R)
    X2T = at("X2T", 0, [P, KT, S])
    WH = at("WH", 32, [P, 2, KT * UC], F32R)
    WL = at("WL", 48, [P, 2, KT * UC], F32R)
    AH = at("AH", 64, [P, KT, S], F32R)
    AL = at("AL", 80, [P, KT, S], F32R)
    XN = at("XN", 64, [P, TT, D])
    MEMT = at("MEMT", 64, [P, 2, D])
    MH = at("MH", 80, [P, KT, M], F32R)
    ML = at("ML", 88, [P, KT, M], F32R)
    LX = at("LX", 64, [P, 4, 3 + S])
    LTH = at("LTH", 64, [P, 4, S])
    LG = at("LG", 72.25, [P, 4, S])
    LC = at("LC", 80.5, [P, 4, S])
    LI = at("LI", 88.5, [P, 4, S])
    LR = at("LR", 152, [P, 4, S])
    YL_ = at("YL_", 80.5, [P, 4, S])
    SE = at("SE", 64, [P, 2, S])
    SP_ = at("SP_", 68, [P, 2, S])
    SC = at("SC", 72, [P, 2, S])
    RBC = at("RBC", 78, [P, S])
    YH2 = at("YH2", 64, [P, 4, S], F32R)
    YL2 = at("YL2", 80, [P, 4, S], F32R)
    SN = at("SN", 64, [P, 2, M])
    TMP = at("TMP", 189.5, [P, 4, S])
    VN = at("VN", 72, [P, TT, 512])
    GQT = at("GQT", 88, [P, TT, 512])
    GT = at("GT", 88, [P, 2, S])
    R0 = 96.5
    RAW = at("RAW", R0, [P, 2, KT * UC])
    RING = at("RING", R0, [P, 8, 2048])
    QT = at("QT", R0 + 16, [P, 4, S])
    KTT = at("KTT", R0 + 24, [P, 4, S])
    VT = at("VT", R0 + 32, [P, TT, 512])
    YT = at("YT", R0 + 40, [P, TT, 512])
    FG = at("FG", R0 + 16, [P, 2, S])
    FP = at("FP", R0 + 20, [P, 2, S])
    VB = at("VB", R0 + 32, [P, 4, 2, 512])
    QG = at("QG", R0 + 16, [P, 4, S])
    KG = at("KG", R0 + 24, [P, 2, S])
    QM = at("QM", R0 + 32, [P, 4, S])
    RT = at("RT", R0 + 24, [P, 3, 640])
    GFIN = at("GFIN", R0 + 16, [P, D])
    LNR = at("LNR", 64, [P, 2, D])
    MG = at("MG", R0 + 48, [P, KT, S])
    KD = at("KD", R0 + 40, [P, TT, 256])
    X = at("X", 160.5, [P, TT, D])
    B48 = at("B48", 160.5, [P, 8, 8, 48])
    CST = at("CST", 176.5, [P, C_N1])
    VEC = at("VEC", 180, [P, V_N])
    ST = at("ST", 181, [P, 128])
    MKT = at("MKT", 181.5, [P, 4, M])
    MV = at("MV", 185.5, [P, 2, 512])
    PB = at("PB", 189.5, [P, 2, 2, S])
    PT = at("PT", 197.5, [P, 4, 256])
    KVT = at("KVT", 201.5, [P, TT, 256])
    BD = at("BD", 201.5, [P, 2, 4, P])
    YN = at("YN", 72, [P, TT, 512])
    IDB = at("IDB", 16, [P, E * CAP])
    OHT = at("OHT", 20, [P, TT, P], F32R)
    XST = at("XST", 24, [P, KT, P])
    SG = at("SG", 28, [P, 512])
    HT = at("HT", 30, [P, KT, CAP])
    YHM = at("YHM", 32, [P, D], F32R)
    YLM = at("YLM", 36, [P, D], F32R)
    SS = at("SS", 40, [P, S], F32R)
    IOTA = at("IOTA", 42, [P, S])
    LN2R = at("LN2R", 44, [P, 2, D])
    AF = at("AF", 52, [E, S])
    VAL = at("VAL", 54, [E, 2 * CAP])
    IDX = at("IDX", 54.5, [E, 2 * CAP])
    IDU = at("IDU", 55, [E, CAP], U32)
    GCOL = at("GCOL", 55.5, [P, E // 2])
    ICOL = at("ICOL", 55.75, [P, E // 2])
    WR = at("WR", 201.5, [P, KT, E])
    LGT = at("LGT", 202.5, [P, TT, E])
    X2H = at("X2H", 64, [P, TT, D], F32R)
    X2L = at("X2L", 80, [P, TT, D], F32R)

    ps = [ctx.enter_context(nc.psum_tensor(f"bank{i}", [P, 512], F32)) for i in range(8)]
    LIN, SB, TR, PV = ps[0:3], ps[3:5], ps[5:7], ps[7]

    ident = CST[:, C_ID:C_ID + P]
    ones = CST[:, C_ONE:C_ONE + P]

    def vec(c, n=1):
        return VEC[:, c:c + n]

    raw_in = [sem(f"raw_in{i}") for i in range(2)]
    names = """w_hi w_lo res evA evD act_hi act_lo tx_ps tx_hi tx_lo ms sd rc nrm conv gmm sig
               lexp lgl lt lm2 lsq lrec ysq ysum ysd yn yhi ylo qk mx e_ab st_d p tr ptA ptD pv o rope gk
               ms_hi ms_lo saved band x2h x2l xal lgp lgs afp af top ixp ixc icp icc fin""".split()
    names.extend(["rms_q", "rsd_q"])
    s = {n: sem(n) for n in names}
    consts_in, mem_in, x_in, rows_in, b48_in, xre_in, out_in, bd_in, bd0, moe_in = (
        sem(n) for n in "consts_in mem_in x_in rows_in b48_in xre_in out_in bd_in bd0 moe_in".split())
    xd = nc.dram_tensor("x_saved", (S, D), F32, kind="Internal").ap().rearrange("(t p) d -> p t d", p=P)

    win_rpb = nc.dram_tensor("win_rpb", (16, 120, 48), F32, kind="Internal").ap()
    win_in = sem("win_in")

    rows2_in = sem("rows2_in")

    def wait(e, name, values, less=0):
        v = values.get(name, 0) - less
        if v > 0:
            e.wait_ge(s[name], v)

    plan = []
    units, results, txs = [], [], []

    def add(kind, counts, **kw):
        st = Step(kind, counts, **kw)
        plan.append(st)
        return st

    def unit(w, c0, K, mode, evac, dst=None, src="x", nt=S, row0=0, **kw):
        nres = 2 if mode == "F" else nt // 256
        shares = {"act": (1, 0), "dve": (0, 1)}
        sh = []
        for r in range(nres):
            if evac == "ffn":
                sh.append("act" if r == 0 else "dve")
            elif evac in ("accX", "mixX", "branch"):
                sh.append("dve")
            elif evac in ("gate", "naq", "scaled"):
                sh.append("act")
            else:
                sh.append("act" if (r + len(units)) % 2 else "dve")
        counts = dict(w_hi=1, w_lo=1, res=nres, evA=sh.count("act"), evD=sh.count("dve"))
        if evac == "ffn":
            counts.update(act_hi=1, act_lo=1)
        st = add("unit", counts, u=len(units), w=w, c0=c0, K=K, mode=mode, evac=evac, dst=dst, src=src,
                 nt=nt, row0=row0, who=sh, r0=len(results), kw=kw)
        units.append(st)
        for r in range(nres):
            results.append((st, r))
        return st

    def tx(src, dh, dl, nf, T, scale=None, perm=False, f32=False, const=1.0, **kw):
        st = add("tx", dict(tx_ps=nf, tx_hi=nf, tx_lo=0 if f32 else nf), src=src, dh=dh, dl=dl, nf=nf,
                 T=T, scale=scale, perm=perm, f32=f32, const=const, n0=len(txs), kw=kw)
        txs.extend([st] * nf)
        return st

    def rms(src, dst, d, grow=None, **kw):
        return add("rms", dict(sd=1, rc=1, nrm=TT), src=src, dst=dst, d=d, grow=grow, kw=kw)

    atts = []

    def attention(kind, heads, halves, fill, after):
        n = heads * halves
        mine = []
        per = len(fill) / n
        done = 0

        def t_step(a):
            many = a.nkt[1] > 2
            a.t = add("T", dict(tr=1, ptA=1, ptD=int(many)), a=a)
        def o_step(a):
            a.o = add("O", dict(pv=1, o=1), a=a)
        for i in range(n + 1):
            if i:
                t_step(mine[i - 1])
            if i < n:
                h, half = divmod(i, halves)
                a = Step("S", dict(qk=2, p=2), att=kind, h=h, half=half, n=len(atts), after=after)
                a.counts.update(dict(e_ab=2, st_d=2) if kind == "stick" else dict(mx=2))
                a.qt = [2 * half, 2 * half + 1]
                a.nkt = [q + 1 for q in a.qt] if kind == "stick" else [4, 4] if kind == "gqa" else [2, 2]
                plan.append(a)
                mine.append(a)
                atts.append(a)
            if i:
                o_step(mine[i - 1])
            while done < len(fill) and done < per * (i + 1):
                fill[done]()
                done += 1
        return mine[-1].o

    win, win2 = w_in[0], w_in2[0]
    tx_mem = tx(MEMT, MH, ML, KT, 2, ready=(mem_in, 16))
    for j in range(2):
        unit(w_memkv[0], UC * j, KT, "F", "copy", dst=lambda r, j=j: MKT[:, 2 * j + r, :], src="m", nt=M)
    for j in range(2):
        mem_last = unit(w_memkv[0], 512 + UC * j, KT, "T", "copy",
                        dst=lambda r, j=j: MV[:, :, UC * j:UC * j + UC], src="m", nt=M)
    rms(X, XN, D, ready=(x_in, 64), war=tx_mem)
    tx(XN, XH, XL, KT, TT, scale=V_GMIX)
    for j in range(2):
        unit(win, UC * j, KT, "F", "copy", dst=lambda r, j=j: LX[:, 2 * j + r, 3:])
    lxu = plan[-1]
    conv = add("conv", dict(conv=1), after=lxu)
    for j in range(2):
        unit(win, 512 + UC * j, KT, "F", "copy", dst=lambda r, j=j: LG[:, 2 * j + r, :])
    lgu = plan[-1]
    add("lgate", dict(gmm=8, sig=8), after=lgu)
    for j in range(2):
        unit(win, 1024 + UC * j, KT, "F", "scaled", dst=lambda r, j=j: QT[:, 2 * j + r, :], scale=0.125)
    lrec = add("lrec", dict(lexp=1, lm2=1, lsq=1, lt=1, lgl=1, lrec=1), after=lgu)
    for j in range(2):
        unit(win, 1536 + UC * j, KT, "F", "copy", dst=lambda r, j=j: KTT[:, 2 * j + r, :])
    for j in range(2):
        unit(win, 2048 + UC * j, KT, "T", "copy", dst=lambda r, j=j: VT[:, 2 * r:2 * r + 2, UC * j:UC * j + UC])
    qkv = plan[-1]
    lout = add("lout", dict(ysq=1, ysum=1, ysd=1, yn=1, yhi=4, ylo=4), after=qkv)
    add("logexp", {})
    last = attention("stick", 8, 2, [], qkv)
    rms(YT, YT, 512, after=last)
    tx(YT, XH[:, 4:8], XL[:, 4:8], 4, TT, scale=V_GATT)
    for j in range(4):
        unit(w_out[0], UC * j, KT, "T", "accX")
    rms(X, XN, D, after=plan[-1])
    tx(XN, XH, XL, KT, TT, scale=V_GFFN)
    for f0, nf in ((0, 8), (8, 8), (16, 6)):
        for f in range(f0, f0 + nf):
            unit(w_ffn_in[0], P * f, KT, "F", "ffn", f=f - f0)
        for j in range(4):
            unit(w_ffn_out[0], UC * j, nf, "T", "accX", src="a", row0=P * f0)
    fin = rms(X, X, D, grow=GFIN, after=plan[-1])
    end1 = len(plan)
    save = add("save", dict(saved=16))
    txx = tx(X, XH, XL, KT, TT)
    for j in range(2):
        unit(win2, UC * j, KT, "F", "naq", dst=lambda r, j=j: QT[:, 2 * j + r, :])
    for j in range(2):
        unit(win2, 512 + UC * j, KT, "F", "copy", dst=lambda r, j=j: KTT[:, 2 * j + r, :])
    for j in range(2):
        unit(win2, 1024 + UC * j, KT, "T", "copy", dst=lambda r, j=j: VN[:, 2 * r:2 * r + 2, UC * j:UC * j + UC])
    naqkv = plan[-1]
    band = add("band", dict(band=16 * 16), after=naqkv)
    fill = [lambda j=j: unit(win2, 1536 + UC * j, KT, "T", "copy",
                             dst=lambda r, j=j: GQT[:, 2 * r:2 * r + 2, UC * j:UC * j + UC]) for j in range(2)]
    fill.append(lambda: unit(win2, 2048, KT, "T", "copy", dst=lambda r: KVT[:, 2 * r:2 * r + 2, :]))
    na_last = attention("na", 8, 2, fill, band)
    add("rope", dict(rope=TT), after=na_last)
    tx(YN, YH2, YL2, 4, TT, perm=True)
    tx(GQT, QG, None, 4, TT, f32=True, const=0.125)
    tx(KD, KG, None, 2, TT, f32=True)
    gq = plan[-1]

    def gate(g, j):
        return lambda: unit(win2, 2816 + D * g + UC * j, KT, "F", "gate", g=g, j=j)

    def branch(g, j):
        return lambda: unit(w_branch[0, g], UC * j, 4, "F", "branch", src="y", g=g, j=j)

    fill = [lambda j=j: unit(win2, 2304 + UC * j, KT, "F", "scaled", dst=lambda r, j=j: QM[:, 2 * j + r, :],
                             scale=float(P) ** -0.5) for j in range(2)]
    for j in range(4):
        fill += [gate(0, j), branch(0, j)]
    gl = attention("gqa", 8, 2, fill, gq)
    tx(YN, YH2, YL2, 4, TT)
    fill = [f for j in range(4) for f in (gate(1, j), branch(1, j))]
    ml = attention("mem", 4, 2, fill, plan[-1])
    tx(YN, YH2, YL2, 4, TT)
    for j in range(4):
        gate(2, j)()
        branch(2, j)()
    add("msplit", dict(ms_hi=KT, ms_lo=KT), after=plan[-1])
    for j in range(4):
        unit(w_out2[0], UC * j, KT, "T", "mixX")
    ln1 = add("ln", dict(ms=1, sd=1, rc=1, nrm=TT), rows=LNR, after=plan[-1])
    end2 = len(plan)
    tx2 = tx(X, X2T, None, KT, TT, f32=True)
    router = add("router", dict(lgp=1, xal=TT))
    if stop == "x1":
        del plan[end1:]
    if stop == "x2":
        del plan[end2:]
    total = number(plan)
    last_step = plan[-1]
    live = set(map(id, plan))
    units = [u for u in units if id(u) in live]
    res_shares = []
    a = d = 0
    for st, r in results:
        a += st.who[r] == "act"
        d += st.who[r] == "dve"
        res_shares.append((a, d))
    tx_free = []
    h = l = 0
    for st in txs:
        h += 1
        l += not st.f32
        tx_free.append((h, l))

    SRC = {"x": (XH, XL), "m": (MH, ML), "a": (AH, AL), "y": (YH2, YL2)}

    def bank_free(e, n):
        if n >= 3:
            a, d = res_shares[n - 3]
            if a:
                e.wait_ge(s["evA"], a)
            if d:
                e.wait_ge(s["evD"], d)

    class Chain:

        def __init__(self, e, name):
            self.e, self.s, self.n, self.p, self.per, self.mark = e, sem(name), 0, None, 0, 0

        def link(self, ins):
            ins.then_inc(self.s, 1)
            self.n += 1
            self.e.wait_ge(self.s, self.n if self.p is None else self.n + self.per * self.p)

        def loop(self, p, per):
            self.p, self.per, self.mark = p, per, self.n

        def leave(self, times):
            assert self.n - self.mark == self.per, (self.n, self.mark, self.per)
            self.n, self.p = self.mark + self.per * times, None


    def pieces(a, b):
        bank = TR[b][:, :].rearrange("p (k q) -> p k q", k=2)
        if a.nkt[0] >= 2 * b + 2:
            return [(PT[:, 2 * b:2 * b + 2, :], bank)]
        return [(PT[:, 2 * b, :], bank[:, 0, :]), (PT[:, 2 * b + 1, P:], bank[:, 1, P:])]

    def shaped(st, bank):
        if st.mode == "F":
            return bank[:, :st.nt]
        return bank[:, :].rearrange("p (t c) -> p t c", t=2)

    def layer_norm_act(act, end):
        wait(act, "ms", end)
        nc.scalar.activation(ST[:, 4:8], ST[:, 97:105:2], ACT.Sqrt,
                             bias=CST[:, C_EPS5:C_EPS5 + 1]).then_inc(s["sd"], 1)

    def layer_norm_dve(dve, link, end, rows_, landed, value):
        V = nc.vector
        for t in range(TT):
            V.bn_stats(ST[:, 48 + 12 * t:54 + 12 * t], X[:, t, 0:512])
            link(V.bn_stats(ST[:, 54 + 12 * t:60 + 12 * t], X[:, t, 512:1024]))
        for t in range(TT):
            ins = V.bn_aggr(ST[:, 96 + 2 * t:98 + 2 * t],
                            ST[:, 48 + 12 * t:60 + 12 * t].rearrange("p (i c) -> p i c", i=2))
        ins.then_inc(s["ms"], 1)
        wait(dve, "sd", end)
        V.reciprocal(ST[:, 8:12], ST[:, 4:8]).then_inc(s["rc"], 1)
        wait(dve, "rc", end)
        wait(dve, "ms", end)
        dve.wait_ge(landed, value)
        for t in range(TT):
            link(V.tensor_scalar(X[:, t, :], X[:, t, :], ST[:, 96 + 2 * t:97 + 2 * t],
                                 ST[:, 8 + t:9 + t], ALU.subtract, ALU.mult))
            link(V.tensor_tensor(X[:, t, :], X[:, t, :], rows_[:, 0, :], ALU.mult))
            V.tensor_tensor(X[:, t, :], X[:, t, :], rows_[:, 1, :], ALU.add).then_inc(s["nrm"], 1)

    ring_in = [sem(f"ring_in{i}") for i in range(8)]
    used, oht, gth, xsA, xsD, su, ht, yh, yl, sct, acc = (
        sem(n) for n in "used oht gth xsA xsD su ht yh yl sct acc".split())
    PAIRS, CH = E // 2, 24
    G_, U_, Y_, XS_, SC_ = LIN[0], LIN[1], SB, TR, (LIN[2], PV)
    gu_v = w_gu[0].rearrange("e (k p) f -> p (e k) f", p=P)
    dn_v = w_down[0].rearrange("e (i k p) d -> p (e i) k d", k=2, p=P)

    def chunk(sp, pair, c):
        j, i = divmod(c, 12)
        slot = RING[:, c % 8, :]
        if i < 8:
            src = gu_v[:, bass.ds((2 * pair + j) * 8 + i, 1), :].rearrange("p a f -> p (a f)")
            sp.dma_start(slot, src).then_inc(ring_in[c % 8], 16)
        else:
            src = dn_v[:, bass.ds((2 * pair + j) * 4 + i - 8, 1), :, :].rearrange("p a k d -> p (a k) d")
            sp.dma_start(slot.rearrange("p (k d) -> p k d", k=2), src).then_inc(ring_in[c % 8], 16)

    def experts_sp(sp):
        wait(sp, "w_lo", total)
        wait(sp, "pv", total)
        for c in range(8):
            chunk(sp, 0, c)
        sp.dma_start(WR[:, :, :], w_router[0].rearrange("(k p) e -> p k e", p=P)).then_inc(moe_in, 16)
        with sp.Fori(0, PAIRS - 1) as p:
            for c in range(8, 8 + CH):
                sp.wait_ge(used, CH * p + c - 7)
                chunk(sp, p + c // CH, c % CH)
        for c in range(8, CH):
            sp.wait_ge(used, CH * (PAIRS - 1) + c - 7)
            chunk(sp, PAIRS - 1, c)
        for t in range(TT):
            sp.wait_ge(s["nrm"], total["nrm"] + t + 1)
            sp.dma_start(out[0].rearrange("(t p) d -> t p d", p=P)[t], X[:, t, :]).then_inc(out_in, 16)
        sp.wait_ge(out_in, 16 * TT)

    def experts_act(act, chain):
        A = nc.scalar.activation
        wait(act, "nrm", total)
        for t in range(TT):
            A(X2H[:, t, :], X[:, t, :], ACT.Copy).then_inc(s["x2h"], 1)
        act.dma_start(IOTA[:, :], consts[:, C_IOTA:C_IOTA + S]).then_inc(moe_in, 16)
        for i in range(2):
            act.dma_start(LN2R[:, i, :], rows[3 + i].partition_broadcast(P)).then_inc(rows2_in, 16)
        act.wait_ge(s["lgs"], 1)
        A(LGT[:, :, :], LGT[:, :, :], ACT.Exp).then_inc(s["afp"], 1)
        act.wait_ge(s["icc"], 1)
        with act.Fori(0, PAIRS) as p:
            act.wait_ge(gth, p + 1)
            A(XST[:, 0:4, :], XS_[0][:, :].rearrange("p (k c) -> p k c", k=4), ACT.Copy).then_inc(xsA, 1)
            for j in range(2):
                act.wait_ge(used, CH * p + 12 * j + 8)
                A(SG[:, :], G_[:, :], ACT.Silu).then_inc(su, 1)
            act.wait_ge(used, CH * p + CH)
            for h in range(2):
                A(YHM[:, 512 * h:512 * h + 512], Y_[h][:, :], ACT.Copy,
                  scale=GCOL[:, bass.ds(p, 1)]).then_inc(yh, 1)
        layer_norm_act(act, {k: v + 1 for k, v in total.items()})

    def experts_dve(dve, chain):
        V, link = nc.vector, chain.link
        dve.wait_ge(s["lgp"], 1)
        lg = PV[:, 0:TT * E].rearrange("p (t e) -> p t e", e=E)
        link(V.tensor_reduce(ST[:, 0:4], lg, AX, ALU.max))
        V.tensor_tensor(LGT[:, :, :], lg, ST[:, 0:4].unsqueeze(2).to_broadcast([P, TT, E]),
                        ALU.subtract).then_inc(s["lgs"], 1)
        dve.wait_ge(s["afp"], 1)
        link(V.tensor_reduce(ST[:, 4:8], LGT[:, :, :], AX, ALU.add))
        link(V.reciprocal(ST[:, 8:12], ST[:, 4:8]))
        V.tensor_tensor(LGT[:, :, :], LGT[:, :, :], ST[:, 8:12].unsqueeze(2).to_broadcast([P, TT, E]),
                        ALU.mult).then_inc(s["af"], 1)
        dve.wait_ge(s["ixp"], 1)
        link(V.tensor_copy(AF[:, :], SB[0][0:E, :]))
        for i in range(CAP // 8):
            r = slice(8 * i, 8 * i + 8)
            link(V.max(VAL[:, r], AF[:, :]))
            V.max_index(IDU[:, r], VAL[:, r], AF[:, :])
            link(V.match_replace(AF[:, :], VAL[:, r], AF[:, :], -1.0))
        V.tensor_copy(VAL[:, CAP:2 * CAP], VAL[:, 0:CAP])
        V.tensor_copy(IDX[:, 0:CAP], IDU[:, :])
        V.tensor_copy(IDX[:, CAP:2 * CAP], IDU[:, :]).then_inc(s["top"], 1)
        dve.wait_ge(s["ixp"], 2)
        for h in range(2):
            r = slice(64 * h, 64 * h + 64)
            V.tensor_copy(GCOL[r, :], SB[1][r, h:E:2])
            V.tensor_copy(ICOL[r, :], SB[1][r, E + h:2 * E:2])
        for h in range(2):
            ins = V.tensor_copy(IDB[:, 512 * h:512 * h + 512], LIN[h][:, :])
        ins.then_inc(s["icc"], 1)
        dve.wait_ge(s["icc"], 1)
        dve.wait_ge(moe_in, 32)
        wait(dve, "xal", total)
        for i in range(2):
            V.memset(ST[:, 12 + i:13 + i], 0.0).then_inc(acc, 1)
        with dve.Fori(0, PAIRS) as p:
            for t in range(TT):
                ins = V.tensor_scalar(OHT[:, t, :], IDB[:, bass.ds(p * P, P)], CST[:, C_TC + t:C_TC + t + 1],
                                      None, ALU.is_equal)
            ins.then_inc(oht, 1)
            V.tensor_scalar(SS[:, :], IOTA[:, :], ICOL[:, bass.ds(p, 1)], None, ALU.is_equal)
            dve.wait_ge(gth, p + 1)
            V.tensor_copy(XST[:, 4:8, :], XS_[1][:, :].rearrange("p (k c) -> p k c", k=4)).then_inc(xsD, 1)
            for j in range(2):
                dve.wait_ge(su, 2 * p + j + 1)
                V.tensor_tensor(HT[:, :, :], U_[:, :].rearrange("p (f c) -> p f c", c=CAP),
                                SG[:, :].rearrange("p (f c) -> p f c", c=CAP), ALU.mult).then_inc(ht, 1)
            for h in range(2):
                dve.wait_ge(yh, 2 * p + 2)
                c = slice(512 * h, 512 * h + 512)
                V.scalar_tensor_tensor(YLM[:, c], Y_[h][:, :], GCOL[:, bass.ds(p, 1)], YHM[:, c].bitcast(F32),
                                       ALU.mult, ALU.subtract).then_inc(yl, 1)
            for i in range(2 * TT):
                dve.wait_ge(sct, 8 * p + i + 1)
                xs = X[:, i // 2, 512 * (i % 2):512 * (i % 2) + 512]
                V.tensor_tensor(xs, SC_[i % 2][:, :], xs, ALU.add).then_inc(acc, 1)
        dve.wait_ge(acc, 2 + 8 * PAIRS)
        layer_norm_dve(dve, link, {k: v + 1 for k, v in total.items()}, LN2R, rows2_in, 32)

    def experts_pe(pe):
        T = nc.tensor
        pe.wait_ge(moe_in, 32)
        wait(pe, "tx_hi", total)
        for name in ("o", "evA", "evD", "p", "ptA", "ptD"):
            wait(pe, name, total)
        for t in range(TT):
            for k in range(KT):
                ins = T.matmul(PV[:, E * t:E * t + E], X2T[:, k, t * P:t * P + P], WR[:, k, :],
                               start=k == 0, stop=k == KT - 1)
        ins.then_inc(s["lgp"], 1)
        pe.wait_ge(s["af"], 1)
        for t in range(TT):
            ins = T.transpose(SB[0][0:E, t * P:t * P + P], LGT[:, t, :], ident)
        ins.then_inc(s["ixp"], 1)
        pe.wait_ge(s["top"], 1)
        T.transpose(SB[1][:, 0:E], VAL[:, :], ident[0:E, 0:E])
        T.transpose(SB[1][:, E:2 * E], IDX[:, :], ident[0:E, 0:E])
        for e in range(E):
            ins = T.matmul(LIN[e // 8][:, (e % 8) * CAP:(e % 8 + 1) * CAP],
                           ident[0:E, e:e + 1].to_broadcast([E, P]), IDX[:, 0:CAP], start=True, stop=True)
        ins.then_inc(s["ixp"], 1)
        pe.wait_ge(s["icc"], 1)
        pe.wait_ge(s["x2l"], TT)
        with pe.Fori(0, PAIRS) as p:
            pe.wait_ge(oht, p + 1)
            for d in range(KT):
                o = XS_[d // 4][:, (d % 4) * P:(d % 4) * P + P]
                for t in range(TT):
                    T.matmul(o, X2H[:, t, d * P:d * P + P], OHT[:, t, :], start=t == 0, stop=False)
                    ins = T.matmul(o, X2L[:, t, d * P:d * P + P], OHT[:, t, :], start=False, stop=t == TT - 1)
            ins.then_inc(gth, 1)
            pe.wait_ge(xsA, p + 1)
            pe.wait_ge(xsD, p + 1)
            for j in range(2):
                xj = slice(CAP * j, CAP * j + CAP)
                for k in range(KT):
                    c = 12 * j + k
                    pe.wait_ge(ring_in[c % 8], 48 * p + 16 * (c // 8 + 1))
                    for f in range(2 * KT):
                        ins = T.matmul((G_, U_)[f // 8][:, (f % 8) * CAP:(f % 8 + 1) * CAP],
                                       RING[:, c % 8, f * P:f * P + P], XST[:, k, xj],
                                       start=k == 0 and f % 8 == 0, stop=k == KT - 1, skip_group_check=True)
                    ins.then_inc(used, 1)
                pe.wait_ge(ht, 2 * p + j + 1)
                for i in range(4):
                    c = 12 * j + 8 + i
                    pe.wait_ge(ring_in[c % 8], 48 * p + 16 * (c // 8 + 1))
                    for k in range(2):
                        for h in range(2):
                            ins = T.matmul(Y_[h][CAP * j:CAP * j + CAP, :], HT[:, 2 * i + k, :],
                                           RING[:, c % 8, k * D + 512 * h:k * D + 512 * h + 512],
                                           start=i + k == 0, stop=i == 3 and k == 1)
                    ins.then_inc(used, 1)
            pe.wait_ge(yh, 2 * p + 2)
            pe.wait_ge(yl, 2 * p + 2)
            for i in range(2 * TT):
                t, c = slice(i // 2 * P, i // 2 * P + P), slice(512 * (i % 2), 512 * (i % 2) + 512)
                pe.wait_ge(acc, 8 * p + i + 1)
                T.matmul(SC_[i % 2][:, :], SS[:, t], YHM[:, c], start=True, stop=False)
                T.matmul(SC_[i % 2][:, :], SS[:, t], YLM[:, c], start=False, stop=True).then_inc(sct, 1)

    block = ctx.enter_context(nc.Block())
    xv = x[0].rearrange("(t p) d -> t p d", p=P)

    @block.sync
    def _(sp):
        sp.dma_start(MEMT[:, :, :], mem[0].rearrange("(t p) d -> p t d", p=P)).then_inc(mem_in, 16)
        for st in plan:
            if st.kind == "unit":
                u, K = st.u, st.K
                if u >= 2:
                    sp.wait_ge(s["w_lo"], u - 1)
                dst = RAW[:, u % 2, :K * UC].rearrange("p (k c) -> p k c", c=UC)
                if st.evac == "ffn":
                    for g in range(2):
                        src = st.w[:, g * DFF + st.c0:g * DFF + st.c0 + P].rearrange("(k p) c -> p k c", p=P)
                        sp.dma_start(dst[:, :, g * P:g * P + P], src).then_inc(raw_in[u % 2], 16)
                else:
                    src = st.w[st.row0:st.row0 + K * P, st.c0:st.c0 + UC].rearrange("(k p) c -> p k c", p=P)
                    for h in range(2):
                        kk = slice(h * K // 2, (h + 1) * K // 2)
                        sp.dma_start(dst[:, kk, :], src[:, kk, :]).then_inc(raw_in[u % 2], 16)
                if u == 1:
                    for t in range(TT):
                        sp.dma_start(X[:, t, :], xv[t]).then_inc(x_in, 16)
            elif st is router:
                experts_sp(sp)
        if stop:
            wait(sp, "nrm", last_step.end)
            sp.dma_start(out[0].rearrange("(t p) d -> p t d", p=P), X[:, :, :]).then_inc(out_in, 16)
            sp.wait_ge(out_in, 16)

    @block.gpsimd
    def _(pool):
        for q in range(16):
            pool.dma_start(win_rpb[q], bass.AP(rpb.tensor, rpb.offset + 15 - q, [[31, 120], [1, 48]])).then_inc(win_in, 16)
        pool.memset(BD[:, :, :, :], 0.0).then_inc(bd0, 1)
        pool.wait_ge(bd0, 1)
        for w, wd in enumerate((w_rg, w_ig)):
            for q in range(2):
                pool.dma_start(BD[q * 64:q * 64 + 64, w, :, q * 64:q * 64 + 64],
                               wd[0].rearrange("(c q) i o -> q i c o", q=2)[q]).then_inc(bd_in, 16)
        for st in plan:
            if st is fin:
                wait(pool, "evD", st.at)
                pool.dma_start(GFIN[:, :], rows[0].partition_broadcast(P)).then_inc(rows_in, 16)
            elif st.kind == "save":
                wait(pool, "nrm", st.at)
                pool.dma_start(xd, X[:, :, :]).then_inc(s["saved"], 16)
            elif st.kind == "rope":
                wait(pool, "mx", st.at)
                pool.dma_start(X[:, :, :], xd).then_inc(xre_in, 16)
            elif st is ln1:
                wait(pool, "ms_lo", st.at)
                for i in range(2):
                    pool.dma_start(LNR[:, i, :], rows[1 + i].partition_broadcast(P)).then_inc(rows_in, 16)
            elif st is router:
                for t in range(TT):
                    pool.wait_ge(s["x2h"], t + 1)
                    nc.gpsimd.tensor_tensor(X2L[:, t, :], X[:, t, :], X2H[:, t, :].bitcast(F32),
                                            ALU.subtract).then_inc(s["x2l"], 1)
                wait(pool, "tx_hi", st.at)
                pool.wait_ge(s["x2l"], TT)
                for t in range(TT):
                    nc.gpsimd.tensor_scalar(X[:, t, :], X[:, t, :], ALPHA, 1.0, ALU.mult,
                                            ALU.mult).then_inc(s["xal"], 1)
            elif st is txx:
                wait(pool, "saved", st.at)
                wait(pool, "tx_lo", st.end)
                pool.wait_ge(win_in, 16 * 16)
                for r in range(8):
                    src = bass.AP(win_rpb.tensor, (7 - r) * 48, [[120 * 48, 16], [15 * 48, 8], [1, 8 * 48]])
                    pool.dma_start(B48[r::8, :, :, :].rearrange("p h r j -> p h (r j)"), src).then_inc(b48_in, 16)
            elif st is band:
                wait(pool, "evA", st.at)
                wait(pool, "evD", st.at)
                for cb, bs in enumerate((0, 8, 24, 32)):
                    for b in range(2):
                        for a in range(2):
                            pool.dma_start(VB[(2 * b + a) * 32:(2 * b + a) * 32 + 32, cb, :, :],
                                           VN[a * 64 + bs:a * 64 + bs + 32, b::2, :]).then_inc(s["band"], 16)

    @block.scalar
    def _(act):
        chain = Chain(act, "act_chain")
        link = chain.link
        A = nc.scalar.activation
        act.dma_start(CST[:, :], consts[:, 0:C_N1]).then_inc(consts_in, 16)
        act.dma_start(VEC[:, :], vecs).then_inc(consts_in, 16)
        act.wait_ge(consts_in, 32)
        eps6, eps5, one = CST[:, C_EPS6:C_EPS6 + 1], CST[:, C_EPS5:C_EPS5 + 1], CST[:, C_ONE:C_ONE + 1]

        def split_hi(u):
            if u >= len(units):
                return
            n = units[u].K * UC
            act.wait_ge(raw_in[u % 2], 32 * (u // 2 + 1))
            if u >= 2:
                act.wait_ge(s["res"], units[u - 1].r0)
            A(WH[:, u % 2, :n], RAW[:, u % 2, :n], ACT.Copy).then_inc(s["w_hi"], 1)

        def evacuate(st):
            for r, who in enumerate(st.who):
                n = st.r0 + r
                bank = LIN[n % 3]
                if st.evac == "ffn" and r == 1:
                    act.wait_ge(s["evD"], res_shares[n][1])
                    f = st.kw["f"]
                    A(AH[:, f, :], FP[:, f % 2, :], ACT.Copy).then_inc(s["act_hi"], 1)
                if who != "act":
                    continue
                act.wait_ge(s["res"], n + 1)
                if st.evac == "ffn":
                    ins = A(FG[:, st.kw["f"] % 2, :], bank[:, :], ACT.Silu)
                elif st.evac == "gate":
                    wait(act, "evD", st.at)
                    ins = A(GT[:, r, :], bank[:, :], ACT.Sigmoid,
                            bias=vec(V_BG + 8 * st.kw["g"] + 2 * st.kw["j"] + r))
                elif st.evac == "naq":
                    ins = A(st.dst(r).rearrange("p (b c r) -> p r b c", b=4, c=16),
                            bank[:, :].rearrange("p (r b c) -> p r b c", r=8, b=4), ACT.Copy, scale=0.125)
                elif st.evac == "scaled":
                    ins = A(st.dst(r), bank[:, :], ACT.Copy, scale=st.kw["scale"])
                else:
                    ins = A(st.dst(r), shaped(st, bank), ACT.Copy)
                ins.then_inc(s["evA"], 1)

        def scores(a):
            n = a.n
            if a.att == "stick":
                for j in range(2):
                    nk = a.nkt[j] * P
                    act.wait_ge(s["qk"], 2 * n + j + 1)
                    link(A(SE[:, j, :nk], SB[j][:, :nk], ACT.Abs))
                    link(A(SE[:, j, :nk], SE[:, j, :nk], ACT.Exp, scale=-1.0))
                    A(SE[:, j, :nk], SE[:, j, :nk], ACT.Ln, bias=one).then_inc(s["e_ab"], 1)
            for j in range(2):
                nk = a.nkt[j] * P
                if n >= 2:
                    act.wait_ge(s["tr"], n - 1)
                if a.att == "stick":
                    act.wait_ge(s["st_d"], a.at.get("st_d", 0) + j + 1)
                    A(PB[:, n % 2, j, :nk], SE[:, j, :nk], ACT.Exp).then_inc(s["p"], 1)
                else:
                    act.wait_ge(s["mx"], a.at.get("mx", 0) + j + 1)
                    c = 2 * (n % 2) + j
                    src = SN[:, j, :] if a.att == "na" else SB[j][:, :nk]
                    A(PB[:, n % 2, j, :nk], src, ACT.Exp, bias=ST[:, 16 + c:17 + c],
                      accum_out=ST[:, 20 + c:21 + c]).then_inc(s["p"], 1)

        split_hi(0)
        for st in plan:
            k = st.kind
            if k == "unit":
                split_hi(st.u + 1)
                evacuate(st)
            elif k == "tx":
                for f in range(st.nf):
                    act.wait_ge(s["tx_ps"], st.n0 + f + 1)
                    src, dst = TR[(st.n0 + f) % 2][:, :st.T * P], st.dh[:, f, :]
                    if st.perm:
                        src = src.rearrange("p (b c r) -> p b c r", b=4, c=16)
                        dst = dst.rearrange("p (r b c) -> p b c r", r=8, b=4)
                    scale = st.const if st.scale is None else vec(st.scale + f)
                    A(dst, src, ACT.Copy, scale=scale).then_inc(s["tx_hi"], 1)
            elif k == "rms":
                if "ready" in st.kw:
                    act.wait_ge(*st.kw["ready"])
                    wait(act, "tx_ps", st.kw["war"].end)
                else:
                    wait(act, "evD", st.at)
                    wait(act, "o", st.at)
                for t in range(TT):
                    dump = PB[:, t // 2, t % 2, :] if st.dst is YT else XN[:, t, :]
                    ins = A(dump, st.src[:, t, :], ACT.Square, accum_out=ST[:, t:t + 1])
                link(ins)
                A(ST[:, 4:8], ST[:, 0:4], ACT.Sqrt, scale=1.0 / st.d, bias=eps6).then_inc(s["sd"], 1)
            elif k == "ln":
                layer_norm_act(act, st.end)
            elif k == "lgate":
                for c in range(4):
                    for w, dst in enumerate((LR, LI)):
                        act.wait_ge(s["gmm"], 2 * c + w + 1)
                        A(dst[:, c, :], (SB, TR)[c % 2][w][:, :], ACT.Sigmoid,
                          bias=vec((V_BRG, V_BIG)[w] + c)).then_inc(s["sig"], 1)
            elif k == "lrec":
                link(A(ST[:, 32:36], vec(V_LAM, 4), ACT.Abs))
                link(A(ST[:, 32:36], ST[:, 32:36], ACT.Exp, scale=-1.0))
                link(A(ST[:, 36:40], vec(V_LAM, 4), ACT.Relu, scale=-1.0))
                A(ST[:, 32:36], ST[:, 32:36], ACT.Ln, bias=one).then_inc(s["lexp"], 1)
                act.wait_ge(s["lgl"], 1)
                act.wait_ge(s["sig"], 8)
                act.wait_ge(s["conv"], 1)
                for c in range(4):
                    A(LTH[:, c, :], LR[:, c, :], ACT.Tanh, scale=ST[:, 40 + c:41 + c])
                for c in range(4):
                    ins = A(LR[:, c, :], LR[:, c, :], ACT.Exp, scale=ST[:, 44 + c:45 + c])
                ins.then_inc(s["lt"], 1)
                A(LG[:, :, :], LG[:, :, :], ACT.Gelu_apprx_tanh).then_inc(s["lsq"], 1)
                act.wait_ge(s["lm2"], 1)
                A(LTH[:, :, :], LTH[:, :, :], ACT.Sqrt).then_inc(s["lsq"], 1)
            elif k == "lout":
                act.wait_ge(s["lrec"], 1)
                A(TMP[:, :, :], YL_[:, :, :], ACT.Square).then_inc(s["ysq"], 1)
                act.wait_ge(s["ysum"], 1)
                A(RBC[:, :], SB[0][:, :], ACT.Sqrt, scale=1.0 / 512, bias=eps6).then_inc(s["ysd"], 1)
                act.wait_ge(s["yn"], 1)
                wait(act, "res", st.at)
                for c in range(4):
                    A(XH[:, c, :], YL_[:, c, :], ACT.Copy, scale=vec(V_GLRU + c)).then_inc(s["yhi"], 1)
            elif k == "rope":
                for t in range(TT):
                    act.wait_ge(s["rms_q"], t + 1)
                    A(ST[:, 114:124], ST[:, 104:114], ACT.Sqrt, bias=eps6).then_inc(s["rsd_q"], 1)
            elif k == "logexp":
                act.preload_act_table_set("natural_log_exp_and_others")
            elif k == "S":
                scores(st)
            elif k == "T":
                act.wait_ge(s["tr"], st.a.n + 1)
                if st.a.n:
                    act.wait_ge(s["pv"], st.a.n)
                for o, i in pieces(st.a, 0):
                    ins = A(o, i, ACT.Copy)
                ins.then_inc(s["ptA"], 1)
            elif k == "msplit":
                wait(act, "evD", st.at)
                wait(act, "res", st.at)
                for f in range(KT):
                    A(XH[:, f, :], MG[:, f, :], ACT.Copy).then_inc(s["ms_hi"], 1)
        if not stop:
            experts_act(act, chain)

    @block.vector
    def _(dve):
        chain = Chain(dve, "dve_chain")
        link = chain.link
        V = nc.vector
        dve.wait_ge(consts_in, 32)

        def split_lo(u):
            if u >= len(units):
                return
            n = units[u].K * UC
            dve.wait_ge(s["w_hi"], u + 1)
            V.tensor_tensor(WL[:, u % 2, :n], RAW[:, u % 2, :n], WH[:, u % 2, :n].bitcast(F32),
                            ALU.subtract).then_inc(s["w_lo"], 1)

        def evacuate(st):
            for r, who in enumerate(st.who):
                if who != "dve":
                    continue
                n = st.r0 + r
                bank = LIN[n % 3]
                dve.wait_ge(s["res"], n + 1)
                if st.evac in ("accX", "mixX"):
                    xs = X[:, 2 * r:2 * r + 2, st.c0:st.c0 + UC]
                if st.evac == "ffn":
                    f = st.kw["f"]
                    dve.wait_ge(s["evA"], res_shares[n][0])
                    V.tensor_tensor(FP[:, f % 2, :], bank[:, :], FG[:, f % 2, :], ALU.mult).then_inc(s["evD"], 1)
                    dve.wait_ge(s["evD"], res_shares[n][1])
                    dve.wait_ge(s["act_hi"], st.end["act_hi"])
                    V.tensor_tensor(AL[:, f, :], FP[:, f % 2, :], AH[:, f, :].bitcast(F32),
                                    ALU.subtract).then_inc(s["act_lo"], 1)
                elif st.evac == "accX":
                    V.tensor_tensor(xs, shaped(st, bank), xs, ALU.add).then_inc(s["evD"], 1)
                elif st.evac == "mixX":
                    dve.wait_ge(xre_in, 16)
                    V.scalar_tensor_tensor(xs, xs, ALPHA, shaped(st, bank), ALU.mult, ALU.add).then_inc(s["evD"], 1)
                elif st.evac == "branch":
                    dve.wait_ge(s["evA"], st.at["evA"])
                    m, g = MG[:, 2 * st.kw["j"] + r, :], GT[:, r, :]
                    if st.kw["g"] == 0:
                        V.tensor_tensor(m, bank[:, :], g, ALU.mult).then_inc(s["evD"], 1)
                    else:
                        link(V.tensor_tensor(g, bank[:, :], g, ALU.mult))
                        V.tensor_tensor(m, m, g, ALU.add).then_inc(s["evD"], 1)
                else:
                    V.tensor_copy(st.dst(r), shaped(st, bank)).then_inc(s["evD"], 1)

        def scores(a):
            n = a.n
            for j in range(2):
                nk = a.nkt[j] * P
                bank = SB[j][:, :nk]
                c = 2 * (n % 2) + j
                if a.att == "stick":
                    dve.wait_ge(s["e_ab"], 2 * n + j + 1)
                    link(V.scalar_tensor_tensor(SP_[:, j, :nk], bank, 0.0, SE[:, j, :nk], ALU.max, ALU.add))
                    d = slice(nk - P, nk)
                    link(V.tensor_tensor(SP_[:, j, d], SP_[:, j, d], CST[:, C_LT:C_LT + P], ALU.mult))
                    link(V.tensor_tensor_scan(SC[:, j, nk - 1::-1],
                                              ones[:, 0:1].to_broadcast([P, nk]), SP_[:, j, nk - 1::-1],
                                              0.0, ALU.mult, ALU.add))
                    link(V.tensor_tensor(SE[:, j, :nk], bank, SC[:, j, :nk], ALU.subtract))
                    V.tensor_tensor(SE[:, j, d], SE[:, j, d], CST[:, C_NEG:C_NEG + P],
                                    ALU.add).then_inc(s["st_d"], 1)
                    continue
                dve.wait_ge(s["qk"], 2 * n + j + 1)
                if n >= 2:
                    wait(dve, "p", a.at, 3 - j)
                if a.att == "na":
                    cb = a.qt[j]
                    o = (16, 8, 8, 0)[cb]
                    mask = CST[:, C_NAM + 32 * min(cb, 1) + 32 * (cb == 3):][:, :32].unsqueeze(1).to_broadcast([P, 8, 32])
                    sn = SN[:, j, :].rearrange("p (r w) -> p r w", r=8)
                    dve.wait_ge(b48_in, 16 * 8)
                    wait(dve, "p", a.at, 1 - j)
                    link(V.tensor_tensor(sn, bank.rearrange("p (r w) -> p r w", r=8),
                                         B48[:, a.h, :, o:o + 32], ALU.add))
                    link(V.tensor_tensor(sn, sn, mask, ALU.add))
                    bank = SN[:, j, :]
                link(V.tensor_reduce(ST[:, 28 + c:29 + c], bank, AX, ALU.max))
                V.tensor_scalar(ST[:, 16 + c:17 + c], ST[:, 28 + c:29 + c], -1.0, None,
                                ALU.mult).then_inc(s["mx"], 1)

        def output(a):
            n = a.n
            dv = P if a.att == "mem" else 64
            y = YT if a.att == "stick" else YN
            if a.att == "stick":
                dve.wait_ge(s["pv"], n + 1)
                V.tensor_copy(y[:, a.qt[0]:a.qt[0] + 2, 64 * a.h:64 * a.h + 64],
                              PV[:, 0:2 * P].rearrange("p (j c) -> p j c", j=2)[:, :, :64]).then_inc(s["o"], 1)
                return
            c = 2 * (n % 2)
            dve.wait_ge(s["p"], 2 * n + 2)
            dve.wait_ge(s["o"], n)
            link(V.reciprocal(ST[:, 24:26], ST[:, 20 + c:22 + c]))
            dve.wait_ge(s["pv"], n + 1)
            for j in range(2):
                ins = V.tensor_scalar(y[:, a.qt[j], dv * a.h:dv * a.h + dv], PV[:, P * j:P * j + dv],
                                      ST[:, 24 + j:25 + j], None, ALU.mult)
            ins.then_inc(s["o"], 1)

        def rope(st):
            H = 10
            xn = RT[:, 0, :].rearrange("p (h c) -> p h c", h=H)
            t12 = RT[:, 1, :].rearrange("p (i h c) -> p i h c", i=2, h=H)
            t34 = RT[:, 2, :].rearrange("p (i h c) -> p i h c", i=2, h=H)
            wait(dve, "evA", st.at)
            for t in range(TT):
                q = GQT[:, t, :].rearrange("p (h c) -> p h c", h=8)
                kk = KVT[:, t, 0:128].rearrange("p (h c) -> p h c", h=2)
                link(V.tensor_tensor(xn[:, 0:8, :], q, q, ALU.mult))
                link(V.tensor_tensor(xn[:, 8:10, :], kk, kk, ALU.mult))
                link(V.tensor_reduce(ST[:, 104:114], xn, AX, ALU.add))
                V.tensor_scalar(ST[:, 104:114], ST[:, 104:114], 1.0 / 64, None, ALU.mult).then_inc(s["rms_q"], 1)
                dve.wait_ge(s["rsd_q"], t + 1)
                link(V.reciprocal(ST[:, 104:114], ST[:, 114:124]))
                r = ST[:, 104:114].unsqueeze(2)
                link(V.tensor_tensor(xn[:, 0:8, :], q, r[:, 0:8].to_broadcast([P, 8, 64]), ALU.mult))
                link(V.tensor_tensor(xn[:, 8:10, :], kk, r[:, 8:10].to_broadcast([P, 2, 64]), ALU.mult))
                link(V.tensor_tensor(xn[:, 0:8, :], xn[:, 0:8, :],
                                     vec(V_GQ, 64).unsqueeze(1).to_broadcast([P, 8, 64]), ALU.mult))
                link(V.tensor_tensor(xn[:, 8:10, :], xn[:, 8:10, :],
                                     vec(V_GQ + 64, 64).unsqueeze(1).to_broadcast([P, 2, 64]), ALU.mult))
                cs = CST[:, C_COS + 32 * t:C_COS + 32 * t + 32].unsqueeze(1).to_broadcast([P, H, 32])
                sn = CST[:, C_SIN + 32 * t:C_SIN + 32 * t + 32].unsqueeze(1).to_broadcast([P, H, 32])
                x1, x2 = xn[:, :, 0::2], xn[:, :, 1::2]
                V.tensor_tensor(t12[:, 0], x1, cs, ALU.mult)
                V.tensor_tensor(t12[:, 1], x2, sn, ALU.mult)
                V.tensor_tensor(t34[:, 0], x1, sn, ALU.mult)
                link(V.tensor_tensor(t34[:, 1], x2, cs, ALU.mult))
                for i, (ta, op) in enumerate(((t12, ALU.subtract), (t34, ALU.add))):
                    V.tensor_tensor(q[:, :, i::2], ta[:, 0, 0:8], ta[:, 1, 0:8], op)
                    for dup in range(2):
                        kd = KD[:, t, :].rearrange("p (g u c) -> p g u c", g=2, u=2)[:, :, dup, i::2]
                        ins = V.tensor_tensor(kd, ta[:, 0, 8:10], ta[:, 1, 8:10], op)
                ins.then_inc(s["rope"], 1)

        split_lo(0)
        for st in plan:
            k = st.kind
            if k == "unit":
                split_lo(st.u + 1)
                evacuate(st)
            elif k == "tx" and not st.f32:
                for f in range(st.nf):
                    dve.wait_ge(s["tx_hi"], tx_free[st.n0 + f][0])
                    src, hi, lo = TR[(st.n0 + f) % 2][:, :st.T * P], st.dh[:, f, :].bitcast(F32), st.dl[:, f, :]
                    if st.perm:
                        src = src.rearrange("p (b c r) -> p b c r", b=4, c=16)
                        hi, lo = (v.rearrange("p (r b c) -> p b c r", r=8, b=4) for v in (hi, lo))
                    if st.scale is None:
                        ins = V.tensor_tensor(lo, src, hi, ALU.subtract)
                    else:
                        ins = V.scalar_tensor_tensor(lo, src, vec(st.scale + f), hi, ALU.mult, ALU.subtract)
                    ins.then_inc(s["tx_lo"], 1)
            elif k == "rms":
                wait(dve, "sd", st.end)
                V.reciprocal(ST[:, 8:12], ST[:, 4:8]).then_inc(s["rc"], 1)
                wait(dve, "rc", st.end)
                if st.grow is not None:
                    dve.wait_ge(rows_in, 16)
                for t in range(TT):
                    r = ST[:, 8 + t:9 + t]
                    if st.grow is None:
                        ins = V.tensor_scalar(st.dst[:, t, :], st.src[:, t, :], r, None, ALU.mult)
                    else:
                        ins = V.scalar_tensor_tensor(st.dst[:, t, :], st.src[:, t, :], r, st.grow[:, :],
                                                     ALU.mult, ALU.mult)
                    ins.then_inc(s["nrm"], 1)
            elif k == "ln":
                wait(dve, "evD", st.at)
                layer_norm_dve(dve, link, st.end, st.rows, rows_in, 48)
            elif k == "conv":
                wait(dve, "evA", st.after.end)
                wait(dve, "evD", st.after.end)
                link(V.memset(LX[:, :, 0:3], 0.0))
                for c in range(4):
                    link(V.tensor_scalar(LC[:, c, :], LX[:, c, 0:S], vec(V_CW + 4 * c), vec(V_CB + c),
                                         ALU.mult, ALU.add))
                    for i in range(1, 4):
                        ins = V.scalar_tensor_tensor(LC[:, c, :], LX[:, c, i:i + S], vec(V_CW + 4 * c + i),
                                                     LC[:, c, :], ALU.mult, ALU.add)
                        if (c, i) != (3, 3):
                            link(ins)
                ins.then_inc(s["conv"], 1)
            elif k == "lrec":
                dve.wait_ge(s["lexp"], 1)
                link(V.tensor_tensor(ST[:, 32:36], ST[:, 32:36], ST[:, 36:40], ALU.add))
                V.tensor_scalar(ST[:, 40:44], ST[:, 32:36], 8.0, None, ALU.mult)
                V.tensor_scalar(ST[:, 44:48], ST[:, 32:36], -8.0, None, ALU.mult).then_inc(s["lgl"], 1)
                dve.wait_ge(s["lt"], 1)
                link(V.tensor_tensor(TMP[:, :, :], LR[:, :, :], LR[:, :, :], ALU.mult))
                V.scalar_tensor_tensor(LTH[:, :, :], TMP[:, :, :], 1.0, LTH[:, :, :],
                                       ALU.add, ALU.mult).then_inc(s["lm2"], 1)
                link(V.tensor_tensor(LI[:, :, :], LI[:, :, :], LC[:, :, :], ALU.mult))
                dve.wait_ge(s["lsq"], 2)
                link(V.tensor_tensor(LI[:, :, :], LI[:, :, :], LTH[:, :, :], ALU.mult))
                for c in range(4):
                    ins = V.tensor_tensor_scan(TMP[:, c, :], LR[:, c, :], LI[:, c, :], 0.0, ALU.mult, ALU.add)
                link(ins)
                V.tensor_tensor(YL_[:, :, :], TMP[:, :, :], LG[:, :, :], ALU.mult).then_inc(s["lrec"], 1)
            elif k == "lout":
                dve.wait_ge(s["ysd"], 1)
                link(V.reciprocal(RBC[:, :], RBC[:, :]))
                V.tensor_tensor(YL_[:, :, :], YL_[:, :, :], RBC[:, :].unsqueeze(1).to_broadcast([P, 4, S]),
                                ALU.mult).then_inc(s["yn"], 1)
                dve.wait_ge(s["yn"], 1)
                for c in range(4):
                    dve.wait_ge(s["yhi"], c + 1)
                    V.scalar_tensor_tensor(XL[:, c, :], YL_[:, c, :], vec(V_GLRU + c), XH[:, c, :].bitcast(F32),
                                           ALU.mult, ALU.subtract).then_inc(s["ylo"], 1)
            elif k == "S":
                scores(st)
            elif k == "T" and st.counts["ptD"]:
                dve.wait_ge(s["tr"], st.a.n + 1)
                if st.a.n:
                    dve.wait_ge(s["pv"], st.a.n)
                for o, i in pieces(st.a, 1):
                    ins = V.tensor_copy(o, i)
                ins.then_inc(s["ptD"], 1)
            elif k == "O":
                output(st.a)
            elif k == "rope":
                rope(st)
            elif k == "msplit":
                for f in range(KT):
                    wait(dve, "ms_hi", st.at, -f - 1)
                    V.tensor_tensor(XL[:, f, :], MG[:, f, :], XH[:, f, :].bitcast(F32),
                                    ALU.subtract).then_inc(s["ms_lo"], 1)
        if not stop:
            experts_dve(dve, chain)

    @block.tensor
    def _(pe):
        T = nc.tensor
        pe.wait_ge(consts_in, 32)

        def product(st):
            XHs, XLs = SRC[st.src]
            wh, wl = (w[:, st.u % 2, :st.K * UC].rearrange("p (k c) -> p k c", c=UC) for w in (WH, WL))
            pe.wait_ge(s["w_lo"], st.u + 1)
            if st.src == "a":
                wait(pe, "act_lo", st.at)
            wait(pe, "tx_lo", st.at)
            wait(pe, "ylo", st.at)
            wait(pe, "ms_lo", st.at)
            for r in range(len(st.who)):
                n = st.r0 + r
                bank = LIN[n % 3]
                bank_free(pe, n)
                if st.mode == "F":
                    c = slice(P * r, P * r + P)
                    for k in range(st.K):
                        hi, lo = XHs[:, k, :st.nt], XLs[:, k, :st.nt]
                        T.matmul(bank[:, :st.nt], wh[:, k, c], hi, start=k == 0, stop=False)
                        T.matmul(bank[:, :st.nt], wh[:, k, c], lo, start=False, stop=False)
                        ins = T.matmul(bank[:, :st.nt], wl[:, k, c], hi, start=False, stop=k == st.K - 1)
                else:
                    for i in range(2):
                        t = slice((2 * r + i) * P, (2 * r + i + 1) * P)
                        o = bank[:, i * UC:i * UC + UC]
                        for k in range(st.K):
                            T.matmul(o, XHs[:, k, t], wh[:, k, :], start=k == 0, stop=False)
                            T.matmul(o, XHs[:, k, t], wl[:, k, :], start=False, stop=False)
                            ins = T.matmul(o, XLs[:, k, t], wh[:, k, :], start=False, stop=k == st.K - 1)
                ins.then_inc(s["res"], 1)

        def banks_idle(st):
            for name in ("ptA", "ptD", "tx_hi", "tx_lo", "sig", "ysd"):
                wait(pe, name, st.at)

        def qk(a, j):
            b = (a.h % 2) * 64
            h2 = a.h // 2
            qc = slice(a.qt[j] * P, a.qt[j] * P + P)
            if a.att == "stick":
                return QT[b:b + 64, h2, qc], KTT[b:b + 64, h2, 0:a.nkt[j] * P]
            if a.att == "na":
                bs = (0, 8, 24, 32)[a.qt[j]]
                return QT[b:b + 64, h2, qc], KTT[b:b + 64, h2, :].rearrange("p (r c) -> p r c", r=8)[:, :, bs:bs + 32]
            if a.att == "gqa":
                return QG[b:b + 64, h2, qc], KG[b:b + 64, a.h // 4, :]
            return QM[:, a.h, qc], MKT[:, a.h, :]

        def values(a, j, kt):
            if a.att == "stick":
                return VT[:, kt, 64 * a.h:64 * a.h + 64]
            if a.att == "na":
                return VB[:, a.qt[j], kt, 64 * a.h:64 * a.h + 64]
            if a.att == "gqa":
                return KVT[:, kt, 128 + 64 * (a.h // 4):192 + 64 * (a.h // 4)]
            return MV[:, kt, P * a.h:P * a.h + P]

        for st in plan:
            k = st.kind
            if k == "unit":
                product(st)
            elif k == "tx":
                if "ready" in st.kw:
                    pe.wait_ge(*st.kw["ready"])
                for name in ("nrm", "o", "rope"):
                    wait(pe, name, st.at)
                banks_idle(st)
                for f in range(st.nf):
                    n = st.n0 + f
                    if f >= 2:
                        hi, lo = tx_free[n - 2]
                        pe.wait_ge(s["tx_hi"], hi)
                        if lo:
                            pe.wait_ge(s["tx_lo"], lo)
                    for t in range(st.T):
                        ins = T.transpose(TR[n % 2][:, t * P:t * P + P], st.src[:, t, f * P:f * P + P], ident)
                    ins.then_inc(s["tx_ps"], 1)
            elif k == "lgate":
                pe.wait_ge(bd_in, 64)
                pe.wait_ge(s["conv"], 1)
                banks_idle(st)
                for c in range(4):
                    for w in range(2):
                        if c >= 2:
                            pe.wait_ge(s["sig"], 2 * (c - 2) + w + 1)
                        T.matmul((SB, TR)[c % 2][w][:, :], BD[:, w, c, :], LC[:, c, :],
                                 start=True, stop=True).then_inc(s["gmm"], 1)
            elif k == "lout":
                pe.wait_ge(s["ysq"], 1)
                banks_idle(st)
                for c in range(4):
                    ins = T.matmul(SB[0][:, :], ones, TMP[:, c, :], start=c == 0, stop=c == 3)
                ins.then_inc(s["ysum"], 1)
            elif k == "S":
                banks_idle(st)
                wait(pe, "evA", st.after.end)
                wait(pe, "evD", st.after.end)
                wait(pe, "band", st.after.end)
                wait(pe, "tx_hi", st.after.end)
                wait(pe, "p", st.at)
                for j in range(2):
                    q, kk = qk(st, j)
                    o = SB[j][:, 0:st.nkt[j] * P]
                    if st.att == "na":
                        o = o.rearrange("p (r c) -> p r c", r=8)
                    T.matmul(o, q, kk, start=True, stop=True).then_inc(s["qk"], 1)
            elif k == "T":
                wait(pe, "p", st.a.end)
                banks_idle(st)
                for j in range(2):
                    for kt in range(st.a.nkt[j]):
                        c = (kt % 2) * 256 + j * P
                        ins = T.transpose(TR[kt // 2][:, c:c + P], PB[:, st.a.n % 2, j, kt * P:kt * P + P], ident)
                ins.then_inc(s["tr"], 1)
            elif k == "O":
                a = st.a
                wait(pe, "ptA", a.t.end)
                wait(pe, "ptD", a.t.end)
                wait(pe, "o", st.at)
                dv = P if a.att == "mem" else 64
                for j in range(2):
                    for kt in range(a.nkt[j]):
                        ins = T.matmul(PV[:, j * P:j * P + dv], PT[:, kt, j * P:j * P + P], values(a, j, kt),
                                       start=kt == 0, stop=kt == a.nkt[j] - 1)
                ins.then_inc(s["pv"], 1)
        if not stop:
            experts_pe(pe)
    ctx.close()


def _constants():
    c = np.zeros((P, C_N), np.float32)
    row, col = np.arange(P)[:, None], np.arange(P)[None, :]
    c[:, C_ID:C_ID + P] = row == col
    c[:, C_LT:C_LT + P] = col < row
    c[:, C_NEG:C_NEG + P] = np.where(col < row, 0.0, NEG)
    for i, (cb, bs) in enumerate(((0, 0), (1, 8), (3, 32))):
        q = cb * 16 + np.arange(P)[:, None] // 8
        start = np.clip(q - 8, 0, 48)
        k = bs + np.arange(32)[None, :]
        c[:, C_NAM + 32 * i:C_NAM + 32 * i + 32] = np.where((k >= start) & (k < start + 16), 0.0, NEG)
    c[:, C_ONE:C_ONE + P] = 1.0
    c[:, C_TC:C_TC + 4] = np.arange(P)[:, None] + P * np.arange(4)[None, :]
    c[:, C_EPS6], c[:, C_EPS5] = 1e-6, 1e-5
    t = np.arange(S)
    inv = np.float32(10000.0) ** (-np.arange(0, 32, 2, dtype=np.float32) / np.float32(32))
    ang = np.concatenate([(t // 64).astype(np.float32)[:, None] * inv, (t % 64).astype(np.float32)[:, None] * inv], 1)
    for at, f in ((C_COS, np.cos), (C_SIN, np.sin)):
        c[:, at:at + 128] = f(ang).astype(np.float32).reshape(TT, P, 32).transpose(1, 0, 2).reshape(P, 128)
    c[:, C_IOTA:C_IOTA + S] = t[None, :]
    return c


def kernel(**inputs):
    import concourse.bacc as _bacc
    from concourse.bass_utils import run_bass_kernel_spmd as _run

    a = {k: np.ascontiguousarray(v) for k, v in inputs.items()}

    def cols(v):
        return v.reshape(-1, P).T

    conv = a["conv_w"][0].reshape(4, 4, P).transpose(2, 1, 0).reshape(P, 16)
    vecs = np.concatenate(
        [cols(a["norm_mix"]), cols(a["norm_ffn"]), conv, cols(a["conv_b"]), cols(a["b_rg"]), cols(a["b_ig"]),
         cols(a["lru_lambda"]), cols(a["norm_lru_out"]), cols(a["norm_att_out"]), cols(a["b_gate_2"]),
         np.tile(a["gqa_q_gain_2"], (P, 1)), np.tile(a["gqa_k_gain_2"], (P, 1))], axis=1)
    rows = np.concatenate([a["norm_final"][None], a["ln1_g_2"], a["ln1_b_2"], a["ln2_g_2"], a["ln2_b_2"]])
    rpb = np.concatenate([np.zeros(16, np.float32), a["na_rpb_2"].reshape(-1), np.zeros(64, np.float32)])
    arrays = dict(
        x=a["x"], w_in=a["w_in"], w_out=a["w_out"], w_ffn_in=a["w_ffn_in"], w_ffn_out=a["w_ffn_out"],
        mem=a["mem_2"], w_in2=a["w_in_2"], w_memkv=a["w_mem_kv_2"], w_branch=a["w_branch_2"],
        w_out2=a["w_out_2"], w_router=a["w_router_2"], w_gu=a["w_gate_up_2"], w_down=a["w_down_2"],
        w_rg=a["w_rg"], w_ig=a["w_ig"], rows=rows, rpb=rpb, vecs=vecs, consts=_constants())
    arrays = {k: np.ascontiguousarray(v) for k, v in arrays.items()}
    nc = _bacc.Bacc("TRN2", target_bir_lowering=False, num_devices=1)
    args = {k: nc.dram_tensor(k, v.shape, F32, kind="ExternalInput").ap() for k, v in arrays.items()}
    args["out"] = nc.dram_tensor("out", (1, S, D), F32, kind="ExternalOutput").ap()
    build(nc, **args)
    return _run(nc, [arrays], core_ids=[0]).results[0]["out"]
```

```python
from contextlib import ExitStack

import numpy as np
import concourse.bass as bass
from concourse import mybir

P = 128
S = 512
D = 1024
KT = D // P
TT = S // P
UC = 256
DFF = 2816
E = 16
CAP = 64
DFE = 1024
M = 256
QE = 4
RS = 6
ALPHA = 2.0 ** 0.25
NEG = -1e30

F32 = mybir.dt.float32
F32R = mybir.dt.float32r
U32 = mybir.dt.uint32
ALU = mybir.AluOpType
ACT = mybir.ActivationFunctionType
AX = mybir.AxisListType.X

C_ID, C_LT, C_NEG, C_NAM, C_ONE, C_TC = 0, 128, 256, 384, 480, 608
C_EPS6, C_EPS5, C_COS, C_SIN, C_IOTA = 612, 613, 614, 742, 870
C_N1 = C_IOTA
C_N = C_IOTA + S
V_GMIX, V_GFFN, V_CW, V_CB, V_BRG, V_BIG, V_LAM, V_GLRU, V_GATT, V_BG, V_GQ = 0, 8, 16, 32, 36, 40, 44, 48, 52, 56, 80
V_N = 80 + 128


class Step:

    def __init__(self, kind, counts, after=None, kw=None, dst=None, src=None,
                 u=None, w=None, c0=0, K=KT, mode=None, evac=None, nt=S, row0=0, who=(), r0=0,
                 dh=None, dl=None, nf=0, T=TT, scale=None, perm=False, f32=False, const=1.0, n0=0,
                 d=0, grow=None, rows=None,
                 att=None, h=0, half=0, n=0, qt=(), nkt=(), a=None):
        self.kind, self.counts, self.after, self.kw, self.dst, self.src = kind, counts, after, kw, dst, src
        self.u, self.w, self.c0, self.K, self.mode, self.evac = u, w, c0, K, mode, evac
        self.nt, self.row0, self.who, self.r0 = nt, row0, who, r0
        self.dh, self.dl, self.nf, self.T, self.scale = dh, dl, nf, T, scale
        self.perm, self.f32, self.const, self.n0 = perm, f32, const, n0
        self.d, self.grow, self.rows = d, grow, rows
        self.att, self.h, self.half, self.n, self.qt, self.nkt, self.a = att, h, half, n, qt, nkt, a
        self.c = self.o = None


def number(plan):
    at = {}
    for st in plan:
        st.at = dict(at)
        for s, n in st.counts.items():
            at[s] = at.get(s, 0) + n
        st.end = dict(at)
    return at


def build(nc, x, w_in, w_out, w_ffn_in, w_ffn_out, mem, w_in2, w_memkv, w_branch, w_out2, w_router,
          w_gu, w_down, w_rg, w_ig, rows, rpb, vecs, consts, out, stop=None):
    ctx = ExitStack()
    base = (nc.sbuf_base + 63) // 64 * 64

    def at(name, kb, shape, dt=F32):
        return nc.alloc_sbuf_tensor_at(name, shape, dt, offset=base + int(kb * 1024), align_bytes=32)

    def sem(name):
        return ctx.enter_context(nc.semaphore(name))

    XH = at("XH", 0, [P, KT, S], F32R)
    XL = at("XL", 16, [P, KT, S], F32R)
    X2T = at("X2T", 0, [P, KT, S])
    WH = at("WH", 32, [P, 2, KT * UC], F32R)
    WL = at("WL", 48, [P, 2, KT * UC], F32R)
    AH = at("AH", 64, [P, KT, S], F32R)
    AL = at("AL", 80, [P, KT, S], F32R)
    XN = at("XN", 64, [P, TT, D])
    MEMT = at("MEMT", 64, [P, 2, D])
    MH = at("MH", 144.5, [P, KT, M], F32R)
    ML = at("ML", 152.5, [P, KT, M], F32R)
    LX = at("LX", 64, [P, 4, 3 + S])
    LTH = at("LTH", 64, [P, 4, S])
    LG = at("LG", 72.25, [P, 4, S])
    LC = at("LC", 80.5, [P, 4, S])
    LI = at("LI", 88.5, [P, 4, S])
    YL_ = at("YL_", 80.5, [P, 4, S])
    SE = at("SE", 64, [P, 2, 2, S])
    SP_ = at("SP_", 72, [P, 2, S])
    SC = at("SC", 92, [P, 2, S])
    RBC = at("RBC", 78, [P, S])
    YH2 = at("YH2", 64, [P, 4, S], F32R)
    YL2 = at("YL2", 80, [P, 4, S], F32R)
    SN = at("SN", 64, [P, 2, 2, M])
    TMP = at("TMP", 189.5, [P, 4, S])
    VN = at("VN", 72, [P, TT, 512])
    GQT = at("GQT", 88, [P, TT, 512])
    GT = at("GT", 88, [P, 2, S])
    R0 = 96.5
    LR = at("LR", R0 + 40, [P, 4, S])
    RAW = at("RAW", R0, [P, 2, KT * UC])
    RING = at("RING", R0, [P, RS, 2048])
    QT = at("QT", R0 + 16, [P, 4, S])
    KTT = at("KTT", R0 + 24, [P, 4, S])
    VT = at("VT", R0 + 32, [P, TT, 512])
    YT = at("YT", R0 + 40, [P, TT, 512])
    FG = at("FG", R0 + 16, [P, 2, S])
    FP = at("FP", R0 + 20, [P, 2, S])
    VB = at("VB", R0 + 32, [P, 4, 2, 512])
    QG = at("QG", R0 + 16, [P, 4, S])
    KG = at("KG", R0 + 24, [P, 2, S])
    QM = at("QM", R0 + 32, [P, 4, S])
    RT = at("RT", R0 + 24, [P, 3, 640])
    GFIN = at("GFIN", R0 + 16, [P, D])
    LNR = at("LNR", 64, [P, 2, D])
    MG = at("MG", R0 + 48, [P, KT, S])
    KD = at("KD", R0 + 40, [P, TT, 256])
    X = at("X", 160.5, [P, TT, D])
    B48 = at("B48", 160.5, [P, 8, 8, 48])
    CST = at("CST", 176.5, [P, C_N1])
    VEC = at("VEC", 180, [P, V_N])
    ST = at("ST", 181, [P, 128])
    MKT = at("MKT", 181.5, [P, 4, M])
    MV = at("MV", 185.5, [P, 2, 512])
    PB = at("PB", 189.5, [P, 2, 2, S])
    PT = at("PT", 197.5, [P, 4, 256])
    KVT = at("KVT", 201.5, [P, TT, 256])
    BD = at("BD", 201.5, [P, 2, 4, P])
    YN = at("YN", 72, [P, TT, 512])
    IDB = at("IDB", 0, [P, E * CAP])
    OHT = at("OHT", 4, [P, TT, QE * CAP], F32R)
    XS = at("XS", 8, [P, KT, QE, 2, CAP], F32R)
    SS = at("SS", 24, [P, 2, S], F32R)
    HT = at("HT", 28, [P, 2, KT, 2, CAP], F32R)
    GUS = at("GUS", 36, [CAP, 4 * 512])
    LOH = at("LOH", 44, [CAP, 4 * 512])
    SG = at("SG", 52, [CAP, DFE])
    YHM = at("YHM", 56, [P, 2, D], F32R)
    YLM = at("YLM", 197.5, [P, 2, D], F32R)
    IOTA = at("IOTA", 205.5, [P, S])
    GCOL = at("GCOL", 180.8125, [P, E])
    ICOL = at("ICOL", 180.875, [P, E])
    WEH = [at(f"WEH{i}", 181.5 + 8 * i, [P, 2048], F32R) for i in range(2)]
    WEL = [at(f"WEL{i}", R0 + 48 + 8 * i, [P, 2048], F32R) for i in range(2)]
    LN2R = at("LN2R", 0, [P, 2, D])
    AF = at("AF", 56, [E, S])
    VAL = at("VAL", 58, [E, 2 * CAP])
    IDX = at("IDX", 58.5, [E, 2 * CAP])
    IDU = at("IDU", 59, [E, CAP], U32)
    WR = at("WR", 60, [P, KT, E])
    LGT = at("LGT", 61, [P, TT, E])
    X2H = at("X2H", 64, [P, TT, D], F32R)
    X2L = at("X2L", 80, [P, TT, D], F32R)

    ps = [ctx.enter_context(nc.psum_tensor(f"bank{i}", [P, 512], F32)) for i in range(8)]
    LIN, SB, TR, PV = ps[0:3], ps[3:5], ps[5:7], ps[7]

    ident = CST[:, C_ID:C_ID + P]
    ones = CST[:, C_ONE:C_ONE + P]

    def vec(c, n=1):
        return VEC[:, c:c + n]

    raw_in = [sem(f"raw_in{i}") for i in range(2)]
    names = """w_hi w_lo res evA evD act_hi act_lo tx_ps tx_hi tx_lo ms sd rc nrm conv gmm sig
               lexp lgl lt lm2 lsq lrec ysq ysum ysd yn yhi ylo qk mx e_ab st_d p tr ptA ptD pv o rope gk
               ms_hi ms_lo saved band x2h x2l xal lgp lgs afp af top ixp ixc icp icc fin""".split()
    names.extend(["rms_q", "rsd_q"])
    s = {n: sem(n) for n in names}
    consts_in, mem_in, x_in, rows_in, b48_in, xre_in, out_in, bd_in, bd0, moe_in = (
        sem(n) for n in "consts_in mem_in x_in rows_in b48_in xre_in out_in bd_in bd0 moe_in".split())
    xd = nc.dram_tensor("x_saved", (S, D), F32, kind="Internal").ap().rearrange("(t p) d -> p t d", p=P)

    win_rpb = nc.dram_tensor("win_rpb", (16, 120, 48), F32, kind="Internal").ap()
    win_in = sem("win_in")

    rows2_in = sem("rows2_in")

    def wait(e, name, values, less=0):
        v = values.get(name, 0) - less
        if v > 0:
            e.wait_ge(s[name], v)

    plan = []
    units, results, txs = [], [], []
    narrow = []
    lin_of, prev_of = [], []

    def add(kind, counts, **kw):
        st = Step(kind, counts, **kw)
        plan.append(st)
        return st

    def unit(w, c0, K, mode, evac, dst=None, src="x", nt=S, row0=0, **kw):
        nres = 2 if mode == "F" else nt // 256
        shares = {"act": (1, 0), "dve": (0, 1)}
        sh = []
        for r in range(nres):
            if evac == "ffn":
                sh.append("act" if r == 0 else "dve")
            elif evac in ("accX", "mixX", "branch"):
                sh.append("dve")
            elif evac in ("gate", "naq", "scaled"):
                sh.append("act")
            else:
                sh.append("act" if (r + len(units)) % 2 else "dve")
        counts = dict(w_hi=1, w_lo=1, res=nres, evA=sh.count("act"), evD=sh.count("dve"))
        if evac == "ffn":
            counts.update(act_hi=1, act_lo=1)
        st = add("unit", counts, u=len(units), w=w, c0=c0, K=K, mode=mode, evac=evac, dst=dst, src=src,
                 nt=nt, row0=row0, who=sh, r0=len(results), kw=kw)
        units.append(st)
        for r in range(nres):
            b = (len(results) if not lin_of else lin_of[-1] + 1) % (2 if narrow else 3)
            prev_of.append(max((i for i, c in enumerate(lin_of) if c == b), default=None))
            lin_of.append(b)
            results.append((st, r))
        return st

    def tx(src, dh, dl, nf, T, scale=None, perm=False, f32=False, const=1.0, **kw):
        st = add("tx", dict(tx_ps=nf, tx_hi=nf, tx_lo=0 if f32 else nf), src=src, dh=dh, dl=dl, nf=nf,
                 T=T, scale=scale, perm=perm, f32=f32, const=const, n0=len(txs), kw=kw)
        txs.extend([st] * nf)
        return st

    def rms(src, dst, d, grow=None, **kw):
        return add("rms", dict(sd=1, rc=1, nrm=TT), src=src, dst=dst, d=d, grow=grow, kw=kw)

    atts = []

    def attention(kind, heads, halves, fill, after):
        n = heads * halves
        mine = []
        per = len(fill) / n
        done = 0
        narrow.append(True)

        def s_step(i):
            h, half = divmod(i, halves)
            a = add("S", dict(qk=2), att=kind, h=h, half=half, n=len(atts), after=after, r0=len(results))
            a.counts.update(dict(e_ab=2, st_d=2) if kind == "stick" else dict(mx=2))
            a.qt = [2 * half, 2 * half + 1]
            a.nkt = [q + 1 for q in a.qt] if kind == "stick" else [4, 4] if kind == "gqa" else [2, 2]
            mine.append(a)
            atts.append(a)

        def x_step(i):
            add("X", dict(p=2), a=mine[i])

        def t_step(i):
            add("T", dict(tr=1), a=mine[i])

        def c_step(i):
            mine[i].c = add("C", dict(ptA=1, ptD=int(mine[i].nkt[1] > 2)), a=mine[i])

        def o_step(i):
            mine[i].o = add("O", dict(pv=1, o=1), a=mine[i])

        turn = (((x_step, 2), (s_step, 0), (o_step, 3), (t_step, 2), (c_step, 2)) if kind == "stick" else
                ((c_step, 2), (s_step, 0), (o_step, 2), (x_step, 1), (t_step, 1)))
        for i in range(n + max(lag for _, lag in turn)):
            for f, lag in turn:
                if 0 <= i - lag < n:
                    f(i - lag)
            while done < len(fill) and done < per * (i + 1):
                fill[done]()
                done += 1
        narrow.clear()
        return mine[-1].o

    win, win2 = w_in[0], w_in2[0]
    tx_mem = tx(MEMT, MH, ML, KT, 2, ready=(mem_in, 16))
    rms(X, XN, D, ready=(x_in, 64), war=tx_mem)
    tx(XN, XH, XL, KT, TT, scale=V_GMIX)
    for j in range(2):
        unit(win, UC * j, KT, "F", "copy", dst=lambda r, j=j: LX[:, 2 * j + r, 3:])
    lxu = plan[-1]
    conv = add("conv", dict(conv=1), after=lxu)
    for j in range(2):
        unit(win, 512 + UC * j, KT, "F", "copy", dst=lambda r, j=j: LG[:, 2 * j + r, :])
    lgu = plan[-1]
    add("lgate", dict(gmm=8, sig=8), after=lgu)
    for j in range(2):
        unit(win, 1024 + UC * j, KT, "F", "scaled", dst=lambda r, j=j: QT[:, 2 * j + r, :], scale=0.125)
    lrec = add("lrec", dict(lexp=1, lm2=1, lsq=1, lt=1, lgl=1, lrec=1), after=lgu)
    for j in range(2):
        unit(win, 1536 + UC * j, KT, "F", "copy", dst=lambda r, j=j: KTT[:, 2 * j + r, :])
    for j in range(2):
        unit(win, 2048 + UC * j, KT, "T", "copy", dst=lambda r, j=j: VT[:, 2 * r:2 * r + 2, UC * j:UC * j + UC])
    qkv = plan[-1]
    lout = add("lout", dict(ysq=1, ysum=1, ysd=1, yn=1, yhi=4, ylo=4), after=qkv)
    add("logexp", {})
    last = attention("stick", 8, 2, [], qkv)
    rms(YT, YT, 512, after=last)
    tx(YT, XH[:, 4:8], XL[:, 4:8], 4, TT, scale=V_GATT)
    for j in range(4):
        unit(w_out[0], UC * j, KT, "T", "accX")
    rms(X, XN, D, after=plan[-1])
    tx(XN, XH, XL, KT, TT, scale=V_GFFN)
    for f0, nf in ((0, 8), (8, 8), (16, 6)):
        for f in range(f0, f0 + nf):
            unit(w_ffn_in[0], P * f, KT, "F", "ffn", f=f - f0)
        for j in range(4):
            unit(w_ffn_out[0], UC * j, nf, "T", "accX", src="a", row0=P * f0)
    fin = rms(X, X, D, grow=GFIN, after=plan[-1])
    end1 = len(plan)
    save = add("save", dict(saved=16))
    txx = tx(X, XH, XL, KT, TT)
    for j in range(2):
        unit(win2, UC * j, KT, "F", "naq", dst=lambda r, j=j: QT[:, 2 * j + r, :])
    for j in range(2):
        unit(win2, 512 + UC * j, KT, "F", "copy", dst=lambda r, j=j: KTT[:, 2 * j + r, :])
    for j in range(2):
        unit(win2, 1024 + UC * j, KT, "T", "copy", dst=lambda r, j=j: VN[:, 2 * r:2 * r + 2, UC * j:UC * j + UC])
    naqkv = plan[-1]
    band = add("band", dict(band=16 * 16), after=naqkv)
    for j in range(2):
        unit(win2, 1536 + UC * j, KT, "T", "copy", dst=lambda r, j=j: GQT[:, 2 * r:2 * r + 2, UC * j:UC * j + UC])
    fill = [lambda: unit(win2, 2048, KT, "T", "copy", dst=lambda r: KVT[:, 2 * r:2 * r + 2, :])]
    fill += [lambda j=j: unit(w_memkv[0], UC * j, KT, "F", "copy", dst=lambda r, j=j: MKT[:, 2 * j + r, :],
                              src="m", nt=M) for j in range(2)]
    fill += [lambda j=j: unit(w_memkv[0], 512 + UC * j, KT, "T", "copy",
                              dst=lambda r, j=j: MV[:, :, UC * j:UC * j + UC], src="m", nt=M) for j in range(2)]
    na_last = attention("na", 8, 2, fill, band)
    for t in range(TT):
        add("rope", dict(rope=1), half=t, after=na_last)
        if t in (1, 2):
            unit(win2, 2304 + UC * (t - 1), KT, "F", "scaled", dst=lambda r, j=t - 1: QM[:, 2 * j + r, :],
                 scale=float(P) ** -0.5)
    tx(YN, YH2, YL2, 4, TT, perm=True)
    tx(GQT, QG, None, 4, TT, f32=True, const=0.125)
    tx(KD, KG, None, 2, TT, f32=True)
    gq = plan[-1]

    def gate(g, j):
        return lambda: unit(win2, 2816 + D * g + UC * j, KT, "F", "gate", g=g, j=j)

    def branch(g, j):
        return lambda: unit(w_branch[0, g], UC * j, 4, "F", "branch", src="y", g=g, j=j)

    fill = []
    for j in range(4):
        fill += [gate(0, j), branch(0, j)]
    gl = attention("gqa", 8, 2, fill, gq)
    tx(YN, YH2, YL2, 4, TT)
    fill = [f for j in range(4) for f in (gate(1, j), branch(1, j))]
    ml = attention("mem", 4, 2, fill, plan[-1])
    tx(YN, YH2, YL2, 4, TT)
    for j in range(4):
        gate(2, j)()
        branch(2, j)()
    add("msplit", dict(ms_hi=KT, ms_lo=KT), after=plan[-1])
    for j in range(4):
        unit(w_out2[0], UC * j, KT, "T", "mixX")
    ln1 = add("ln", dict(ms=1, sd=1, rc=1, nrm=TT), rows=LNR, after=plan[-1])
    end2 = len(plan)
    tx2 = tx(X, X2T, None, KT, TT, f32=True)
    router = add("router", dict(lgp=1, xal=TT))
    if stop == "x1":
        del plan[end1:]
    if stop == "x2":
        del plan[end2:]
    total = number(plan)
    last_step = plan[-1]
    live = set(map(id, plan))
    units = [u for u in units if id(u) in live]
    res_shares = []
    a = d = 0
    for st, r in results:
        a += st.who[r] == "act"
        d += st.who[r] == "dve"
        res_shares.append((a, d))
    tx_free = []
    h = l = 0
    for st in txs:
        h += 1
        l += not st.f32
        tx_free.append((h, l))

    SRC = {"x": (XH, XL), "m": (MH, ML), "a": (AH, AL), "y": (YH2, YL2)}

    def bank_free(e, st, n):
        if prev_of[n] is not None:
            evacuated(e, prev_of[n])
        if lin_of[n]:
            wait(e, "st_d", st.at)
        if lin_of[n] == 2:
            wait(e, "mx", st.at)
            wait(e, "p", st.at)

    class Chain:

        def __init__(self, e, name):
            self.e, self.s, self.n = e, sem(name), 0

        def link(self, ins):
            ins.then_inc(self.s, 1)
            self.n += 1
            self.e.wait_ge(self.s, self.n)

        def sign(self, ins):
            ins.then_inc(self.s, 1)
            self.n += 1
            return self.n

        def need(self, value):
            self.e.wait_ge(self.s, value)


    def pieces(a, b):
        bank = TR[b][:, :].rearrange("p (k q) -> p k q", k=2)
        if a.nkt[0] >= 2 * b + 2:
            return [(PT[:, 2 * b:2 * b + 2, :], bank)]
        return [(PT[:, 2 * b, :], bank[:, 0, :]), (PT[:, 2 * b + 1, P:], bank[:, 1, P:])]

    score_banks, score_prev = [], []
    for a in atts:
        turn = [3, 4, 2, 1] if a.att == "stick" else [3, 4, 2]
        for j in range(2):
            b = turn[(2 * a.n + j) % len(turn)]
            score_prev.append(max((i for i, c in enumerate(score_banks) if c == b), default=None))
            score_banks.append(b)

    def score_bank(a, j):
        return ps[score_banks[2 * a.n + j]]

    def evacuated(e, n):
        a, d = res_shares[n]
        if a:
            e.wait_ge(s["evA"], a)
        if d:
            e.wait_ge(s["evD"], d)

    def score_bank_free(e, a, j):
        for n in range(a.r0 - 1, -1, -1):
            if ps[lin_of[n]] is score_bank(a, j):
                evacuated(e, n)
                break
        q = score_prev[2 * a.n + j]
        if q is not None:
            b = atts[q // 2]
            name = {"stick": "st_d", "na": "mx"}.get(b.att)
            if name:
                e.wait_ge(s[name], b.at.get(name, 0) + q % 2 + 1)
            else:
                e.wait_ge(s["p"], q + 1)

    def shaped(st, bank):
        if st.mode == "F":
            return bank[:, :st.nt]
        return bank[:, :].rearrange("p (t c) -> p t c", t=2)

    def layer_norm_act(act, end):
        wait(act, "ms", end)
        nc.scalar.activation(ST[:, 4:8], ST[:, 97:105:2], ACT.Sqrt,
                             bias=CST[:, C_EPS5:C_EPS5 + 1]).then_inc(s["sd"], 1)

    def layer_norm_dve(dve, link, end, rows_, landed, value):
        V = nc.vector
        for t in range(TT):
            V.bn_stats(ST[:, 48 + 12 * t:54 + 12 * t], X[:, t, 0:512])
            link(V.bn_stats(ST[:, 54 + 12 * t:60 + 12 * t], X[:, t, 512:1024]))
        for t in range(TT):
            ins = V.bn_aggr(ST[:, 96 + 2 * t:98 + 2 * t],
                            ST[:, 48 + 12 * t:60 + 12 * t].rearrange("p (i c) -> p i c", i=2))
        ins.then_inc(s["ms"], 1)
        wait(dve, "sd", end)
        V.reciprocal(ST[:, 8:12], ST[:, 4:8]).then_inc(s["rc"], 1)
        wait(dve, "rc", end)
        wait(dve, "ms", end)
        dve.wait_ge(landed, value)
        for t in range(TT):
            link(V.tensor_scalar(X[:, t, :], X[:, t, :], ST[:, 96 + 2 * t:97 + 2 * t],
                                 ST[:, 8 + t:9 + t], ALU.subtract, ALU.mult))
            link(V.tensor_tensor(X[:, t, :], X[:, t, :], rows_[:, 0, :], ALU.mult))
            V.tensor_tensor(X[:, t, :], X[:, t, :], rows_[:, 1, :], ALU.add).then_inc(s["nrm"], 1)

    QUADS, CH = E // QE, 24
    ring_in = [sem(f"ring_in{i}") for i in range(RS)]
    (wh, wlD, wlP, used, oht, ssr, gth, xsh, xsl, ev_lo, ev, su, hm, tp, hh, hl, yh, yl, sct, acc) = (
        sem(n) for n in "wh wlD wlP used oht ssr gth xsh xsl ev_lo ev su hm tp hh hl yh yl sct acc".split())
    GU = [LIN[0], LIN[1], LIN[2], PV]
    XG = [SB[0], SB[1], GU[2], GU[3]]
    YB = [SB, TR]
    HB = TR[0]
    PC = 640
    gu_v = w_gu[0].rearrange("e (k p) f -> p (e k) f", p=P)
    dn_v = w_down[0].rearrange("e (i k p) d -> p (e i) k d", k=2, p=P)

    def quads(e, body):
        body(0, True, False)
        with e.Fori(1, QUADS - 1) as p:
            body(p, False, False)
        body(QUADS - 1, False, True)

    def experts_sp(sp):
        wait(sp, "w_lo", total)
        wait(sp, "pv", total)

        def body(p, first, last):
            for n in range(2 * CH):
                i, c = divmod(n, CH)
                slot = RING[:, n % RS, :]
                if not (first and n < RS):
                    sp.wait_ge(wlD, 2 * CH * p + n - RS + 1)
                    sp.wait_ge(wlP, 2 * CH * p + n - RS + 1)
                if c < 16:
                    row = (QE * p + 2 * i + c // 8) * 8 + c % 8
                    src = gu_v[:, bass.ds(row, 1), :].rearrange("p a f -> p (a f)")
                    sp.dma_start(slot, src).then_inc(ring_in[n % RS], 16)
                else:
                    row = (QE * p + 2 * i + (c - 16) // 4) * 4 + c % 4
                    src = dn_v[:, bass.ds(row, 1), :, :].rearrange("p a k d -> p (a k) d")
                    sp.dma_start(slot.rearrange("p (k d) -> p k d", k=2), src).then_inc(ring_in[n % RS], 16)
                if first and n == RS - 1:
                    wait(sp, "res", total)
                    sp.dma_start(WR[:, :, :], w_router[0].rearrange("(k p) e -> p k e", p=P)).then_inc(moe_in, 16)

        quads(sp, body)
        for t in range(TT):
            sp.wait_ge(s["nrm"], total["nrm"] + t + 1)
            sp.dma_start(out[0].rearrange("(t p) d -> t p d", p=P)[t], X[:, t, :]).then_inc(out_in, 16)
        sp.wait_ge(out_in, 16 * TT)

    def experts_pool(pool):
        def body(p, first, last):
            for n in range(2 * CH):
                i, c = divmod(n, CH)
                pool.wait_ge(wh, 2 * CH * p + n + 1)
                nc.gpsimd.tensor_tensor(WEL[n % 2][:, 2048 - PC:], RING[:, n % RS, 2048 - PC:],
                                        WEH[n % 2][:, 2048 - PC:].bitcast(F32), ALU.subtract).then_inc(wlP, 1)

        quads(pool, body)
        pool.wait_ge(gth, 4 * QUADS)
        for i in range(2):
            pool.dma_start(LN2R[:, i, :], rows[3 + i].partition_broadcast(P)).then_inc(rows2_in, 16)

    def experts_act(act, chain):
        A = nc.scalar.activation
        wait(act, "nrm", total)
        for t in range(TT):
            A(X2H[:, t, :], X[:, t, :], ACT.Copy).then_inc(s["x2h"], 1)
        wait(act, "pv", total)
        act.dma_start(IOTA[:, :], consts[:, C_IOTA:C_IOTA + S]).then_inc(moe_in, 16)
        act.wait_ge(s["lgs"], 1)
        A(LGT[:, :, :], LGT[:, :, :], ACT.Exp).then_inc(s["afp"], 1)
        act.wait_ge(s["icc"], 1)

        def outputs(x, e):
            for h in range(2):
                A(YHM[:, e, 512 * h:512 * h + 512], YB[e][h][:, :], ACT.Copy,
                  scale=GCOL[:, bass.ds(x, 1)]).then_inc(yh, 1)

        def body(p, first, last):
            for n in range(2 * CH):
                i, c = divmod(n, CH)
                C, x = 2 * CH * p + n, QE * p + 2 * i
                act.wait_ge(ring_in[n % RS], 16 * (2 * CH // RS * p + n // RS + 1))
                if not (first and n < 2):
                    act.wait_ge(used, C - 1)
                A(WEH[n % 2][:, :], RING[:, n % RS, :], ACT.Copy).then_inc(wh, 1)
                if c == 0 and not (first and i == 0):
                    act.wait_ge(used, C)
                    outputs(x - 1, 1)
                if n == 0:
                    for b in range(4):
                        act.wait_ge(gth, 4 * p + b + 1)
                        A(XS[:, 2 * b:2 * b + 2, :, 0, :],
                          XG[b][:, :].rearrange("p (k e c) -> p k e c", k=2, e=QE), ACT.Copy).then_inc(xsh, 1)
                if c in (8, 16):
                    act.wait_ge(used, C)
                    if not (first and n == 8):
                        act.wait_ge(ev, 4 * (x + c // 8 - 1))
                    for b in range(4):
                        A(LOH[:, 512 * b:512 * b + 512], GU[b][CAP:P, :], ACT.Copy).then_inc(ev_lo, 1)
                if c in (9, 17):
                    act.wait_ge(ev, 4 * (x + c // 8 - 1) + 2)
                    if not (first and n == 9):
                        act.wait_ge(tp, x + c // 8 - 1)
                    A(SG[:, :], GUS[:, 0:DFE], ACT.Silu).then_inc(su, 1)
                if c in (11, 19):
                    act.wait_ge(tp, x + c // 8)
                    A(HT[:, c // 8 - 1, :, 0, :], HB[:, :].rearrange("p (f c) -> p f c", c=CAP),
                      ACT.Copy).then_inc(hh, 1)
                if c == 20:
                    act.wait_ge(used, C)
                    outputs(x, 0)

        quads(act, body)
        act.wait_ge(used, 2 * CH * QUADS)
        outputs(E - 1, 1)
        layer_norm_act(act, {k: v + 1 for k, v in total.items()})

    def experts_dve(dve, chain):
        V, link = nc.vector, chain.link
        dve.wait_ge(s["lgp"], 1)
        lg = PV[:, 0:TT * E].rearrange("p (t e) -> p t e", e=E)
        link(V.tensor_reduce(ST[:, 0:4], lg, AX, ALU.max))
        V.tensor_tensor(LGT[:, :, :], lg, ST[:, 0:4].unsqueeze(2).to_broadcast([P, TT, E]),
                        ALU.subtract).then_inc(s["lgs"], 1)
        dve.wait_ge(s["afp"], 1)
        link(V.tensor_reduce(ST[:, 4:8], LGT[:, :, :], AX, ALU.add))
        link(V.reciprocal(ST[:, 8:12], ST[:, 4:8]))
        V.tensor_tensor(LGT[:, :, :], LGT[:, :, :], ST[:, 8:12].unsqueeze(2).to_broadcast([P, TT, E]),
                        ALU.mult).then_inc(s["af"], 1)
        dve.wait_ge(s["ixp"], 1)
        link(V.tensor_copy(AF[:, :], SB[0][0:E, :]))
        for i in range(CAP // 8):
            r = slice(8 * i, 8 * i + 8)
            link(V.max(VAL[:, r], AF[:, :]))
            V.max_index(IDU[:, r], VAL[:, r], AF[:, :])
            link(V.match_replace(AF[:, :], VAL[:, r], AF[:, :], -1.0))
        V.tensor_copy(VAL[:, CAP:2 * CAP], VAL[:, 0:CAP])
        V.tensor_copy(IDX[:, 0:CAP], IDU[:, :])
        V.tensor_copy(IDX[:, CAP:2 * CAP], IDU[:, :]).then_inc(s["top"], 1)
        dve.wait_ge(s["ixp"], 2)
        V.tensor_copy(GCOL[:, :], SB[1][:, 0:E])
        V.tensor_copy(ICOL[:, :], SB[1][:, E:2 * E])
        for h in range(2):
            ins = V.tensor_copy(IDB[:, 512 * h:512 * h + 512], LIN[h][:, :])
        ins.then_inc(s["icc"], 1)
        dve.wait_ge(s["icc"], 1)
        wait(dve, "xal", total)

        def outputs(x, e):
            for h in range(2):
                dve.wait_ge(yh, 2 * x + h + 1)
                c = slice(512 * h, 512 * h + 512)
                V.scalar_tensor_tensor(YLM[:, e, c], YB[e][h][:, :], GCOL[:, bass.ds(x, 1)],
                                       YHM[:, e, c].bitcast(F32), ALU.mult, ALU.subtract).then_inc(yl, 1)

        def one_hot_tokens(p):
            for t in range(TT):
                ins = V.tensor_scalar(OHT[:, t, :], IDB[:, bass.ds(p * QE * CAP, QE * CAP)],
                                      CST[:, C_TC + t:C_TC + t + 1], None, ALU.is_equal)
            ins.then_inc(oht, 1)

        def accumulate(g, k):
            dve.wait_ge(sct, 8 * g + k + 1)
            xs = X[:, k // 2, 512 * (k % 2):512 * (k % 2) + 512]
            V.tensor_tensor(xs, TR[k % 2][:, :], xs, ALU.add).then_inc(acc, 1)

        def body(p, first, last):
            for n in range(2 * CH):
                i, c = divmod(n, CH)
                x = QE * p + 2 * i
                dve.wait_ge(wh, 2 * CH * p + n + 1)
                V.tensor_tensor(WEL[n % 2][:, :2048 - PC], RING[:, n % RS, :2048 - PC],
                                WEH[n % 2][:, :2048 - PC].bitcast(F32), ALU.subtract).then_inc(wlD, 1)
                if c == 0 and not (first and i == 0):
                    outputs(x - 1, 1)
                if n == 0:
                    for b in range(4):
                        dve.wait_ge(xsh, 4 * p + b + 1)
                        V.tensor_tensor(XS[:, 2 * b:2 * b + 2, :, 1, :],
                                        XG[b][:, :].rearrange("p (k e c) -> p k e c", k=2, e=QE),
                                        XS[:, 2 * b:2 * b + 2, :, 0, :].bitcast(F32), ALU.subtract).then_inc(xsl, 1)
                if c in (8, 16):
                    for b in range(4):
                        dve.wait_ge(ev_lo, 4 * (x + c // 8 - 1) + b + 1)
                        V.tensor_tensor(GUS[:, 512 * b:512 * b + 512], GU[b][0:CAP, :],
                                        LOH[:, 512 * b:512 * b + 512], ALU.add).then_inc(ev, 1)
                if c in (9, 17):
                    dve.wait_ge(su, x + c // 8)
                    dve.wait_ge(ev, 4 * (x + c // 8))
                    V.tensor_tensor(SG[:, :], SG[:, :], GUS[:, DFE:], ALU.mult).then_inc(hm, 1)
                if c in (11, 19):
                    dve.wait_ge(hh, x + c // 8)
                    j = c // 8 - 1
                    V.tensor_tensor(HT[:, j, :, 1, :], HB[:, :].rearrange("p (f c) -> p f c", c=CAP),
                                    HT[:, j, :, 0, :].bitcast(F32), ALU.subtract).then_inc(hl, 1)
                if 2 <= c < 10 and not (first and i == 0):
                    accumulate(2 * p + i - 1, c - 2)
                if c == 20:
                    outputs(x, 0)
                if c == 12:
                    if not (first and i == 0):
                        dve.wait_ge(sct, 8 * (2 * p + i))
                    for e in range(2):
                        ins = V.tensor_scalar(SS[:, e, :], IOTA[:, :], ICOL[:, bass.ds(QE * p + 2 * i + e, 1)],
                                              None, ALU.is_equal)
                    ins.then_inc(ssr, 1)
                if n == 14 and not last:
                    dve.wait_ge(gth, 4 * p + 4)
                    one_hot_tokens(p + 1)

        dve.wait_ge(moe_in, 32)
        one_hot_tokens(0)
        quads(dve, body)
        outputs(E - 1, 1)
        for k in range(2 * TT):
            accumulate(E // 2 - 1, k)
        dve.wait_ge(acc, 8 * (E // 2))
        layer_norm_dve(dve, link, {k: v + 1 for k, v in total.items()}, LN2R, rows2_in, 32)

    def experts_pe(pe):
        T = nc.tensor
        pe.wait_ge(moe_in, 32)
        wait(pe, "tx_hi", total)
        for name in ("o", "evA", "evD", "p", "ptA", "ptD"):
            wait(pe, name, total)
        for t in range(TT):
            for k in range(KT):
                ins = T.matmul(PV[:, E * t:E * t + E], X2T[:, k, t * P:t * P + P], WR[:, k, :],
                               start=k == 0, stop=k == KT - 1)
        ins.then_inc(s["lgp"], 1)
        pe.wait_ge(s["af"], 1)
        for t in range(TT):
            ins = T.transpose(SB[0][0:E, t * P:t * P + P], LGT[:, t, :], ident)
        ins.then_inc(s["ixp"], 1)
        pe.wait_ge(s["top"], 1)
        T.transpose(SB[1][:, 0:E], VAL[:, :], ident[0:E, 0:E])
        T.transpose(SB[1][:, E:2 * E], IDX[:, :], ident[0:E, 0:E])
        for e in range(E):
            ins = T.matmul(LIN[e // 8][:, (e % 8) * CAP:(e % 8 + 1) * CAP],
                           ident[0:E, e:e + 1].to_broadcast([E, P]), IDX[:, 0:CAP], start=True, stop=True)
        ins.then_inc(s["ixp"], 1)
        pe.wait_ge(s["icc"], 1)
        pe.wait_ge(s["x2l"], TT)

        def gather(p):
            pe.wait_ge(oht, p + 1)
            for d in range(KT):
                o = XG[d // 2][:, d % 2 * 256:d % 2 * 256 + 256]
                for t in range(TT):
                    T.matmul(o, X2H[:, t, d * P:d * P + P], OHT[:, t, :], start=t == 0, stop=False)
                    ins = T.matmul(o, X2L[:, t, d * P:d * P + P], OHT[:, t, :], start=False, stop=t == TT - 1)
                if d % 2:
                    ins.then_inc(gth, 1)

        def scatter(g, k, experts):
            t, c = slice(k // 2 * P, k // 2 * P + P), slice(512 * (k % 2), 512 * (k % 2) + 512)
            if k == 0:
                pe.wait_ge(yh, 2 * experts)
                pe.wait_ge(yl, 2 * experts)
                pe.wait_ge(ssr, g + 1)
            if k >= 2:
                pe.wait_ge(acc, 8 * g + k - 1)
            for e in range(2):
                T.matmul(TR[k % 2][:, :], SS[:, e, t], YHM[:, e, c], start=e == 0, stop=False)
                ins = T.matmul(TR[k % 2][:, :], SS[:, e, t], YLM[:, e, c], start=False, stop=e == 1)
            ins.then_inc(sct, 1)

        def body(p, first, last):
            for n in range(2 * CH):
                i, c = divmod(n, CH)
                C, x, g = 2 * CH * p + n, QE * p + 2 * i, 2 * p + i
                H, L = WEH[n % 2], WEL[n % 2]
                if n == 0:
                    pe.wait_ge(xsh, 4 * p + 4)
                    pe.wait_ge(xsl, 4 * p + 4)
                pe.wait_ge(wh, C + 1)
                if c < 16:
                    e, k = divmod(c, 8)
                    xk = XS[:, k, 2 * i + e, :, :].rearrange("p a c -> p (a c)")
                    for b in range(4):
                        if k == 0 and not (first and n == 0):
                            pe.wait_ge(ev, 4 * (x + e - 1) + b + 1)
                        T.matmul(GU[b][:, :], xk, H[:, 512 * b:512 * b + 512], start=k == 0, stop=False)
                    pe.wait_ge(wlD, C + 1)
                    pe.wait_ge(wlP, C + 1)
                    for b in range(4):
                        ins = T.matmul(GU[b][:, :], xk, L[:, 512 * b:512 * b + 512], start=False, stop=k == 7)
                else:
                    e, r = divmod(c - 16, 4)
                    if r == 0:
                        pe.wait_ge(hl, x + e + 1)
                        if e == 0 and not (first and i == 0):
                            pe.wait_ge(yl, 2 * (x - 1))
                    for part in (H, L):
                        if part is L:
                            pe.wait_ge(wlD, C + 1)
                            pe.wait_ge(wlP, C + 1)
                        for k in range(2):
                            hk = HT[:, e, 2 * r + k, :, :].rearrange("p a c -> p (a c)")
                            for h in range(2):
                                ins = T.matmul(YB[e][h][:, :], hk, part[:, D * k + 512 * h:D * k + 512 * h + 512],
                                               start=r + k == 0 and part is H, stop=r == 3 and k == 1 and part is L)
                ins.then_inc(used, 1)
                if c < 8 and not (first and i == 0):
                    scatter(g - 1, c, x)
                if c in (10, 18):
                    e = c // 8 - 1
                    pe.wait_ge(hm, x + e + 1)
                    if e:
                        pe.wait_ge(hl, x + 1)
                    elif not (first and i == 0):
                        pe.wait_ge(acc, 8 * g)
                    for f in range(KT):
                        ins = T.matmul(HB[:, CAP * f:CAP * f + CAP], SG[:, f * P:f * P + P], ident[0:CAP, 0:CAP],
                                       start=True, stop=True)
                    ins.then_inc(tp, 1)
            if not last:
                pe.wait_ge(yl, 2 * (QE * p + 3))
                pe.wait_ge(ev, 4 * (QE * p + 4))
                gather(p + 1)

        gather(0)
        quads(pe, body)
        for k in range(2 * TT):
            scatter(E // 2 - 1, k, E)

    block = ctx.enter_context(nc.Block())
    xv = x[0].rearrange("(t p) d -> t p d", p=P)

    @block.sync
    def _(sp):
        sp.dma_start(MEMT[:, :, :], mem[0].rearrange("(t p) d -> p t d", p=P)).then_inc(mem_in, 16)
        for st in plan:
            if st.kind == "unit":
                u, K = st.u, st.K
                if u >= 2:
                    sp.wait_ge(s["w_lo"], u - 1)
                dst = RAW[:, u % 2, :K * UC].rearrange("p (k c) -> p k c", c=UC)
                if st.evac == "ffn":
                    for g in range(2):
                        src = st.w[:, g * DFF + st.c0:g * DFF + st.c0 + P].rearrange("(k p) c -> p k c", p=P)
                        sp.dma_start(dst[:, :, g * P:g * P + P], src).then_inc(raw_in[u % 2], 16)
                else:
                    src = st.w[st.row0:st.row0 + K * P, st.c0:st.c0 + UC].rearrange("(k p) c -> p k c", p=P)
                    for h in range(2):
                        kk = slice(h * K // 2, (h + 1) * K // 2)
                        sp.dma_start(dst[:, kk, :], src[:, kk, :]).then_inc(raw_in[u % 2], 16)
                if u == 1:
                    for t in range(TT):
                        sp.dma_start(X[:, t, :], xv[t]).then_inc(x_in, 16)
            elif st is router:
                experts_sp(sp)
        if stop:
            wait(sp, "nrm", last_step.end)
            sp.dma_start(out[0].rearrange("(t p) d -> p t d", p=P), X[:, :, :]).then_inc(out_in, 16)
            sp.wait_ge(out_in, 16)

    @block.gpsimd
    def _(pool):
        for q in range(16):
            pool.dma_start(win_rpb[q], bass.AP(rpb.tensor, rpb.offset + 15 - q, [[31, 120], [1, 48]])).then_inc(win_in, 16)
        pool.memset(BD[:, :, :, :], 0.0).then_inc(bd0, 1)
        pool.wait_ge(bd0, 1)
        for w, wd in enumerate((w_rg, w_ig)):
            for q in range(2):
                pool.dma_start(BD[q * 64:q * 64 + 64, w, :, q * 64:q * 64 + 64],
                               wd[0].rearrange("(c q) i o -> q i c o", q=2)[q]).then_inc(bd_in, 16)
        for st in plan:
            if st is fin:
                wait(pool, "evD", st.at)
                pool.dma_start(GFIN[:, :], rows[0].partition_broadcast(P)).then_inc(rows_in, 16)
            elif st.kind == "save":
                wait(pool, "nrm", st.at)
                pool.dma_start(xd, X[:, :, :]).then_inc(s["saved"], 16)
            elif st.kind == "rope" and st.half == 0:
                wait(pool, "mx", st.at)
                pool.dma_start(X[:, :, :], xd).then_inc(xre_in, 16)
            elif st is ln1:
                wait(pool, "ms_lo", st.at)
                for i in range(2):
                    pool.dma_start(LNR[:, i, :], rows[1 + i].partition_broadcast(P)).then_inc(rows_in, 16)
            elif st is router:
                for t in range(TT):
                    pool.wait_ge(s["x2h"], t + 1)
                    nc.gpsimd.tensor_tensor(X2L[:, t, :], X[:, t, :], X2H[:, t, :].bitcast(F32),
                                            ALU.subtract).then_inc(s["x2l"], 1)
                wait(pool, "tx_hi", st.at)
                pool.wait_ge(s["x2l"], TT)
                for t in range(TT):
                    nc.gpsimd.tensor_scalar(X[:, t, :], X[:, t, :], ALPHA, 1.0, ALU.mult,
                                            ALU.mult).then_inc(s["xal"], 1)
                experts_pool(pool)
            elif st is txx:
                wait(pool, "saved", st.at)
                wait(pool, "tx_lo", st.end)
                pool.wait_ge(win_in, 16 * 16)
                for r in range(8):
                    src = bass.AP(win_rpb.tensor, (7 - r) * 48, [[120 * 48, 16], [15 * 48, 8], [1, 8 * 48]])
                    pool.dma_start(B48[r::8, :, :, :].rearrange("p h r j -> p h (r j)"), src).then_inc(b48_in, 16)
            elif st is band:
                wait(pool, "evA", st.at)
                wait(pool, "evD", st.at)
                for cb, bs in enumerate((0, 8, 24, 32)):
                    for b in range(2):
                        for a in range(2):
                            pool.dma_start(VB[(2 * b + a) * 32:(2 * b + a) * 32 + 32, cb, :, :],
                                           VN[a * 64 + bs:a * 64 + bs + 32, b::2, :]).then_inc(s["band"], 16)

    @block.scalar
    def _(act):
        chain = Chain(act, "act_chain")
        link = chain.link
        A = nc.scalar.activation
        act.dma_start(CST[:, :], consts[:, 0:C_N1]).then_inc(consts_in, 16)
        act.dma_start(VEC[:, :], vecs).then_inc(consts_in, 16)
        act.wait_ge(consts_in, 32)
        eps6, eps5, one = CST[:, C_EPS6:C_EPS6 + 1], CST[:, C_EPS5:C_EPS5 + 1], CST[:, C_ONE:C_ONE + 1]

        def split_hi(u):
            if u >= len(units):
                return
            n = units[u].K * UC
            act.wait_ge(raw_in[u % 2], 32 * (u // 2 + 1))
            if u >= 2:
                act.wait_ge(s["res"], units[u - 1].r0)
            A(WH[:, u % 2, :n], RAW[:, u % 2, :n], ACT.Copy).then_inc(s["w_hi"], 1)

        def evacuate(st):
            for r, who in enumerate(st.who):
                n = st.r0 + r
                bank = LIN[lin_of[n]]
                if st.evac == "ffn" and r == 1:
                    act.wait_ge(s["evD"], res_shares[n][1])
                    f = st.kw["f"]
                    A(AH[:, f, :], FP[:, f % 2, :], ACT.Copy).then_inc(s["act_hi"], 1)
                if who != "act":
                    continue
                act.wait_ge(s["res"], n + 1)
                if st.evac == "ffn":
                    ins = A(FG[:, st.kw["f"] % 2, :], bank[:, :], ACT.Silu)
                elif st.evac == "gate":
                    wait(act, "evD", st.at)
                    ins = A(GT[:, r, :], bank[:, :], ACT.Sigmoid,
                            bias=vec(V_BG + 8 * st.kw["g"] + 2 * st.kw["j"] + r))
                elif st.evac == "naq":
                    ins = A(st.dst(r).rearrange("p (b c r) -> p r b c", b=4, c=16),
                            bank[:, :].rearrange("p (r b c) -> p r b c", r=8, b=4), ACT.Copy, scale=0.125)
                elif st.evac == "scaled":
                    ins = A(st.dst(r), bank[:, :], ACT.Copy, scale=st.kw["scale"])
                else:
                    ins = A(st.dst(r), shaped(st, bank), ACT.Copy)
                ins.then_inc(s["evA"], 1)

        def pre_scores(a):
            n, v = a.n, [0, 0]
            for i in range(3):
                for j in range(2):
                    nk = a.nkt[j] * P
                    e = SE[:, n % 2, j, :nk]
                    if i == 0:
                        if n >= 2:
                            act.wait_ge(s["p"], 2 * n + j - 3)
                        act.wait_ge(s["qk"], 2 * n + j + 1)
                        v[j] = chain.sign(A(e, score_bank(a, j)[:, :nk], ACT.Abs))
                    else:
                        chain.need(v[j])
                        if i == 1:
                            v[j] = chain.sign(A(e, e, ACT.Exp, scale=-1.0))
                        else:
                            A(e, e, ACT.Ln, bias=one).then_inc(s["e_ab"], 1)

        def exponentials(a):
            n = a.n
            if n >= 2:
                act.wait_ge(s["tr"], n - 1)
                if a.att != "stick":
                    act.wait_ge(s["o"], n - 1)
            for j in range(2):
                nk = a.nkt[j] * P
                if a.att == "stick":
                    act.wait_ge(s["st_d"], 2 * n + j + 1)
                    A(PB[:, n % 2, j, :nk], SE[:, n % 2, j, :nk], ACT.Exp).then_inc(s["p"], 1)
                else:
                    act.wait_ge(s["mx"], a.at.get("mx", 0) + j + 1)
                    c = 2 * (n % 2) + j
                    src = SN[:, n % 2, j, :] if a.att == "na" else score_bank(a, j)[:, :nk]
                    A(PB[:, n % 2, j, :nk], src, ACT.Exp, bias=ST[:, 16 + c:17 + c],
                      accum_out=ST[:, 20 + c:21 + c]).then_inc(s["p"], 1)

        split_hi(0)
        for st in plan:
            k = st.kind
            if k == "unit":
                split_hi(st.u + 1)
                evacuate(st)
            elif k == "tx":
                for f in range(st.nf):
                    act.wait_ge(s["tx_ps"], st.n0 + f + 1)
                    src, dst = TR[(st.n0 + f) % 2][:, :st.T * P], st.dh[:, f, :]
                    if st.perm:
                        src = src.rearrange("p (b c r) -> p b c r", b=4, c=16)
                        dst = dst.rearrange("p (r b c) -> p b c r", r=8, b=4)
                    scale = st.const if st.scale is None else vec(st.scale + f)
                    A(dst, src, ACT.Copy, scale=scale).then_inc(s["tx_hi"], 1)
            elif k == "rms":
                if "ready" in st.kw:
                    act.wait_ge(*st.kw["ready"])
                    wait(act, "tx_ps", st.kw["war"].end)
                else:
                    wait(act, "evD", st.at)
                    wait(act, "o", st.at)
                for t in range(TT):
                    dump = PB[:, t // 2, t % 2, :] if st.dst is YT else XN[:, t, :]
                    ins = A(dump, st.src[:, t, :], ACT.Square, accum_out=ST[:, t:t + 1])
                link(ins)
                A(ST[:, 4:8], ST[:, 0:4], ACT.Sqrt, scale=1.0 / st.d, bias=eps6).then_inc(s["sd"], 1)
            elif k == "ln":
                layer_norm_act(act, st.end)
            elif k == "lgate":
                for c in range(4):
                    for w, dst in enumerate((LR, LI)):
                        act.wait_ge(s["gmm"], 2 * c + w + 1)
                        A(dst[:, c, :], (SB, TR)[c % 2][w][:, :], ACT.Sigmoid,
                          bias=vec((V_BRG, V_BIG)[w] + c)).then_inc(s["sig"], 1)
            elif k == "lrec":
                link(A(ST[:, 32:36], vec(V_LAM, 4), ACT.Abs))
                link(A(ST[:, 32:36], ST[:, 32:36], ACT.Exp, scale=-1.0))
                link(A(ST[:, 36:40], vec(V_LAM, 4), ACT.Relu, scale=-1.0))
                A(ST[:, 32:36], ST[:, 32:36], ACT.Ln, bias=one).then_inc(s["lexp"], 1)
                act.wait_ge(s["lgl"], 1)
                act.wait_ge(s["sig"], 8)
                act.wait_ge(s["conv"], 1)
                for c in range(4):
                    A(LTH[:, c, :], LR[:, c, :], ACT.Tanh, scale=ST[:, 40 + c:41 + c])
                for c in range(4):
                    ins = A(LR[:, c, :], LR[:, c, :], ACT.Exp, scale=ST[:, 44 + c:45 + c])
                ins.then_inc(s["lt"], 1)
                A(LG[:, :, :], LG[:, :, :], ACT.Gelu_apprx_tanh).then_inc(s["lsq"], 1)
                act.wait_ge(s["lm2"], 1)
                A(LTH[:, :, :], LTH[:, :, :], ACT.Sqrt).then_inc(s["lsq"], 1)
            elif k == "lout":
                act.wait_ge(s["lrec"], 1)
                A(TMP[:, :, :], YL_[:, :, :], ACT.Square).then_inc(s["ysq"], 1)
                act.wait_ge(s["ysum"], 1)
                A(RBC[:, :], SB[0][:, :], ACT.Sqrt, scale=1.0 / 512, bias=eps6).then_inc(s["ysd"], 1)
                act.wait_ge(s["yn"], 1)
                wait(act, "res", st.at)
                for c in range(4):
                    A(XH[:, c, :], YL_[:, c, :], ACT.Copy, scale=vec(V_GLRU + c)).then_inc(s["yhi"], 1)
            elif k == "rope":
                act.wait_ge(s["rms_q"], st.half + 1)
                A(ST[:, 114:124], ST[:, 104:114], ACT.Sqrt, bias=eps6).then_inc(s["rsd_q"], 1)
            elif k == "logexp":
                act.preload_act_table_set("natural_log_exp_and_others")
            elif k == "S" and st.att == "stick":
                pre_scores(st)
            elif k == "X":
                exponentials(st.a)
            elif k == "C":
                act.wait_ge(s["tr"], st.a.n + 1)
                if st.a.n:
                    act.wait_ge(s["pv"], st.a.n)
                for o, i in pieces(st.a, 0):
                    ins = A(o, i, ACT.Copy)
                ins.then_inc(s["ptA"], 1)
            elif k == "msplit":
                wait(act, "evD", st.at)
                wait(act, "res", st.at)
                for f in range(KT):
                    A(XH[:, f, :], MG[:, f, :], ACT.Copy).then_inc(s["ms_hi"], 1)
        if not stop:
            experts_act(act, chain)

    @block.vector
    def _(dve):
        chain = Chain(dve, "dve_chain")
        link = chain.link
        V = nc.vector
        dve.wait_ge(consts_in, 32)

        def split_lo(u):
            if u >= len(units):
                return
            n = units[u].K * UC
            dve.wait_ge(s["w_hi"], u + 1)
            V.tensor_tensor(WL[:, u % 2, :n], RAW[:, u % 2, :n], WH[:, u % 2, :n].bitcast(F32),
                            ALU.subtract).then_inc(s["w_lo"], 1)

        def evacuate(st):
            for r, who in enumerate(st.who):
                if who != "dve":
                    continue
                n = st.r0 + r
                bank = LIN[lin_of[n]]
                dve.wait_ge(s["res"], n + 1)
                if st.evac in ("accX", "mixX"):
                    xs = X[:, 2 * r:2 * r + 2, st.c0:st.c0 + UC]
                if st.evac == "ffn":
                    f = st.kw["f"]
                    dve.wait_ge(s["evA"], res_shares[n][0])
                    V.tensor_tensor(FP[:, f % 2, :], bank[:, :], FG[:, f % 2, :], ALU.mult).then_inc(s["evD"], 1)
                    dve.wait_ge(s["evD"], res_shares[n][1])
                    dve.wait_ge(s["act_hi"], st.end["act_hi"])
                    V.tensor_tensor(AL[:, f, :], FP[:, f % 2, :], AH[:, f, :].bitcast(F32),
                                    ALU.subtract).then_inc(s["act_lo"], 1)
                elif st.evac == "accX":
                    V.tensor_tensor(xs, shaped(st, bank), xs, ALU.add).then_inc(s["evD"], 1)
                elif st.evac == "mixX":
                    dve.wait_ge(xre_in, 16)
                    V.scalar_tensor_tensor(xs, xs, ALPHA, shaped(st, bank), ALU.mult, ALU.add).then_inc(s["evD"], 1)
                elif st.evac == "branch":
                    dve.wait_ge(s["evA"], st.at["evA"])
                    m, g = MG[:, 2 * st.kw["j"] + r, :], GT[:, r, :]
                    if st.kw["g"] == 0:
                        V.tensor_tensor(m, bank[:, :], g, ALU.mult).then_inc(s["evD"], 1)
                    else:
                        link(V.tensor_tensor(g, bank[:, :], g, ALU.mult))
                        V.tensor_tensor(m, m, g, ALU.add).then_inc(s["evD"], 1)
                else:
                    V.tensor_copy(st.dst(r), shaped(st, bank)).then_inc(s["evD"], 1)

        def weights(a):
            n, v = a.n, [0, 0]
            for i in range(5):
                for j in range(2):
                    nk = a.nkt[j] * P
                    bank, e, d = score_bank(a, j)[:, :nk], SE[:, n % 2, j, :nk], slice(nk - P, nk)
                    ed, sp = SE[:, n % 2, j, d], SP_[:, j, :nk]
                    if i:
                        chain.need(v[j])
                    if i == 0:
                        dve.wait_ge(s["e_ab"], 2 * n + j + 1)
                        ins = V.scalar_tensor_tensor(sp, bank, 0.0, e, ALU.max, ALU.add)
                    elif i == 1:
                        ins = V.tensor_tensor(SP_[:, j, d], SP_[:, j, d], CST[:, C_LT:C_LT + P], ALU.mult)
                    elif i == 2:
                        ins = V.tensor_tensor_scan(SC[:, j, nk - 1::-1], ones[:, 0:1].to_broadcast([P, nk]),
                                                   SP_[:, j, nk - 1::-1], 0.0, ALU.mult, ALU.add)
                    elif i == 3:
                        ins = V.tensor_tensor(e, bank, SC[:, j, :nk], ALU.subtract)
                    else:
                        V.tensor_tensor(ed, ed, CST[:, C_NEG:C_NEG + P], ALU.add).then_inc(s["st_d"], 1)
                        continue
                    v[j] = chain.sign(ins)

        def maxima(a):
            n = a.n
            for j in range(2):
                nk = a.nkt[j] * P
                bank = score_bank(a, j)[:, :nk]
                c = 2 * (n % 2) + j
                dve.wait_ge(s["qk"], 2 * n + j + 1)
                if n >= 2:
                    dve.wait_ge(s["p"], 2 * n + j - 3)
                if a.att == "na":
                    cb = a.qt[j]
                    o = (16, 8, 8, 0)[cb]
                    mask = CST[:, C_NAM + 32 * min(cb, 1) + 32 * (cb == 3):][:, :32].unsqueeze(1).to_broadcast([P, 8, 32])
                    sn = SN[:, n % 2, j, :].rearrange("p (r w) -> p r w", r=8)
                    dve.wait_ge(b48_in, 16 * 8)
                    link(V.tensor_tensor(sn, bank.rearrange("p (r w) -> p r w", r=8),
                                         B48[:, a.h, :, o:o + 32], ALU.add))
                    link(V.tensor_tensor(sn, sn, mask, ALU.add))
                    bank = SN[:, n % 2, j, :]
                link(V.tensor_reduce(ST[:, 28 + c:29 + c], bank, AX, ALU.max))
                V.tensor_scalar(ST[:, 16 + c:17 + c], ST[:, 28 + c:29 + c], -1.0, None,
                                ALU.mult).then_inc(s["mx"], 1)

        def output(a):
            n = a.n
            dv = P if a.att == "mem" else 64
            y = YT if a.att == "stick" else YN
            if a.att == "stick":
                dve.wait_ge(s["pv"], n + 1)
                V.tensor_copy(y[:, a.qt[0]:a.qt[0] + 2, 64 * a.h:64 * a.h + 64],
                              PV[:, 0:2 * P].rearrange("p (j c) -> p j c", j=2)[:, :, :64]).then_inc(s["o"], 1)
                return
            c = 2 * (n % 2)
            dve.wait_ge(s["p"], 2 * n + 2)
            dve.wait_ge(s["o"], n)
            link(V.reciprocal(ST[:, 24:26], ST[:, 20 + c:22 + c]))
            dve.wait_ge(s["pv"], n + 1)
            for j in range(2):
                ins = V.tensor_scalar(y[:, a.qt[j], dv * a.h:dv * a.h + dv], PV[:, P * j:P * j + dv],
                                      ST[:, 24 + j:25 + j], None, ALU.mult)
            ins.then_inc(s["o"], 1)

        def rope(st):
            H = 10
            xn = RT[:, 0, :].rearrange("p (h c) -> p h c", h=H)
            t12 = RT[:, 1, :].rearrange("p (i h c) -> p i h c", i=2, h=H)
            t34 = RT[:, 2, :].rearrange("p (i h c) -> p i h c", i=2, h=H)
            wait(dve, "evA", st.at)
            for t in (st.half,):
                q = GQT[:, t, :].rearrange("p (h c) -> p h c", h=8)
                kk = KVT[:, t, 0:128].rearrange("p (h c) -> p h c", h=2)
                link(V.tensor_tensor(xn[:, 0:8, :], q, q, ALU.mult))
                link(V.tensor_tensor(xn[:, 8:10, :], kk, kk, ALU.mult))
                link(V.tensor_reduce(ST[:, 104:114], xn, AX, ALU.add))
                V.tensor_scalar(ST[:, 104:114], ST[:, 104:114], 1.0 / 64, None, ALU.mult).then_inc(s["rms_q"], 1)
                dve.wait_ge(s["rsd_q"], t + 1)
                link(V.reciprocal(ST[:, 104:114], ST[:, 114:124]))
                r = ST[:, 104:114].unsqueeze(2)
                link(V.tensor_tensor(xn[:, 0:8, :], q, r[:, 0:8].to_broadcast([P, 8, 64]), ALU.mult))
                link(V.tensor_tensor(xn[:, 8:10, :], kk, r[:, 8:10].to_broadcast([P, 2, 64]), ALU.mult))
                link(V.tensor_tensor(xn[:, 0:8, :], xn[:, 0:8, :],
                                     vec(V_GQ, 64).unsqueeze(1).to_broadcast([P, 8, 64]), ALU.mult))
                link(V.tensor_tensor(xn[:, 8:10, :], xn[:, 8:10, :],
                                     vec(V_GQ + 64, 64).unsqueeze(1).to_broadcast([P, 2, 64]), ALU.mult))
                cs = CST[:, C_COS + 32 * t:C_COS + 32 * t + 32].unsqueeze(1).to_broadcast([P, H, 32])
                sn = CST[:, C_SIN + 32 * t:C_SIN + 32 * t + 32].unsqueeze(1).to_broadcast([P, H, 32])
                x1, x2 = xn[:, :, 0::2], xn[:, :, 1::2]
                V.tensor_tensor(t12[:, 0], x1, cs, ALU.mult)
                V.tensor_tensor(t12[:, 1], x2, sn, ALU.mult)
                V.tensor_tensor(t34[:, 0], x1, sn, ALU.mult)
                link(V.tensor_tensor(t34[:, 1], x2, cs, ALU.mult))
                for i, (ta, op) in enumerate(((t12, ALU.subtract), (t34, ALU.add))):
                    V.tensor_tensor(q[:, :, i::2], ta[:, 0, 0:8], ta[:, 1, 0:8], op)
                    for dup in range(2):
                        kd = KD[:, t, :].rearrange("p (g u c) -> p g u c", g=2, u=2)[:, :, dup, i::2]
                        ins = V.tensor_tensor(kd, ta[:, 0, 8:10], ta[:, 1, 8:10], op)
                ins.then_inc(s["rope"], 1)

        split_lo(0)
        for st in plan:
            k = st.kind
            if k == "unit":
                split_lo(st.u + 1)
                evacuate(st)
            elif k == "tx" and not st.f32:
                for f in range(st.nf):
                    dve.wait_ge(s["tx_hi"], tx_free[st.n0 + f][0])
                    src, hi, lo = TR[(st.n0 + f) % 2][:, :st.T * P], st.dh[:, f, :].bitcast(F32), st.dl[:, f, :]
                    if st.perm:
                        src = src.rearrange("p (b c r) -> p b c r", b=4, c=16)
                        hi, lo = (v.rearrange("p (r b c) -> p b c r", r=8, b=4) for v in (hi, lo))
                    if st.scale is None:
                        ins = V.tensor_tensor(lo, src, hi, ALU.subtract)
                    else:
                        ins = V.scalar_tensor_tensor(lo, src, vec(st.scale + f), hi, ALU.mult, ALU.subtract)
                    ins.then_inc(s["tx_lo"], 1)
            elif k == "rms":
                wait(dve, "sd", st.end)
                V.reciprocal(ST[:, 8:12], ST[:, 4:8]).then_inc(s["rc"], 1)
                wait(dve, "rc", st.end)
                if st.grow is not None:
                    dve.wait_ge(rows_in, 16)
                for t in range(TT):
                    r = ST[:, 8 + t:9 + t]
                    if st.grow is None:
                        ins = V.tensor_scalar(st.dst[:, t, :], st.src[:, t, :], r, None, ALU.mult)
                    else:
                        ins = V.scalar_tensor_tensor(st.dst[:, t, :], st.src[:, t, :], r, st.grow[:, :],
                                                     ALU.mult, ALU.mult)
                    ins.then_inc(s["nrm"], 1)
            elif k == "ln":
                wait(dve, "evD", st.at)
                layer_norm_dve(dve, link, st.end, st.rows, rows_in, 48)
            elif k == "conv":
                wait(dve, "evA", st.after.end)
                wait(dve, "evD", st.after.end)
                link(V.memset(LX[:, :, 0:3], 0.0))
                for c in range(4):
                    link(V.tensor_scalar(LC[:, c, :], LX[:, c, 0:S], vec(V_CW + 4 * c), vec(V_CB + c),
                                         ALU.mult, ALU.add))
                    for i in range(1, 4):
                        ins = V.scalar_tensor_tensor(LC[:, c, :], LX[:, c, i:i + S], vec(V_CW + 4 * c + i),
                                                     LC[:, c, :], ALU.mult, ALU.add)
                        if (c, i) != (3, 3):
                            link(ins)
                ins.then_inc(s["conv"], 1)
            elif k == "lrec":
                dve.wait_ge(s["lexp"], 1)
                link(V.tensor_tensor(ST[:, 32:36], ST[:, 32:36], ST[:, 36:40], ALU.add))
                V.tensor_scalar(ST[:, 40:44], ST[:, 32:36], 8.0, None, ALU.mult)
                V.tensor_scalar(ST[:, 44:48], ST[:, 32:36], -8.0, None, ALU.mult).then_inc(s["lgl"], 1)
                dve.wait_ge(s["lt"], 1)
                link(V.tensor_tensor(TMP[:, :, :], LR[:, :, :], LR[:, :, :], ALU.mult))
                V.scalar_tensor_tensor(LTH[:, :, :], TMP[:, :, :], 1.0, LTH[:, :, :],
                                       ALU.add, ALU.mult).then_inc(s["lm2"], 1)
                link(V.tensor_tensor(LI[:, :, :], LI[:, :, :], LC[:, :, :], ALU.mult))
                dve.wait_ge(s["lsq"], 2)
                link(V.tensor_tensor(LI[:, :, :], LI[:, :, :], LTH[:, :, :], ALU.mult))
                for c in range(4):
                    ins = V.tensor_tensor_scan(TMP[:, c, :], LR[:, c, :], LI[:, c, :], 0.0, ALU.mult, ALU.add)
                link(ins)
                V.tensor_tensor(YL_[:, :, :], TMP[:, :, :], LG[:, :, :], ALU.mult).then_inc(s["lrec"], 1)
            elif k == "lout":
                dve.wait_ge(s["ysd"], 1)
                link(V.reciprocal(RBC[:, :], RBC[:, :]))
                V.tensor_tensor(YL_[:, :, :], YL_[:, :, :], RBC[:, :].unsqueeze(1).to_broadcast([P, 4, S]),
                                ALU.mult).then_inc(s["yn"], 1)
                dve.wait_ge(s["yn"], 1)
                for c in range(4):
                    dve.wait_ge(s["yhi"], c + 1)
                    V.scalar_tensor_tensor(XL[:, c, :], YL_[:, c, :], vec(V_GLRU + c), XH[:, c, :].bitcast(F32),
                                           ALU.mult, ALU.subtract).then_inc(s["ylo"], 1)
            elif k == "S" and st.att == "stick":
                weights(st)
            elif k == "S":
                maxima(st)
            elif k == "C" and st.counts["ptD"]:
                dve.wait_ge(s["tr"], st.a.n + 1)
                if st.a.n:
                    dve.wait_ge(s["pv"], st.a.n)
                for o, i in pieces(st.a, 1):
                    ins = V.tensor_copy(o, i)
                ins.then_inc(s["ptD"], 1)
            elif k == "O":
                output(st.a)
            elif k == "rope":
                rope(st)
            elif k == "msplit":
                for f in range(KT):
                    wait(dve, "ms_hi", st.at, -f - 1)
                    V.tensor_tensor(XL[:, f, :], MG[:, f, :], XH[:, f, :].bitcast(F32),
                                    ALU.subtract).then_inc(s["ms_lo"], 1)
        if not stop:
            experts_dve(dve, chain)

    @block.tensor
    def _(pe):
        T = nc.tensor
        pe.wait_ge(consts_in, 32)

        def product(st):
            XHs, XLs = SRC[st.src]
            wh, wl = (w[:, st.u % 2, :st.K * UC].rearrange("p (k c) -> p k c", c=UC) for w in (WH, WL))
            pe.wait_ge(s["w_lo"], st.u + 1)
            if st.src == "a":
                wait(pe, "act_lo", st.at)
            wait(pe, "tx_lo", st.at)
            wait(pe, "ylo", st.at)
            wait(pe, "ms_lo", st.at)
            for r in range(len(st.who)):
                n = st.r0 + r
                bank = LIN[lin_of[n]]
                bank_free(pe, st, n)
                if st.mode == "F":
                    c = slice(P * r, P * r + P)
                    for k in range(st.K):
                        hi, lo = XHs[:, k, :st.nt], XLs[:, k, :st.nt]
                        T.matmul(bank[:, :st.nt], wh[:, k, c], hi, start=k == 0, stop=False)
                        T.matmul(bank[:, :st.nt], wh[:, k, c], lo, start=False, stop=False)
                        ins = T.matmul(bank[:, :st.nt], wl[:, k, c], hi, start=False, stop=k == st.K - 1)
                else:
                    for i in range(2):
                        t = slice((2 * r + i) * P, (2 * r + i + 1) * P)
                        o = bank[:, i * UC:i * UC + UC]
                        for k in range(st.K):
                            T.matmul(o, XHs[:, k, t], wh[:, k, :], start=k == 0, stop=False)
                            T.matmul(o, XHs[:, k, t], wl[:, k, :], start=False, stop=False)
                            ins = T.matmul(o, XLs[:, k, t], wh[:, k, :], start=False, stop=k == st.K - 1)
                ins.then_inc(s["res"], 1)

        def banks_idle(st):
            for name in ("ptA", "ptD", "tx_hi", "tx_lo", "sig", "ysd"):
                wait(pe, name, st.at)

        def qk(a, j):
            b = (a.h % 2) * 64
            h2 = a.h // 2
            qc = slice(a.qt[j] * P, a.qt[j] * P + P)
            if a.att == "stick":
                return QT[b:b + 64, h2, qc], KTT[b:b + 64, h2, 0:a.nkt[j] * P]
            if a.att == "na":
                bs = (0, 8, 24, 32)[a.qt[j]]
                return QT[b:b + 64, h2, qc], KTT[b:b + 64, h2, :].rearrange("p (r c) -> p r c", r=8)[:, :, bs:bs + 32]
            if a.att == "gqa":
                return QG[b:b + 64, h2, qc], KG[b:b + 64, a.h // 4, :]
            return QM[:, a.h, qc], MKT[:, a.h, :]

        later = []

        def scores(a, j):
            q, kk = qk(a, j)
            o = score_bank(a, j)[:, 0:a.nkt[j] * P]
            if a.att == "na":
                o = o.rearrange("p (r c) -> p r c", r=8)
            score_bank_free(pe, a, j)
            T.matmul(o, q, kk, start=True, stop=True).then_inc(s["qk"], 1)

        def flush():
            while later:
                scores(later.pop(), 1)

        def values(a, j, kt):
            if a.att == "stick":
                return VT[:, kt, 64 * a.h:64 * a.h + 64]
            if a.att == "na":
                return VB[:, a.qt[j], kt, 64 * a.h:64 * a.h + 64]
            if a.att == "gqa":
                return KVT[:, kt, 128 + 64 * (a.h // 4):192 + 64 * (a.h // 4)]
            return MV[:, kt, P * a.h:P * a.h + P]

        for st in plan:
            k = st.kind
            if k == "unit":
                flush()
                product(st)
            elif k == "tx":
                if "ready" in st.kw:
                    pe.wait_ge(*st.kw["ready"])
                for name in ("nrm", "o", "rope"):
                    wait(pe, name, st.at)
                banks_idle(st)
                for f in range(st.nf):
                    n = st.n0 + f
                    if f >= 2:
                        hi, lo = tx_free[n - 2]
                        pe.wait_ge(s["tx_hi"], hi)
                        if lo:
                            pe.wait_ge(s["tx_lo"], lo)
                    for t in range(st.T):
                        ins = T.transpose(TR[n % 2][:, t * P:t * P + P], st.src[:, t, f * P:f * P + P], ident)
                    ins.then_inc(s["tx_ps"], 1)
            elif k == "lgate":
                pe.wait_ge(bd_in, 64)
                pe.wait_ge(s["conv"], 1)
                banks_idle(st)
                for c in range(4):
                    for w in range(2):
                        if c >= 2:
                            pe.wait_ge(s["sig"], 2 * (c - 2) + w + 1)
                        T.matmul((SB, TR)[c % 2][w][:, :], BD[:, w, c, :], LC[:, c, :],
                                 start=True, stop=True).then_inc(s["gmm"], 1)
            elif k == "lout":
                pe.wait_ge(s["ysq"], 1)
                banks_idle(st)
                for c in range(4):
                    ins = T.matmul(SB[0][:, :], ones, TMP[:, c, :], start=c == 0, stop=c == 3)
                ins.then_inc(s["ysum"], 1)
            elif k == "S":
                wait(pe, "evA", st.after.end)
                wait(pe, "evD", st.after.end)
                wait(pe, "band", st.after.end)
                wait(pe, "tx_hi", st.after.end)
                wait(pe, "sig", st.at)
                wait(pe, "ysd", st.at)
                later.append(st)
                scores(st, 0)
                if st.att in ("stick", "na"):
                    flush()
            elif k == "T":
                flush()
                wait(pe, "p", st.at)
                banks_idle(st)
                for j in range(2):
                    for kt in range(st.a.nkt[j]):
                        c = (kt % 2) * 256 + j * P
                        ins = T.transpose(TR[kt // 2][:, c:c + P], PB[:, st.a.n % 2, j, kt * P:kt * P + P], ident)
                ins.then_inc(s["tr"], 1)
            elif k == "O":
                a = st.a
                wait(pe, "ptA", a.c.end)
                wait(pe, "ptD", a.c.end)
                wait(pe, "o", st.at)
                dv = P if a.att == "mem" else 64
                for j in range(2):
                    for kt in range(a.nkt[j]):
                        ins = T.matmul(PV[:, j * P:j * P + dv], PT[:, kt, j * P:j * P + P], values(a, j, kt),
                                       start=kt == 0, stop=kt == a.nkt[j] - 1)
                ins.then_inc(s["pv"], 1)
                flush()
        if not stop:
            experts_pe(pe)
    ctx.close()


def _constants():
    c = np.zeros((P, C_N), np.float32)
    row, col = np.arange(P)[:, None], np.arange(P)[None, :]
    c[:, C_ID:C_ID + P] = row == col
    c[:, C_LT:C_LT + P] = col < row
    c[:, C_NEG:C_NEG + P] = np.where(col < row, 0.0, NEG)
    for i, (cb, bs) in enumerate(((0, 0), (1, 8), (3, 32))):
        q = cb * 16 + np.arange(P)[:, None] // 8
        start = np.clip(q - 8, 0, 48)
        k = bs + np.arange(32)[None, :]
        c[:, C_NAM + 32 * i:C_NAM + 32 * i + 32] = np.where((k >= start) & (k < start + 16), 0.0, NEG)
    c[:, C_ONE:C_ONE + P] = 1.0
    c[:, C_TC:C_TC + 4] = np.arange(P)[:, None] + P * np.arange(4)[None, :]
    c[:, C_EPS6], c[:, C_EPS5] = 1e-6, 1e-5
    t = np.arange(S)
    inv = np.float32(10000.0) ** (-np.arange(0, 32, 2, dtype=np.float32) / np.float32(32))
    ang = np.concatenate([(t // 64).astype(np.float32)[:, None] * inv, (t % 64).astype(np.float32)[:, None] * inv], 1)
    for at, f in ((C_COS, np.cos), (C_SIN, np.sin)):
        c[:, at:at + 128] = f(ang).astype(np.float32).reshape(TT, P, 32).transpose(1, 0, 2).reshape(P, 128)
    c[:, C_IOTA:C_IOTA + S] = t[None, :]
    return c


def kernel(**inputs):
    import concourse.bacc as _bacc
    from concourse.bass_utils import run_bass_kernel_spmd as _run

    a = {k: np.ascontiguousarray(v) for k, v in inputs.items()}

    def cols(v):
        return v.reshape(-1, P).T

    conv = a["conv_w"][0].reshape(4, 4, P).transpose(2, 1, 0).reshape(P, 16)
    vecs = np.concatenate(
        [cols(a["norm_mix"]), cols(a["norm_ffn"]), conv, cols(a["conv_b"]), cols(a["b_rg"]), cols(a["b_ig"]),
         cols(a["lru_lambda"]), cols(a["norm_lru_out"]), cols(a["norm_att_out"]), cols(a["b_gate_2"]),
         np.tile(a["gqa_q_gain_2"], (P, 1)), np.tile(a["gqa_k_gain_2"], (P, 1))], axis=1)
    rows = np.concatenate([a["norm_final"][None], a["ln1_g_2"], a["ln1_b_2"], a["ln2_g_2"], a["ln2_b_2"]])
    rpb = np.concatenate([np.zeros(16, np.float32), a["na_rpb_2"].reshape(-1), np.zeros(64, np.float32)])
    arrays = dict(
        x=a["x"], w_in=a["w_in"], w_out=a["w_out"], w_ffn_in=a["w_ffn_in"], w_ffn_out=a["w_ffn_out"],
        mem=a["mem_2"], w_in2=a["w_in_2"], w_memkv=a["w_mem_kv_2"], w_branch=a["w_branch_2"],
        w_out2=a["w_out_2"], w_router=a["w_router_2"], w_gu=a["w_gate_up_2"], w_down=a["w_down_2"],
        w_rg=a["w_rg"], w_ig=a["w_ig"], rows=rows, rpb=rpb, vecs=vecs, consts=_constants())
    arrays = {k: np.ascontiguousarray(v) for k, v in arrays.items()}
    nc = _bacc.Bacc("TRN2", target_bir_lowering=False, num_devices=1)
    args = {k: nc.dram_tensor(k, v.shape, F32, kind="ExternalInput").ap() for k, v in arrays.items()}
    args["out"] = nc.dram_tensor("out", (1, S, D), F32, kind="ExternalOutput").ap()
    build(nc, **args)
    return _run(nc, [arrays], core_ids=[0]).results[0]["out"]
```

```python
from contextlib import ExitStack

import numpy as np
import concourse.bass as bass
from concourse import mybir

P = 128
S = 512
D = 1024
KT = D // P
TT = S // P
UC = 256
DFF = 2816
E = 16
CAP = 64
DFE = 1024
M = 256
QE = 4
RS = 6
ALPHA = 2.0 ** 0.25
NEG = -1e30

F32 = mybir.dt.float32
F32R = mybir.dt.float32r
U32 = mybir.dt.uint32
ALU = mybir.AluOpType
ACT = mybir.ActivationFunctionType
AX = mybir.AxisListType.X

C_ID, C_LT, C_NEG, C_NAM, C_ONE, C_TC = 0, 128, 256, 384, 480, 608
C_EPS6, C_EPS5, C_COS, C_SIN, C_IOTA = 612, 613, 614, 742, 870
C_N1 = C_IOTA
C_N = C_IOTA + S
V_GMIX, V_GFFN, V_CW, V_CB, V_BRG, V_BIG, V_LAM, V_GLRU, V_GATT, V_BG, V_GQ = 0, 8, 16, 32, 36, 40, 44, 48, 52, 56, 80
V_N = 80 + 128


class Step:

    def __init__(self, kind, counts, after=None, kw=None, dst=None, src=None,
                 u=None, w=None, c0=0, K=KT, mode=None, evac=None, nt=S, row0=0, who=(), r0=0,
                 dh=None, dl=None, nf=0, T=TT, scale=None, perm=False, f32=False, const=1.0, n0=0,
                 d=0, grow=None, rows=None,
                 att=None, h=0, half=0, n=0, qt=(), nkt=(), a=None):
        self.kind, self.counts, self.after, self.kw, self.dst, self.src = kind, counts, after, kw, dst, src
        self.u, self.w, self.c0, self.K, self.mode, self.evac = u, w, c0, K, mode, evac
        self.nt, self.row0, self.who, self.r0 = nt, row0, who, r0
        self.dh, self.dl, self.nf, self.T, self.scale = dh, dl, nf, T, scale
        self.perm, self.f32, self.const, self.n0 = perm, f32, const, n0
        self.d, self.grow, self.rows = d, grow, rows
        self.att, self.h, self.half, self.n, self.qt, self.nkt, self.a = att, h, half, n, qt, nkt, a
        self.c = self.o = None


def number(plan):
    at = {}
    for st in plan:
        st.at = dict(at)
        for s, n in st.counts.items():
            at[s] = at.get(s, 0) + n
        st.end = dict(at)
    return at


def build(nc, x, w_in, w_out, w_ffn_in, w_ffn_out, mem, w_in2, w_memkv, w_branch, w_out2, w_router,
          w_gu, w_down, w_rg, w_ig, rows, rpb, vecs, consts, out):
    ctx = ExitStack()
    base = (nc.sbuf_base + 63) // 64 * 64

    def at(name, kb, shape, dt=F32):
        return nc.alloc_sbuf_tensor_at(name, shape, dt, offset=base + int(kb * 1024), align_bytes=32)

    def sem(name):
        return ctx.enter_context(nc.semaphore(name))

    XH = at("XH", 0, [P, KT, S], F32R)
    XL = at("XL", 16, [P, KT, S], F32R)
    YSQ = at("YSQ", 24, [P, 4, S])
    X2T = at("X2T", 0, [P, KT, S])
    WH = at("WH", 32, [P, 2, KT * UC], F32R)
    WL = at("WL", 48, [P, 2, KT * UC], F32R)
    AH = at("AH", 64, [P, KT, S], F32R)
    AL = at("AL", 80, [P, KT, S], F32R)
    XN = at("XN", 64, [P, TT, D])
    MH = at("MH", 144.5, [P, KT, M], F32R)
    ML = at("ML", 152.5, [P, KT, M], F32R)
    LX = at("LX", 64, [P, 4, 3 + S])
    LTH = at("LTH", 64, [P, 4, S])
    LG = at("LG", 72.25, [P, 4, S])
    LC = at("LC", 80.5, [P, 4, S])
    LI = at("LI", 88.5, [P, 4, S])
    YL_ = at("YL_", 80.5, [P, 4, S])
    SE = at("SE", 64, [P, 2, 2, S])
    SP_ = at("SP_", 72, [P, 2, S])
    SC = at("SC", 92, [P, 2, S])
    RBC = at("RBC", 78, [P, S])
    YH2 = at("YH2", 64, [P, 4, S], F32R)
    YL2 = at("YL2", 80, [P, 4, S], F32R)
    SN = at("SN", 64, [P, 2, 2, M])
    TMP = at("TMP", 189.5, [P, 4, S])
    VN = at("VN", 72, [P, TT, 512])
    GQT = at("GQT", 88, [P, TT, 512])
    R0 = 96.5
    LR = at("LR", R0 + 40, [P, 4, S])
    MEMT = at("MEMT", R0 + 40, [P, 2, D])
    RAW = at("RAW", R0, [P, 2, KT * UC])
    RING = at("RING", R0, [P, RS, 2048])
    QT = at("QT", R0 + 16, [P, 4, S])
    KTT = at("KTT", R0 + 24, [P, 4, S])
    VT = at("VT", R0 + 32, [P, TT, 512])
    YT = at("YT", R0 + 40, [P, TT, 512])
    FG = at("FG", R0 + 16, [P, 2, S])
    FP = at("FP", R0 + 20, [P, 2, S])
    VB = at("VB", R0 + 32, [P, 4, 2, 512])
    QG = at("QG", R0 + 16, [P, 4, S])
    KG = at("KG", R0 + 24, [P, 2, S])
    QM = at("QM", R0 + 32, [P, 4, S])
    RT = at("RT", R0 + 24, [P, 3, 640])
    GFIN = at("GFIN", R0 + 16, [P, D])
    LNR = at("LNR", 64, [P, 2, D])
    GT = at("GT", R0 + 44, [P, 2, S])
    MG = at("MG", R0 + 48, [P, KT, S])
    KD = at("KD", R0 + 40, [P, TT, 256])
    X = at("X", 160.5, [P, TT, D])
    B48 = at("B48", 160.5, [P, 8, 8, 48])
    CST = at("CST", 176.5, [P, C_N1])
    VEC = at("VEC", 180, [P, V_N])
    ST = at("ST", 181, [P, 128])
    MKT = at("MKT", 181.5, [P, 4, M])
    MV = at("MV", 185.5, [P, 2, 512])
    PB = at("PB", 189.5, [P, 2, 2, S])
    PT = at("PT", 197.5, [P, 4, 256])
    KVT = at("KVT", 201.5, [P, TT, 256])
    BD = at("BD", 201.5, [P, 2, 4, P])
    YN = at("YN", 72, [P, TT, 512])
    IDB = at("IDB", 0, [P, E * CAP])
    OHT = at("OHT", 4, [P, TT, QE * CAP], F32R)
    XS = at("XS", 8, [P, KT, QE, 2, CAP], F32R)
    SS = at("SS", 24, [P, 2, S], F32R)
    HT = at("HT", 28, [P, 2, KT, 2, CAP], F32R)
    GUS = at("GUS", 36, [CAP, 4 * 512])
    LOH = at("LOH", 44, [CAP, 4 * 512])
    SG = at("SG", 52, [CAP, DFE])
    YHM = at("YHM", 56, [P, 2, D], F32R)
    YLM = at("YLM", 197.5, [P, 2, D], F32R)
    IOTA = at("IOTA", 205.5, [P, S])
    GCOL = at("GCOL", 180.8125, [P, E])
    ICOL = at("ICOL", 180.875, [P, E])
    WEH = [at(f"WEH{i}", 181.5 + 8 * i, [P, 2048], F32R) for i in range(2)]
    WEL = [at(f"WEL{i}", R0 + 48 + 8 * i, [P, 2048], F32R) for i in range(2)]
    LN2R = at("LN2R", 0, [P, 2, D])
    AF = at("AF", 56, [E, S])
    VAL = at("VAL", 58, [E, 2 * CAP])
    IDX = at("IDX", 58.5, [E, 2 * CAP])
    IDU = at("IDU", 59, [E, CAP], U32)
    WR = at("WR", 60, [P, KT, E])
    LGT = at("LGT", 61, [P, TT, E])
    X2H = at("X2H", 64, [P, TT, D], F32R)
    X2L = at("X2L", 80, [P, TT, D], F32R)

    ps = [ctx.enter_context(nc.psum_tensor(f"bank{i}", [P, 512], F32)) for i in range(8)]
    LIN, SB, TR, PV = ps[0:3], ps[3:5], ps[5:7], ps[7]

    TXB = [TR[0], TR[1], SB[0], SB[1]]

    ident = CST[:, C_ID:C_ID + P]
    ones = CST[:, C_ONE:C_ONE + P]

    def vec(c, n=1):
        return VEC[:, c:c + n]

    raw_in = [sem(f"raw_in{i}") for i in range(2)]
    names = """w_hi w_lo res evA evD act_hi act_lo tx_ps tx_hi tx_lo ms sd rc nrm conv gmm sig
               lexp lgl lt lm2 lsq lin lrec ysq ysum ysd yn yhi ylo qk mx e_ab st_d p tr ptA ptD pv o rope rxn rope_p
               ms_hi ms_lo saved band x2h x2l xal lgp lgs afp af top ixp icc""".split()
    names.extend(["rms_q", "rsd_q"])
    s = {n: sem(n) for n in names}
    x_in = [sem(f"x_in{t}") for t in range(TT)]
    consts_in, mem_in, rows_in, b48_in, xre_in, out_in, bd_in, bd0, moe_in = (
        sem(n) for n in "consts_in mem_in rows_in b48_in xre_in out_in bd_in bd0 moe_in".split())
    xd = nc.dram_tensor("x_saved", (S, D), F32, kind="Internal").ap().rearrange("(t p) d -> p t d", p=P)

    win_rpb = nc.dram_tensor("win_rpb", (16, 120, 48), F32, kind="Internal").ap()
    win_in = sem("win_in")

    rows2_in = sem("rows2_in")
    wr_in = sem("wr_in")

    def wait(e, name, values, less=0):
        v = values.get(name, 0) - less
        if v > 0:
            e.wait_ge(s[name], v)

    plan = []
    units, results, txs = [], [], []
    narrow = []
    lin_of, prev_of = [], []

    def add(kind, counts, **kw):
        st = Step(kind, counts, **kw)
        plan.append(st)
        return st

    def unit(w, c0, K, mode, evac, dst=None, src="x", nt=S, row0=0, **kw):
        nres = 2 if mode == "F" else nt // 256
        sh = []
        for r in range(nres):
            if evac == "ffn":
                sh.append("act" if r == 0 else "dve")
            elif evac in ("accX", "mixX", "branch"):
                sh.append("dve")
            elif evac in ("gate", "naq", "scaled"):
                sh.append("act")
            else:
                sh.append("act" if (r + len(units)) % 2 else "dve")
        counts = dict(w_hi=1, w_lo=1, res=nres, evA=sh.count("act"), evD=sh.count("dve"))
        if evac == "ffn":
            counts.update(act_hi=1, act_lo=1)
        st = add("unit", counts, u=len(units), w=w, c0=c0, K=K, mode=mode, evac=evac, dst=dst, src=src,
                 nt=nt, row0=row0, who=sh, r0=len(results), kw=kw)
        units.append(st)
        for r in range(nres):
            b = (len(results) if not lin_of else lin_of[-1] + 1) % (2 if narrow else 3)
            prev_of.append(max((i for i, c in enumerate(lin_of) if c == b), default=None))
            lin_of.append(b)
            results.append((st, r))
        return st

    def tx(src, dh, dl, nf, T, scale=None, perm=False, f32=False, const=1.0, **kw):
        st = add("tx", dict(tx_ps=nf, tx_hi=nf, tx_lo=0 if f32 else nf), src=src, dh=dh, dl=dl, nf=nf,
                 T=T, scale=scale, perm=perm, f32=f32, const=const, n0=len(txs), kw=kw)
        txs.extend([st] * nf)
        return st

    def rms(src, dst, d, grow=None, **kw):
        return add("rms", dict(sd=1, rc=1, nrm=TT), src=src, dst=dst, d=d, grow=grow, kw=kw)

    atts = []

    def attention(kind, heads, halves, fill, after):
        n = heads * halves
        mine = []
        per = len(fill) / n
        done = 0
        narrow.append(True)

        def s_step(i):
            h, half = divmod(i, halves)
            a = add("S", dict(qk=2), att=kind, h=h, half=half, n=len(atts), after=after, r0=len(results))
            a.counts.update(dict(e_ab=2) if kind == "stick" else dict(mx=2))
            a.qt = [2 * half, 2 * half + 1]
            a.nkt = [q + 1 for q in a.qt] if kind == "stick" else [4, 4] if kind == "gqa" else [2, 2]
            mine.append(a)
            atts.append(a)

        def w_step(i):
            add("W", dict(st_d=2), a=mine[i])

        def x_step(i):
            add("X", dict(p=2), a=mine[i])

        def t_step(i):
            add("T", dict(tr=1), a=mine[i])

        def c_step(i):
            mine[i].c = add("C", dict(ptA=1, ptD=int(mine[i].nkt[1] > 2)), a=mine[i])

        def o_step(i):
            mine[i].o = add("O", dict(pv=1, o=1), a=mine[i])

        turn = (((x_step, 2), (s_step, 0), (o_step, 3), (t_step, 2), (c_step, 2), (w_step, 0)) if kind == "stick" else
                ((c_step, 2), (s_step, 0), (o_step, 2), (x_step, 1), (t_step, 1)))
        for i in range(n + max(lag for _, lag in turn)):
            for f, lag in turn:
                if 0 <= i - lag < n:
                    f(i - lag)
            while done < len(fill) and done < per * (i + 1):
                fill[done]()
                done += 1
        narrow.clear()
        return mine[-1].o

    win, win2 = w_in[0], w_in2[0]
    rms(X, XN, D, ready=x_in)
    tx(XN, XH, XL, KT, TT, scale=V_GMIX, feeds="x")
    for j in range(2):
        unit(win, UC * j, KT, "F", "copy", dst=lambda r, j=j: LX[:, 2 * j + r, 3:])
        if j == 0:
            tx(MEMT, MH, ML, KT, 2, landed=(mem_in, 16))
    lxu = plan[-1]
    conv = add("conv", dict(conv=1), after=lxu)
    for j in range(2):
        unit(win, 512 + UC * j, KT, "F", "copy", dst=lambda r, j=j: LG[:, 2 * j + r, :])
    lgu = plan[-1]
    for j in range(2):
        unit(win, 1024 + UC * j, KT, "F", "scaled", dst=lambda r, j=j: QT[:, 2 * j + r, :], scale=0.125)
    add("lgate", dict(gmm=8, sig=8), after=lgu)
    for j in range(2):
        unit(win, 1536 + UC * j, KT, "F", "copy", dst=lambda r, j=j: KTT[:, 2 * j + r, :])
        add(*(("ldecay", dict(lexp=1, lgl=1, lt=1, lm2=1)), ("lroot", dict(lsq=2, lin=1)))[j], after=lgu)
    for j in range(2):
        unit(win, 2048 + UC * j, KT, "T", "copy", dst=lambda r, j=j: VT[:, 2 * r:2 * r + 2, UC * j:UC * j + UC])
        if j == 0:
            add("lscan", dict(lrec=1), after=lgu)
    qkv = plan[-1]
    add("logexp", {})
    fill = [lambda: add("lsquare", dict(ysq=1), after=qkv),
            lambda: add("lnorm", dict(ysum=1, ysd=1, yn=1), after=qkv),
            lambda: add("lsplit", dict(yhi=4, ylo=4), after=qkv)]
    last = attention("stick", 8, 2, fill, qkv)
    rms(YT, YT, 512, after=last)
    tx(YT, XH[:, 4:8], XL[:, 4:8], 4, TT, scale=V_GATT, k0=4, feeds="x")
    for j in range(4):
        unit(w_out[0], UC * j, KT, "T", "accX")
    rms(X, XN, D, after=plan[-1])
    tx(XN, XH, XL, KT, TT, scale=V_GFFN, feeds="x")
    for f0, nf in ((0, 8), (8, 8), (16, 6)):
        for f in range(f0, f0 + nf):
            unit(w_ffn_in[0], P * f, KT, "F", "ffn", f=f - f0)
        for j in range(4):
            unit(w_ffn_out[0], UC * j, nf, "T", "accX", src="a", row0=P * f0)
    fin = rms(X, X, D, grow=GFIN, after=plan[-1])
    save = add("save", dict(saved=16))
    txx = tx(X, XH, XL, KT, TT, norm=fin)
    for j in range(2):
        unit(win2, UC * j, KT, "F", "naq", dst=lambda r, j=j: QT[:, 2 * j + r, :])
    for j in range(2):
        unit(win2, 512 + UC * j, KT, "F", "copy", dst=lambda r, j=j: KTT[:, 2 * j + r, :])
    for j in range(2):
        unit(win2, 1024 + UC * j, KT, "T", "copy", dst=lambda r, j=j: VN[:, 2 * r:2 * r + 2, UC * j:UC * j + UC])
    naqkv = plan[-1]
    band = add("band", dict(band=16 * 16), after=naqkv)
    for j in range(2):
        unit(win2, 1536 + UC * j, KT, "T", "copy", dst=lambda r, j=j: GQT[:, 2 * r:2 * r + 2, UC * j:UC * j + UC])
    fill = [lambda: unit(win2, 2048, KT, "T", "copy", dst=lambda r: KVT[:, 2 * r:2 * r + 2, :])]
    fill += [lambda j=j: unit(w_memkv[0], UC * j, KT, "F", "copy", dst=lambda r, j=j: MKT[:, 2 * j + r, :],
                              src="m", nt=M) for j in range(2)]
    fill += [lambda j=j: unit(w_memkv[0], 512 + UC * j, KT, "T", "copy",
                              dst=lambda r, j=j: MV[:, :, UC * j:UC * j + UC], src="m", nt=M) for j in range(2)]
    na_last = attention("na", 8, 2, fill, band)
    def gate(g, j):
        return lambda: unit(win2, 2816 + D * g + UC * j, KT, "F", "gate", g=g, j=j)

    def branch(g, j):
        return lambda: unit(w_branch[0, g], UC * j, 4, "F", "branch", src="y", g=g, j=j)

    for t in range(TT):
        add("rope", dict(rope=1, rxn=1, rope_p=1), half=t, after=na_last)
        if t == 2:
            tx(YN, YH2, YL2, 4, TT, perm=True)
            gate(0, 0)()
        if t < 2:
            unit(win2, 2304 + UC * t, KT, "F", "scaled", dst=lambda r, j=t: QM[:, 2 * j + r, :],
                 scale=float(P) ** -0.5)
    branch(0, 0)()
    tx(GQT, QG, None, 4, TT, f32=True, const=0.125)
    tx(KD, KG, None, 2, TT, f32=True)
    gq = plan[-1]

    fill = []
    for j in range(1, 4):
        fill += [gate(0, j), branch(0, j)]
    gl = attention("gqa", 8, 2, fill, gq)
    tx(YN, YH2, YL2, 4, TT)
    fill = [f for j in range(4) for f in (gate(1, j), branch(1, j))]
    ml = attention("mem", 4, 2, fill, plan[-1])
    tx(YN, YH2, YL2, 4, TT)
    for j in range(4):
        gate(2, j)()
        branch(2, j)()
    add("msplit", dict(ms_hi=KT, ms_lo=KT), after=plan[-1])
    for j in range(4):
        unit(w_out2[0], UC * j, KT, "T", "mixX")
    last_mix = plan[-1]
    ln1 = add("ln", dict(ms=1, sd=1, rc=1, nrm=TT), rows=LNR, after=plan[-1])
    tx2 = tx(X, X2T, None, KT, TT, f32=True, norm=ln1)
    router = add("router", dict(lgp=1, xal=TT))
    total = number(plan)
    res_shares = []
    a = d = 0
    for st, r in results:
        a += st.who[r] == "act"
        d += st.who[r] == "dve"
        res_shares.append((a, d))
    tx_free = []
    h = l = 0
    for st in txs:
        h += 1
        l += not st.f32
        tx_free.append((h, l))

    SRC = {"x": (XH, XL), "m": (MH, ML), "a": (AH, AL), "y": (YH2, YL2)}

    def bank_free(e, st, n):
        if prev_of[n] is not None:
            evacuated(e, prev_of[n])
        if lin_of[n]:
            wait(e, "st_d", st.at)
        if lin_of[n] == 2:
            wait(e, "mx", st.at)
            wait(e, "p", st.at)

    class Chain:

        def __init__(self, e, name):
            self.e, self.s, self.n = e, sem(name), 0

        def link(self, ins):
            ins.then_inc(self.s, 1)
            self.n += 1
            self.e.wait_ge(self.s, self.n)

        def sign(self, ins):
            ins.then_inc(self.s, 1)
            self.n += 1
            return self.n

        def need(self, value):
            self.e.wait_ge(self.s, value)


    def pieces(a, b):
        bank = TR[b][:, :].rearrange("p (k q) -> p k q", k=2)
        if a.nkt[0] >= 2 * b + 2:
            return [(PT[:, 2 * b:2 * b + 2, :], bank)]
        return [(PT[:, 2 * b, :], bank[:, 0, :]), (PT[:, 2 * b + 1, P:], bank[:, 1, P:])]

    score_banks, score_prev = [], []
    for a in atts:
        turn = [3, 4, 2, 1] if a.att == "stick" else [3, 4, 2]
        for j in range(2):
            b = turn[(2 * a.n + j) % len(turn)]
            score_prev.append(max((i for i, c in enumerate(score_banks) if c == b), default=None))
            score_banks.append(b)

    def score_bank(a, j):
        return ps[score_banks[2 * a.n + j]]

    def evacuated(e, n):
        a, d = res_shares[n]
        if a:
            e.wait_ge(s["evA"], a)
        if d:
            e.wait_ge(s["evD"], d)

    def score_bank_free(e, a, j):
        for n in range(a.r0 - 1, -1, -1):
            if ps[lin_of[n]] is score_bank(a, j):
                evacuated(e, n)
                break
        q = score_prev[2 * a.n + j]
        if q is not None:
            b = atts[q // 2]
            name = {"stick": "st_d", "na": "mx"}.get(b.att)
            if name:
                e.wait_ge(s[name], b.at.get(name, 0) + q % 2 + 1)
            else:
                e.wait_ge(s["p"], q + 1)

    def shaped(st, bank):
        if st.mode == "F":
            return bank[:, :st.nt]
        return bank[:, :].rearrange("p (t c) -> p t c", t=2)

    def rope_views():
        return (RT[:, 0, :].rearrange("p (h c) -> p h c", h=10),
                RT[:, 1, :].rearrange("p (i h c) -> p i h c", i=2, h=10),
                RT[:, 2, :].rearrange("p (i h c) -> p i h c", i=2, h=10))

    def rotate(engine, link, t, two, i, factors, op):
        xn = rope_views()[0]
        for n, col in enumerate(factors):
            f = CST[:, col + 32 * t:col + 32 * t + 32].unsqueeze(1).to_broadcast([P, 10, 32])
            ins = engine.tensor_tensor(two[:, n], xn[:, :, n::2], f, ALU.mult)
        link(ins)
        q = GQT[:, t, :].rearrange("p (h c) -> p h c", h=8)
        engine.tensor_tensor(q[:, :, i::2], two[:, 0, 0:8], two[:, 1, 0:8], op)
        for dup in range(2):
            kd = KD[:, t, :].rearrange("p (g u c) -> p g u c", g=2, u=2)[:, :, dup, i::2]
            ins = engine.tensor_tensor(kd, two[:, 0, 8:10], two[:, 1, 8:10], op)
        return ins

    def tokens_first(st, f, bank, dst):
        t, g = divmod(f, 2)
        return bank.rearrange("p (f c) -> p f c", c=P), dst[:, 4 * g:4 * g + 4, t * P:t * P + P]

    def layer_norm_act(act, end):
        wait(act, "ms", end)
        nc.scalar.activation(ST[:, 4:8], ST[:, 97:105:2], ACT.Sqrt,
                             bias=CST[:, C_EPS5:C_EPS5 + 1]).then_inc(s["sd"], 1)

    def layer_norm_stats(link, tiles):
        V = nc.vector
        for t in tiles:
            V.bn_stats(ST[:, 48 + 12 * t:54 + 12 * t], X[:, t, 0:512])
            link(V.bn_stats(ST[:, 54 + 12 * t:60 + 12 * t], X[:, t, 512:1024]))

    def layer_norm_dve(dve, link, end, rows_, landed, value, tiles=range(TT)):
        V = nc.vector
        layer_norm_stats(link, tiles)
        for t in range(TT):
            ins = V.bn_aggr(ST[:, 96 + 2 * t:98 + 2 * t],
                            ST[:, 48 + 12 * t:60 + 12 * t].rearrange("p (i c) -> p i c", i=2))
        ins.then_inc(s["ms"], 1)
        wait(dve, "sd", end)
        V.reciprocal(ST[:, 8:12], ST[:, 4:8]).then_inc(s["rc"], 1)
        wait(dve, "rc", end)
        wait(dve, "ms", end)
        dve.wait_ge(landed, value)
        for t in range(TT):
            link(V.scalar_tensor_tensor(X[:, t, :], X[:, t, :], ST[:, 96 + 2 * t:97 + 2 * t],
                                        rows_[:, 0, :], ALU.subtract, ALU.mult))
            V.scalar_tensor_tensor(X[:, t, :], X[:, t, :], ST[:, 8 + t:9 + t],
                                   rows_[:, 1, :], ALU.mult, ALU.add).then_inc(s["nrm"], 1)

    QUADS, CH = E // QE, 24
    ring_in = [sem(f"ring_in{i}") for i in range(RS)]
    (wh, wlD, wlP, used, oht, ssr, gth, xsh, xsl, ev_lo, ev, su, hm, tp, hh, hl, yh, yl, sct, acc) = (
        sem(n) for n in "wh wlD wlP used oht ssr gth xsh xsl ev_lo ev su hm tp hh hl yh yl sct acc".split())
    GU = [LIN[0], LIN[1], LIN[2], PV]
    XG = [SB[0], SB[1], GU[2], GU[3]]
    YB = [SB, TR]
    HB = TR[0]
    PC = 704
    gu_v = w_gu[0].rearrange("e (k p) f -> p (e k) f", p=P)
    dn_v = w_down[0].rearrange("e (i k p) d -> p (e i) k d", k=2, p=P)

    def quads(e, body):
        body(0, True, False)
        with e.Fori(1, QUADS - 1) as p:
            body(p, False, False)
        body(QUADS - 1, False, True)

    def experts_sp(sp):
        wait(sp, "w_lo", total)
        wait(sp, "pv", total)

        def body(p, first, last):
            for n in range(2 * CH):
                i, c = divmod(n, CH)
                slot = RING[:, n % RS, :]
                if not (first and n < RS):
                    sp.wait_ge(wlD, 2 * CH * p + n - RS + 1)
                    sp.wait_ge(wlP, 2 * CH * p + n - RS + 1)
                if c < 16:
                    row = (QE * p + 2 * i + c // 8) * 8 + c % 8
                    src = gu_v[:, bass.ds(row, 1), :].rearrange("p a f -> p (a f)")
                    sp.dma_start(slot, src).then_inc(ring_in[n % RS], 16)
                else:
                    row = (QE * p + 2 * i + (c - 16) // 4) * 4 + c % 4
                    src = dn_v[:, bass.ds(row, 1), :, :].rearrange("p a k d -> p (a k) d")
                    sp.dma_start(slot.rearrange("p (k d) -> p k d", k=2), src).then_inc(ring_in[n % RS], 16)
                if first and n == RS - 1:
                    wait(sp, "res", total)
                    sp.dma_start(WR[:, :, :], w_router[0].rearrange("(k p) e -> p k e", p=P)).then_inc(wr_in, 16)

        quads(sp, body)
        for t in range(TT):
            sp.wait_ge(s["nrm"], total["nrm"] + t + 1)
            sp.dma_start(out[0].rearrange("(t p) d -> t p d", p=P)[t], X[:, t, :]).then_inc(out_in, 16)
        sp.wait_ge(out_in, 16 * TT)

    def experts_pool(pool):
        def body(p, first, last):
            for n in range(2 * CH):
                i, c = divmod(n, CH)
                pool.wait_ge(wh, 2 * CH * p + n + 1)
                nc.gpsimd.tensor_tensor(WEL[n % 2][:, 2048 - PC:], RING[:, n % RS, 2048 - PC:],
                                        WEH[n % 2][:, 2048 - PC:].bitcast(F32), ALU.subtract).then_inc(wlP, 1)

        quads(pool, body)
        pool.wait_ge(gth, 4 * QUADS)
        for i in range(2):
            pool.dma_start(LN2R[:, i, :], rows[3 + i].partition_broadcast(P)).then_inc(rows2_in, 16)

    def experts_act(act, chain):
        A = nc.scalar.activation
        wait(act, "nrm", total)
        for t in range(TT):
            A(X2H[:, t, :], X[:, t, :], ACT.Copy).then_inc(s["x2h"], 1)
        wait(act, "pv", total)
        act.dma_start(IOTA[:, :], consts[:, C_IOTA:C_IOTA + S]).then_inc(moe_in, 16)
        act.wait_ge(s["lgs"], 1)
        A(LGT[:, :, :], LGT[:, :, :], ACT.Exp).then_inc(s["afp"], 1)
        act.wait_ge(s["icc"], 1)

        def outputs(x, e):
            for h in range(2):
                A(YHM[:, e, 512 * h:512 * h + 512], YB[e][h][:, :], ACT.Copy,
                  scale=GCOL[:, bass.ds(x, 1)]).then_inc(yh, 1)

        def body(p, first, last):
            for n in range(2 * CH):
                i, c = divmod(n, CH)
                C, x = 2 * CH * p + n, QE * p + 2 * i
                act.wait_ge(ring_in[n % RS], 16 * (2 * CH // RS * p + n // RS + 1))
                if not (first and n < 2):
                    act.wait_ge(used, C - 1)
                A(WEH[n % 2][:, :], RING[:, n % RS, :], ACT.Copy).then_inc(wh, 1)
                if c == 0 and not (first and i == 0):
                    act.wait_ge(used, C)
                    outputs(x - 1, 1)
                if n == 0:
                    for b in range(4):
                        act.wait_ge(gth, 4 * p + b + 1)
                        A(XS[:, 2 * b:2 * b + 2, :, 0, :],
                          XG[b][:, :].rearrange("p (k e c) -> p k e c", k=2, e=QE), ACT.Copy).then_inc(xsh, 1)
                if c in (8, 16):
                    act.wait_ge(used, C)
                    if not (first and n == 8):
                        act.wait_ge(ev, 4 * (x + c // 8 - 1))
                    for b in range(4):
                        A(LOH[:, 512 * b:512 * b + 512], GU[b][CAP:P, :], ACT.Copy).then_inc(ev_lo, 1)
                if c in (9, 17):
                    act.wait_ge(ev, 4 * (x + c // 8 - 1) + 2)
                    if not (first and n == 9):
                        act.wait_ge(tp, x + c // 8 - 1)
                    A(SG[:, :], GUS[:, 0:DFE], ACT.Silu).then_inc(su, 1)
                if c in (11, 19):
                    act.wait_ge(tp, x + c // 8)
                    A(HT[:, c // 8 - 1, :, 0, :], HB[:, :].rearrange("p (f c) -> p f c", c=CAP),
                      ACT.Copy).then_inc(hh, 1)
                if c == 20:
                    act.wait_ge(used, C)
                    outputs(x, 0)

        quads(act, body)
        act.wait_ge(used, 2 * CH * QUADS)
        outputs(E - 1, 1)
        layer_norm_act(act, {k: v + 1 for k, v in total.items()})

    def experts_dve(dve, chain):
        V, link = nc.vector, chain.link
        dve.wait_ge(s["lgp"], 1)
        lg = PV[:, 0:TT * E].rearrange("p (t e) -> p t e", e=E)
        link(V.tensor_reduce(ST[:, 0:4], lg, AX, ALU.max))
        V.tensor_tensor(LGT[:, :, :], lg, ST[:, 0:4].unsqueeze(2).to_broadcast([P, TT, E]),
                        ALU.subtract).then_inc(s["lgs"], 1)
        dve.wait_ge(s["afp"], 1)
        link(V.tensor_reduce(ST[:, 4:8], LGT[:, :, :], AX, ALU.add))
        link(V.reciprocal(ST[:, 8:12], ST[:, 4:8]))
        V.tensor_tensor(LGT[:, :, :], LGT[:, :, :], ST[:, 8:12].unsqueeze(2).to_broadcast([P, TT, E]),
                        ALU.mult).then_inc(s["af"], 1)
        dve.wait_ge(s["ixp"], 1)
        link(V.tensor_copy(AF[:, :], SB[0][0:E, :]))
        for i in range(CAP // 8):
            r = slice(8 * i, 8 * i + 8)
            link(V.max(VAL[:, r], AF[:, :]))
            V.max_index(IDU[:, r], VAL[:, r], AF[:, :])
            link(V.match_replace(AF[:, :], VAL[:, r], AF[:, :], -1.0))
        V.tensor_copy(VAL[:, CAP:2 * CAP], VAL[:, 0:CAP])
        V.tensor_copy(IDX[:, 0:CAP], IDU[:, :])
        V.tensor_copy(IDX[:, CAP:2 * CAP], IDU[:, :]).then_inc(s["top"], 1)
        dve.wait_ge(s["ixp"], 2)
        V.tensor_copy(GCOL[:, :], SB[1][:, 0:E])
        V.tensor_copy(ICOL[:, :], SB[1][:, E:2 * E])
        for h in range(2):
            ins = V.tensor_copy(IDB[:, 512 * h:512 * h + 512], LIN[h][:, :])
        ins.then_inc(s["icc"], 1)
        dve.wait_ge(s["icc"], 1)
        wait(dve, "xal", total)

        def outputs(x, e):
            for h in range(2):
                dve.wait_ge(yh, 2 * x + h + 1)
                c = slice(512 * h, 512 * h + 512)
                V.scalar_tensor_tensor(YLM[:, e, c], YB[e][h][:, :], GCOL[:, bass.ds(x, 1)],
                                       YHM[:, e, c].bitcast(F32), ALU.mult, ALU.subtract).then_inc(yl, 1)

        def one_hot_tokens(p):
            for t in range(TT):
                ins = V.tensor_scalar(OHT[:, t, :], IDB[:, bass.ds(p * QE * CAP, QE * CAP)],
                                      CST[:, C_TC + t:C_TC + t + 1], None, ALU.is_equal)
            ins.then_inc(oht, 1)

        def accumulate(g, k):
            dve.wait_ge(sct, 8 * g + k + 1)
            xs = X[:, k // 2, 512 * (k % 2):512 * (k % 2) + 512]
            V.tensor_tensor(xs, TR[k % 2][:, :], xs, ALU.add).then_inc(acc, 1)

        def body(p, first, last):
            for n in range(2 * CH):
                i, c = divmod(n, CH)
                x = QE * p + 2 * i
                dve.wait_ge(wh, 2 * CH * p + n + 1)
                V.tensor_tensor(WEL[n % 2][:, :2048 - PC], RING[:, n % RS, :2048 - PC],
                                WEH[n % 2][:, :2048 - PC].bitcast(F32), ALU.subtract).then_inc(wlD, 1)
                if c == 0 and not (first and i == 0):
                    outputs(x - 1, 1)
                if n == 0:
                    for b in range(4):
                        dve.wait_ge(xsh, 4 * p + b + 1)
                        V.tensor_tensor(XS[:, 2 * b:2 * b + 2, :, 1, :],
                                        XG[b][:, :].rearrange("p (k e c) -> p k e c", k=2, e=QE),
                                        XS[:, 2 * b:2 * b + 2, :, 0, :].bitcast(F32), ALU.subtract).then_inc(xsl, 1)
                if c in (8, 16):
                    for b in range(4):
                        dve.wait_ge(ev_lo, 4 * (x + c // 8 - 1) + b + 1)
                        V.tensor_tensor(GUS[:, 512 * b:512 * b + 512], GU[b][0:CAP, :],
                                        LOH[:, 512 * b:512 * b + 512], ALU.add).then_inc(ev, 1)
                if c in (9, 17):
                    dve.wait_ge(su, x + c // 8)
                    dve.wait_ge(ev, 4 * (x + c // 8))
                    V.tensor_tensor(SG[:, :], SG[:, :], GUS[:, DFE:], ALU.mult).then_inc(hm, 1)
                if c in (11, 19):
                    dve.wait_ge(hh, x + c // 8)
                    j = c // 8 - 1
                    V.tensor_tensor(HT[:, j, :, 1, :], HB[:, :].rearrange("p (f c) -> p f c", c=CAP),
                                    HT[:, j, :, 0, :].bitcast(F32), ALU.subtract).then_inc(hl, 1)
                if 2 <= c < 10 and not (first and i == 0):
                    accumulate(2 * p + i - 1, c - 2)
                if c == 20:
                    outputs(x, 0)
                if c == 12:
                    if not (first and i == 0):
                        dve.wait_ge(sct, 8 * (2 * p + i))
                    for e in range(2):
                        ins = V.tensor_scalar(SS[:, e, :], IOTA[:, :], ICOL[:, bass.ds(QE * p + 2 * i + e, 1)],
                                              None, ALU.is_equal)
                    ins.then_inc(ssr, 1)
                if n == 14 and not last:
                    dve.wait_ge(gth, 4 * p + 4)
                    one_hot_tokens(p + 1)

        dve.wait_ge(moe_in, 16)
        one_hot_tokens(0)
        quads(dve, body)
        outputs(E - 1, 1)
        for k in range(2 * TT):
            accumulate(E // 2 - 1, k)
        dve.wait_ge(acc, 8 * (E // 2))
        layer_norm_dve(dve, link, {k: v + 1 for k, v in total.items()}, LN2R, rows2_in, 32)

    def affinities(t):
        nc.tensor.wait_ge(s["tx_hi"], tx2.at["tx_hi"] + 2 * t + 2)
        for k in range(KT):
            ins = nc.tensor.matmul(PV[:, E * t:E * t + E], X2T[:, k, t * P:t * P + P], WR[:, k, :],
                                   start=k == 0, stop=k == KT - 1)
        if t == TT - 1:
            ins.then_inc(s["lgp"], 1)

    def experts_pe(pe):
        T = nc.tensor
        for name in ("o", "evA", "evD", "p", "ptA", "ptD"):
            wait(pe, name, total)
        affinities(TT - 1)
        pe.wait_ge(s["af"], 1)
        for t in range(TT):
            ins = T.transpose(SB[0][0:E, t * P:t * P + P], LGT[:, t, :], ident)
        ins.then_inc(s["ixp"], 1)
        pe.wait_ge(s["top"], 1)
        T.transpose(SB[1][:, 0:E], VAL[:, :], ident[0:E, 0:E])
        T.transpose(SB[1][:, E:2 * E], IDX[:, :], ident[0:E, 0:E])
        for e in range(E):
            ins = T.matmul(LIN[e // 8][:, (e % 8) * CAP:(e % 8 + 1) * CAP],
                           ident[0:E, e:e + 1].to_broadcast([E, P]), IDX[:, 0:CAP], start=True, stop=True)
        ins.then_inc(s["ixp"], 1)
        pe.wait_ge(s["icc"], 1)
        pe.wait_ge(s["x2l"], TT)

        def gather(p):
            pe.wait_ge(oht, p + 1)
            for d in range(KT):
                o = XG[d // 2][:, d % 2 * 256:d % 2 * 256 + 256]
                for t in range(TT):
                    T.matmul(o, X2H[:, t, d * P:d * P + P], OHT[:, t, :], start=t == 0, stop=False)
                    ins = T.matmul(o, X2L[:, t, d * P:d * P + P], OHT[:, t, :], start=False, stop=t == TT - 1)
                if d % 2:
                    ins.then_inc(gth, 1)

        def scatter(g, k, experts):
            t, c = slice(k // 2 * P, k // 2 * P + P), slice(512 * (k % 2), 512 * (k % 2) + 512)
            if k == 0:
                pe.wait_ge(yh, 2 * experts)
                pe.wait_ge(yl, 2 * experts)
                pe.wait_ge(ssr, g + 1)
            if k >= 2:
                pe.wait_ge(acc, 8 * g + k - 1)
            for e in range(2):
                T.matmul(TR[k % 2][:, :], SS[:, e, t], YHM[:, e, c], start=e == 0, stop=False)
                ins = T.matmul(TR[k % 2][:, :], SS[:, e, t], YLM[:, e, c], start=False, stop=e == 1)
            ins.then_inc(sct, 1)

        def body(p, first, last):
            for n in range(2 * CH):
                i, c = divmod(n, CH)
                C, x, g = 2 * CH * p + n, QE * p + 2 * i, 2 * p + i
                H, L = WEH[n % 2], WEL[n % 2]
                if n == 0:
                    pe.wait_ge(xsh, 4 * p + 4)
                    pe.wait_ge(xsl, 4 * p + 4)
                pe.wait_ge(wh, C + 1)
                if c < 16:
                    e, k = divmod(c, 8)
                    xk = XS[:, k, 2 * i + e, :, :].rearrange("p a c -> p (a c)")
                    for b in range(4):
                        if k == 0 and not (first and n == 0):
                            pe.wait_ge(ev, 4 * (x + e - 1) + b + 1)
                        T.matmul(GU[b][:, :], xk, H[:, 512 * b:512 * b + 512], start=k == 0, stop=False)
                    pe.wait_ge(wlD, C + 1)
                    pe.wait_ge(wlP, C + 1)
                    for b in range(4):
                        ins = T.matmul(GU[b][:, :], xk, L[:, 512 * b:512 * b + 512], start=False, stop=k == 7)
                else:
                    e, r = divmod(c - 16, 4)
                    if r == 0:
                        pe.wait_ge(hl, x + e + 1)
                        if e == 0 and not (first and i == 0):
                            pe.wait_ge(yl, 2 * (x - 1))
                    for part in (H, L):
                        if part is L:
                            pe.wait_ge(wlD, C + 1)
                            pe.wait_ge(wlP, C + 1)
                        for k in range(2):
                            hk = HT[:, e, 2 * r + k, :, :].rearrange("p a c -> p (a c)")
                            for h in range(2):
                                ins = T.matmul(YB[e][h][:, :], hk, part[:, D * k + 512 * h:D * k + 512 * h + 512],
                                               start=r + k == 0 and part is H, stop=r == 3 and k == 1 and part is L)
                ins.then_inc(used, 1)
                if c < 8 and not (first and i == 0):
                    scatter(g - 1, c, x)
                if c in (10, 18):
                    e = c // 8 - 1
                    pe.wait_ge(hm, x + e + 1)
                    if e:
                        pe.wait_ge(hl, x + 1)
                    elif not (first and i == 0):
                        pe.wait_ge(acc, 8 * g)
                    T.matmul(HB[:, 0:CAP], SG[:, 0:P], ident[0:CAP, 0:CAP], start=True, stop=True)
                    for f in range(1, KT):
                        ins = T.transpose(HB[:, CAP * f:CAP * f + CAP], SG[:, f * P:f * P + P], ident[0:CAP, 0:CAP])
                    ins.then_inc(tp, 1)
            if not last:
                pe.wait_ge(yl, 2 * (QE * p + 3))
                pe.wait_ge(ev, 4 * (QE * p + 4))
                gather(p + 1)

        gather(0)
        quads(pe, body)
        for k in range(2 * TT):
            scatter(E // 2 - 1, k, E)

    block = ctx.enter_context(nc.Block())
    xv = x[0].rearrange("(t p) d -> t p d", p=P)

    @block.sync
    def _(sp):
        for t in range(TT):
            sp.dma_start(X[:, t, :], xv[t]).then_inc(x_in[t], 16)
        for st in plan:
            if st.kind == "unit":
                u, K = st.u, st.K
                if u >= 2:
                    sp.wait_ge(s["w_lo"], u - 1)
                dst = RAW[:, u % 2, :K * UC].rearrange("p (k c) -> p k c", c=UC)
                if st.evac == "ffn":
                    for g in range(2):
                        src = st.w[:, g * DFF + st.c0:g * DFF + st.c0 + P].rearrange("(k p) c -> p k c", p=P)
                        sp.dma_start(dst[:, :, g * P:g * P + P], src).then_inc(raw_in[u % 2], 16)
                else:
                    src = st.w[st.row0:st.row0 + K * P, st.c0:st.c0 + UC].rearrange("(k p) c -> p k c", p=P)
                    for h in range(2):
                        kk = slice(h * K // 2, (h + 1) * K // 2)
                        sp.dma_start(dst[:, kk, :], src[:, kk, :]).then_inc(raw_in[u % 2], 16)
                if u == 1:
                    sp.dma_start(MEMT[:, :, :], mem[0].rearrange("(t p) d -> p t d", p=P)).then_inc(mem_in, 16)
            elif st is router:
                experts_sp(sp)

    @block.gpsimd
    def _(pool):
        pool_chain = Chain(pool, "pool_chain")
        pool.memset(BD[:, :, :, :], 0.0).then_inc(bd0, 1)
        pool.wait_ge(bd0, 1)
        for w, wd in enumerate((w_rg, w_ig)):
            for q in range(2):
                pool.dma_start(BD[q * 64:q * 64 + 64, w, :, q * 64:q * 64 + 64],
                               wd[0].rearrange("(c q) i o -> q i c o", q=2)[q]).then_inc(bd_in, 16)
        for q in range(16):
            pool.dma_start(win_rpb[q], bass.AP(rpb.tensor, rpb.offset + 15 - q, [[31, 120], [1, 48]])).then_inc(win_in, 16)
        for st in plan:
            if st is fin:
                wait(pool, "evD", st.at)
                pool.dma_start(GFIN[:, :], rows[0].partition_broadcast(P)).then_inc(rows_in, 16)
            elif st.kind == "save":
                wait(pool, "nrm", st.at)
                pool.dma_start(xd, X[:, :, :]).then_inc(s["saved"], 16)
            elif st.kind == "rope":
                if st.half == 0:
                    wait(pool, "mx", st.at)
                    pool.dma_start(X[:, :, :], xd).then_inc(xre_in, 16)
                t = st.half
                pool.wait_ge(s["rxn"], t + 1)
                rotate(nc.gpsimd, pool_chain.link, t, rope_views()[2], 1, (C_SIN, C_COS),
                       ALU.add).then_inc(s["rope_p"], 1)
            elif st is ln1:
                wait(pool, "ms_lo", st.at)
                for i in range(2):
                    pool.dma_start(LNR[:, i, :], rows[1 + i].partition_broadcast(P)).then_inc(rows_in, 16)
            elif st is router:
                for t in range(TT):
                    pool.wait_ge(s["x2h"], t + 1)
                    nc.gpsimd.tensor_tensor(X2L[:, t, :], X[:, t, :], X2H[:, t, :].bitcast(F32),
                                            ALU.subtract).then_inc(s["x2l"], 1)
                wait(pool, "tx_hi", st.at)
                pool.wait_ge(s["x2l"], TT)
                for t in range(TT):
                    nc.gpsimd.tensor_scalar(X[:, t, :], X[:, t, :], ALPHA, 1.0, ALU.mult,
                                            ALU.mult).then_inc(s["xal"], 1)
                experts_pool(pool)
            elif st is txx:
                wait(pool, "saved", st.at)
                wait(pool, "tx_lo", st.end)
                pool.wait_ge(win_in, 16 * 16)
                for r in range(8):
                    src = bass.AP(win_rpb.tensor, (7 - r) * 48, [[120 * 48, 16], [15 * 48, 8], [1, 8 * 48]])
                    pool.dma_start(B48[r::8, :, :, :].rearrange("p h r j -> p h (r j)"), src).then_inc(b48_in, 16)
            elif st is band:
                wait(pool, "evA", st.at)
                wait(pool, "evD", st.at)
                for cb, bs in enumerate((0, 8, 24, 32)):
                    for b in range(2):
                        for a in range(2):
                            pool.dma_start(VB[(2 * b + a) * 32:(2 * b + a) * 32 + 32, cb, :, :],
                                           VN[a * 64 + bs:a * 64 + bs + 32, b::2, :]).then_inc(s["band"], 16)

    @block.scalar
    def _(act):
        chain = Chain(act, "act_chain")
        link = chain.link
        A = nc.scalar.activation
        act.dma_start(CST[:, :], consts[:, 0:C_N1]).then_inc(consts_in, 16)
        act.dma_start(VEC[:, :], vecs).then_inc(consts_in, 16)
        act.wait_ge(consts_in, 32)
        eps6, eps5, one = CST[:, C_EPS6:C_EPS6 + 1], CST[:, C_EPS5:C_EPS5 + 1], CST[:, C_ONE:C_ONE + 1]

        def split_hi(u):
            if u >= len(units):
                return
            n = units[u].K * UC
            act.wait_ge(raw_in[u % 2], 32 * (u // 2 + 1))
            if u >= 2:
                act.wait_ge(s["res"], units[u - 1].r0)
            A(WH[:, u % 2, :n], RAW[:, u % 2, :n], ACT.Copy).then_inc(s["w_hi"], 1)

        def evacuate(st):
            for r, who in enumerate(st.who):
                n = st.r0 + r
                bank = LIN[lin_of[n]]
                if st.evac == "ffn" and r == 1:
                    act.wait_ge(s["evD"], res_shares[n][1])
                    f = st.kw["f"]
                    A(AH[:, f, :], FP[:, f % 2, :], ACT.Copy).then_inc(s["act_hi"], 1)
                if who != "act":
                    continue
                act.wait_ge(s["res"], n + 1)
                if st.evac == "ffn":
                    ins = A(FG[:, st.kw["f"] % 2, :], bank[:, :], ACT.Silu)
                elif st.evac == "gate":
                    wait(act, "evD", st.at)
                    ins = A(GT[:, r, :], bank[:, :], ACT.Sigmoid,
                            bias=vec(V_BG + 8 * st.kw["g"] + 2 * st.kw["j"] + r))
                elif st.evac == "naq":
                    ins = A(st.dst(r).rearrange("p (b c r) -> p r b c", b=4, c=16),
                            bank[:, :].rearrange("p (r b c) -> p r b c", r=8, b=4), ACT.Copy, scale=0.125)
                elif st.evac == "scaled":
                    ins = A(st.dst(r), bank[:, :], ACT.Copy, scale=st.kw["scale"])
                else:
                    ins = A(st.dst(r), shaped(st, bank), ACT.Copy)
                ins.then_inc(s["evA"], 1)

        def pre_scores(a):
            n, v = a.n, [0, 0]
            for i in range(3):
                for j in range(2):
                    nk = a.nkt[j] * P
                    e = SE[:, n % 2, j, :nk]
                    if i == 0:
                        if n >= 2:
                            act.wait_ge(s["p"], 2 * n + j - 3)
                        act.wait_ge(s["qk"], 2 * n + j + 1)
                        v[j] = chain.sign(A(e, score_bank(a, j)[:, :nk], ACT.Abs))
                    else:
                        chain.need(v[j])
                        if i == 1:
                            v[j] = chain.sign(A(e, e, ACT.Exp, scale=-1.0))
                        else:
                            A(e, e, ACT.Ln, bias=one).then_inc(s["e_ab"], 1)

        def exponentials(a):
            n = a.n
            if n >= 2:
                act.wait_ge(s["tr"], n - 1)
                if a.att != "stick":
                    act.wait_ge(s["o"], n - 1)
            for j in range(2):
                nk = a.nkt[j] * P
                if a.att == "stick":
                    act.wait_ge(s["st_d"], 2 * n + j + 1)
                    A(PB[:, n % 2, j, :nk], SE[:, n % 2, j, :nk], ACT.Exp).then_inc(s["p"], 1)
                else:
                    act.wait_ge(s["mx"], a.at.get("mx", 0) + j + 1)
                    c = 2 * (n % 2) + j
                    src = SN[:, n % 2, j, :] if a.att == "na" else score_bank(a, j)[:, :nk]
                    A(PB[:, n % 2, j, :nk], src, ACT.Exp, bias=ST[:, 16 + c:17 + c],
                      accum_out=ST[:, 20 + c:21 + c]).then_inc(s["p"], 1)

        for st in plan:
            k = st.kind
            if k == "unit":
                split_hi(st.u + 1)
                evacuate(st)
            elif k == "tx":
                for f in range(st.nf):
                    act.wait_ge(s["tx_ps"], st.n0 + f + 1)
                    src, dst = TXB[(st.n0 + f) % 4][:, :st.T * P], st.dh[:, f, :]
                    if "norm" in st.kw:
                        src, dst = tokens_first(st, f, src, st.dh)
                    if st.perm:
                        src = src.rearrange("p (b c r) -> p b c r", b=4, c=16)
                        dst = dst.rearrange("p (r b c) -> p b c r", r=8, b=4)
                    scale = st.const if st.scale is None else vec(st.scale + f)
                    A(dst, src, ACT.Copy, scale=scale).then_inc(s["tx_hi"], 1)
            elif k == "rms":
                for t in range(TT):
                    if "ready" in st.kw:
                        act.wait_ge(st.kw["ready"][t], 16)
                    elif st.src is YT:
                        wait(act, "o", st.at)
                    else:
                        wait(act, "evD", st.at, int(t < 2))
                    if st.dst is YT:
                        dump = PB[:, t // 2, t % 2, :]
                    else:
                        dump = XN[:, t, :] if t >= 2 or "ready" in st.kw else PB[:, t, :, :].rearrange("p a b -> p (a b)")
                    ins = A(dump, st.src[:, t, :], ACT.Square, accum_out=ST[:, t:t + 1])
                link(ins)
                A(ST[:, 4:8], ST[:, 0:4], ACT.Sqrt, scale=1.0 / st.d, bias=eps6).then_inc(s["sd"], 1)
                if "ready" in st.kw:
                    split_hi(0)
            elif k == "ln":
                layer_norm_act(act, st.end)
            elif k == "lgate":
                for c in range(4):
                    for w, dst in enumerate((LR, LI)):
                        act.wait_ge(s["gmm"], 2 * c + w + 1)
                        A(dst[:, c, :], (SB, TR)[c % 2][w][:, :], ACT.Sigmoid,
                          bias=vec((V_BRG, V_BIG)[w] + c)).then_inc(s["sig"], 1)
            elif k == "ldecay":
                link(A(ST[:, 32:36], vec(V_LAM, 4), ACT.Abs))
                link(A(ST[:, 32:36], ST[:, 32:36], ACT.Exp, scale=-1.0))
                link(A(ST[:, 36:40], vec(V_LAM, 4), ACT.Relu, scale=-1.0))
                A(ST[:, 32:36], ST[:, 32:36], ACT.Ln, bias=one).then_inc(s["lexp"], 1)
                act.wait_ge(s["lgl"], 1)
                act.wait_ge(s["sig"], 8)
                act.wait_ge(s["conv"], 1)
                for c in range(4):
                    A(LTH[:, c, :], LR[:, c, :], ACT.Tanh, scale=ST[:, 40 + c:41 + c])
                for c in range(4):
                    ins = A(LR[:, c, :], LR[:, c, :], ACT.Exp, scale=ST[:, 44 + c:45 + c])
                ins.then_inc(s["lt"], 1)
            elif k == "lroot":
                A(LG[:, :, :], LG[:, :, :], ACT.Gelu_apprx_tanh).then_inc(s["lsq"], 1)
                act.wait_ge(s["lm2"], 1)
                A(LTH[:, :, :], LTH[:, :, :], ACT.Sqrt).then_inc(s["lsq"], 1)
            elif k == "lsquare":
                act.wait_ge(s["lrec"], 1)
                wait(act, "res", st.after.end)
                A(YSQ[:, :, :], YL_[:, :, :], ACT.Square).then_inc(s["ysq"], 1)
            elif k == "lnorm":
                act.wait_ge(s["ysum"], 1)
                A(RBC[:, :], LIN[0][:, :], ACT.Sqrt, scale=1.0 / 512, bias=eps6).then_inc(s["ysd"], 1)
                act.preload_act_table_set("natural_log_exp_and_others")
            elif k == "lsplit":
                act.wait_ge(s["yn"], 1)
                for c in range(4):
                    A(XH[:, c, :], YL_[:, c, :], ACT.Copy, scale=vec(V_GLRU + c)).then_inc(s["yhi"], 1)
            elif k == "rope":
                act.wait_ge(s["rms_q"], st.half + 1)
                A(ST[:, 114:124], ST[:, 104:114], ACT.Sqrt, bias=eps6).then_inc(s["rsd_q"], 1)
            elif k == "logexp":
                act.preload_act_table_set("natural_log_exp_and_others")
            elif k == "S" and st.att == "stick":
                pre_scores(st)
            elif k == "X":
                exponentials(st.a)
            elif k == "C":
                act.wait_ge(s["tr"], st.a.n + 1)
                if st.a.n:
                    act.wait_ge(s["pv"], st.a.n)
                for o, i in pieces(st.a, 0):
                    ins = A(o, i, ACT.Copy)
                ins.then_inc(s["ptA"], 1)
            elif k == "msplit":
                wait(act, "evD", st.at)
                wait(act, "res", st.at)
                for f in range(KT):
                    A(XH[:, f, :], MG[:, f, :], ACT.Copy).then_inc(s["ms_hi"], 1)
        experts_act(act, chain)

    @block.vector
    def _(dve):
        chain = Chain(dve, "dve_chain")
        link = chain.link
        V = nc.vector
        dve.wait_ge(consts_in, 32)

        def split_lo(u):
            if u >= len(units):
                return
            n = units[u].K * UC
            dve.wait_ge(s["w_hi"], u + 1)
            V.tensor_tensor(WL[:, u % 2, :n], RAW[:, u % 2, :n], WH[:, u % 2, :n].bitcast(F32),
                            ALU.subtract).then_inc(s["w_lo"], 1)

        def evacuate(st):
            for r, who in enumerate(st.who):
                if who != "dve":
                    continue
                n = st.r0 + r
                bank = LIN[lin_of[n]]
                dve.wait_ge(s["res"], n + 1)
                if st.evac in ("accX", "mixX"):
                    xs = X[:, 2 * r:2 * r + 2, st.c0:st.c0 + UC]
                if st.evac == "ffn":
                    f = st.kw["f"]
                    dve.wait_ge(s["evA"], res_shares[n][0])
                    V.tensor_tensor(FP[:, f % 2, :], bank[:, :], FG[:, f % 2, :], ALU.mult).then_inc(s["evD"], 1)
                    dve.wait_ge(s["evD"], res_shares[n][1])
                    dve.wait_ge(s["act_hi"], st.end["act_hi"])
                    V.tensor_tensor(AL[:, f, :], FP[:, f % 2, :], AH[:, f, :].bitcast(F32),
                                    ALU.subtract).then_inc(s["act_lo"], 1)
                elif st.evac == "accX":
                    V.tensor_tensor(xs, shaped(st, bank), xs, ALU.add).then_inc(s["evD"], 1)
                elif st.evac == "mixX":
                    dve.wait_ge(xre_in, 16)
                    V.scalar_tensor_tensor(xs, xs, ALPHA, shaped(st, bank), ALU.mult, ALU.add).then_inc(s["evD"], 1)
                    if st is last_mix and r == 0:
                        dve.wait_ge(s["evD"], res_shares[n][1])
                        layer_norm_stats(link, (0, 1))
                elif st.evac == "branch":
                    dve.wait_ge(s["evA"], st.at["evA"])
                    m, g = MG[:, 2 * st.kw["j"] + r, :], GT[:, r, :]
                    if st.kw["g"] == 0:
                        V.tensor_tensor(m, bank[:, :], g, ALU.mult).then_inc(s["evD"], 1)
                    else:
                        link(V.tensor_tensor(g, bank[:, :], g, ALU.mult))
                        V.tensor_tensor(m, m, g, ALU.add).then_inc(s["evD"], 1)
                else:
                    V.tensor_copy(st.dst(r), shaped(st, bank)).then_inc(s["evD"], 1)

        def weights(a):
            n, v = a.n, [0, 0]
            for i in range(5):
                for j in range(2):
                    nk = a.nkt[j] * P
                    bank, e, d = score_bank(a, j)[:, :nk], SE[:, n % 2, j, :nk], slice(nk - P, nk)
                    ed, sp = SE[:, n % 2, j, d], SP_[:, j, :nk]
                    if i:
                        chain.need(v[j])
                    if i == 0:
                        dve.wait_ge(s["e_ab"], 2 * n + j + 1)
                        ins = V.scalar_tensor_tensor(sp, bank, 0.0, e, ALU.max, ALU.add)
                    elif i == 1:
                        ins = V.tensor_tensor(SP_[:, j, d], SP_[:, j, d], CST[:, C_LT:C_LT + P], ALU.mult)
                    elif i == 2:
                        ins = V.tensor_tensor_scan(SC[:, j, nk - 1::-1], ones[:, 0:1].to_broadcast([P, nk]),
                                                   SP_[:, j, nk - 1::-1], 0.0, ALU.mult, ALU.add)
                    elif i == 3:
                        ins = V.tensor_tensor(e, bank, SC[:, j, :nk], ALU.subtract)
                    else:
                        V.tensor_tensor(ed, ed, CST[:, C_NEG:C_NEG + P], ALU.add).then_inc(s["st_d"], 1)
                        continue
                    v[j] = chain.sign(ins)

        def maxima(a):
            n, v = a.n, [0, 0]
            for i in range(0 if a.att == "na" else 2, 4):
                for j in range(2):
                    c = 2 * (n % 2) + j
                    src = SN[:, n % 2, j, :] if a.att == "na" else score_bank(a, j)[:, :a.nkt[j] * P]
                    sn, cb = SN[:, n % 2, j, :].rearrange("p (r w) -> p r w", r=8), a.qt[j]
                    if i == (0 if a.att == "na" else 2):
                        dve.wait_ge(s["qk"], 2 * n + j + 1)
                        if n >= 2:
                            dve.wait_ge(s["p"], 2 * n + j - 3)
                    else:
                        chain.need(v[j])
                    if i == 0:
                        dve.wait_ge(b48_in, 16 * 8)
                        o = (16, 8, 8, 0)[cb]
                        ins = V.tensor_tensor(sn, score_bank(a, j)[:, :2 * P].rearrange("p (r w) -> p r w", r=8),
                                              B48[:, a.h, :, o:o + 32], ALU.add)
                    elif i == 1:
                        mask = CST[:, C_NAM + 32 * min(cb, 1) + 32 * (cb == 3):][:, :32]
                        ins = V.tensor_tensor(sn, sn, mask.unsqueeze(1).to_broadcast([P, 8, 32]), ALU.add)
                    elif i == 2:
                        ins = V.tensor_reduce(ST[:, 28 + c:29 + c], src, AX, ALU.max)
                    else:
                        V.tensor_scalar(ST[:, 16 + c:17 + c], ST[:, 28 + c:29 + c], -1.0, None,
                                        ALU.mult).then_inc(s["mx"], 1)
                        continue
                    v[j] = chain.sign(ins)

        def output(a):
            n = a.n
            dv = P if a.att == "mem" else 64
            y = YT if a.att == "stick" else YN
            if a.att == "stick":
                dve.wait_ge(s["pv"], n + 1)
                V.tensor_copy(y[:, a.qt[0]:a.qt[0] + 2, 64 * a.h:64 * a.h + 64],
                              PV[:, 0:2 * P].rearrange("p (j c) -> p j c", j=2)[:, :, :64]).then_inc(s["o"], 1)
                return
            c = 2 * (n % 2)
            dve.wait_ge(s["p"], 2 * n + 2)
            dve.wait_ge(s["o"], n)
            link(V.reciprocal(ST[:, 24:26], ST[:, 20 + c:22 + c]))
            dve.wait_ge(s["pv"], n + 1)
            for j in range(2):
                ins = V.tensor_scalar(y[:, a.qt[j], dv * a.h:dv * a.h + dv], PV[:, P * j:P * j + dv],
                                      ST[:, 24 + j:25 + j], None, ALU.mult)
            ins.then_inc(s["o"], 1)

        def rope(st):
            H = 10
            xn, t12, _ = rope_views()
            wait(dve, "evA", st.at)
            t = st.half
            if t:
                dve.wait_ge(s["rope_p"], t)
            q = GQT[:, t, :].rearrange("p (h c) -> p h c", h=8)
            kk = KVT[:, t, 0:128].rearrange("p (h c) -> p h c", h=2)
            link(V.tensor_tensor(xn[:, 0:8, :], q, q, ALU.mult))
            link(V.tensor_tensor(xn[:, 8:10, :], kk, kk, ALU.mult))
            link(V.tensor_reduce(ST[:, 104:114], xn, AX, ALU.add))
            V.tensor_scalar(ST[:, 104:114], ST[:, 104:114], 1.0 / 64, None, ALU.mult).then_inc(s["rms_q"], 1)
            dve.wait_ge(s["rsd_q"], t + 1)
            link(V.reciprocal(ST[:, 104:114], ST[:, 114:124]))
            r = ST[:, 104:114].unsqueeze(2)
            link(V.tensor_tensor(xn[:, 0:8, :], q, r[:, 0:8].to_broadcast([P, 8, 64]), ALU.mult))
            link(V.tensor_tensor(xn[:, 8:10, :], kk, r[:, 8:10].to_broadcast([P, 2, 64]), ALU.mult))
            link(V.tensor_tensor(xn[:, 0:8, :], xn[:, 0:8, :],
                                 vec(V_GQ, 64).unsqueeze(1).to_broadcast([P, 8, 64]), ALU.mult))
            V.tensor_tensor(xn[:, 8:10, :], xn[:, 8:10, :],
                            vec(V_GQ + 64, 64).unsqueeze(1).to_broadcast([P, 2, 64]), ALU.mult).then_inc(s["rxn"], 1)
            dve.wait_ge(s["rxn"], t + 1)
            ins = rotate(V, link, t, t12, 0, (C_COS, C_SIN), ALU.subtract)
            ins.then_inc(s["rope"], 1)

        for st in plan:
            k = st.kind
            if k == "unit":
                split_lo(st.u + 1)
                evacuate(st)
            elif k == "tx" and not st.f32:
                for f in range(st.nf):
                    dve.wait_ge(s["tx_hi"], tx_free[st.n0 + f][0])
                    src, hi, lo = TXB[(st.n0 + f) % 4][:, :st.T * P], st.dh[:, f, :].bitcast(F32), st.dl[:, f, :]
                    if "norm" in st.kw:
                        bank = src
                        src, hi = tokens_first(st, f, bank, st.dh)
                        src, lo = tokens_first(st, f, bank, st.dl)
                        hi = hi.bitcast(F32)
                    if st.perm:
                        src = src.rearrange("p (b c r) -> p b c r", b=4, c=16)
                        hi, lo = (v.rearrange("p (r b c) -> p b c r", r=8, b=4) for v in (hi, lo))
                    if st.scale is None:
                        ins = V.tensor_tensor(lo, src, hi, ALU.subtract)
                    else:
                        ins = V.scalar_tensor_tensor(lo, src, vec(st.scale + f), hi, ALU.mult, ALU.subtract)
                    ins.then_inc(s["tx_lo"], 1)
            elif k == "rms":
                wait(dve, "sd", st.end)
                V.reciprocal(ST[:, 8:12], ST[:, 4:8]).then_inc(s["rc"], 1)
                wait(dve, "rc", st.end)
                if st.grow is not None:
                    dve.wait_ge(rows_in, 16)
                for t in range(TT):
                    r = ST[:, 8 + t:9 + t]
                    if st.grow is None:
                        ins = V.tensor_scalar(st.dst[:, t, :], st.src[:, t, :], r, None, ALU.mult)
                    else:
                        ins = V.scalar_tensor_tensor(st.dst[:, t, :], st.src[:, t, :], r, st.grow[:, :],
                                                     ALU.mult, ALU.mult)
                    ins.then_inc(s["nrm"], 1)
                if "ready" in st.kw:
                    split_lo(0)
            elif k == "ln":
                wait(dve, "evD", st.at)
                layer_norm_dve(dve, link, st.end, st.rows, rows_in, 48, tiles=(2, 3))
            elif k == "conv":
                wait(dve, "evA", st.after.end)
                wait(dve, "evD", st.after.end)
                link(V.memset(LX[:, :, 0:3], 0.0))
                for c in range(4):
                    link(V.tensor_scalar(LC[:, c, :], LX[:, c, 0:S], vec(V_CW + 4 * c), vec(V_CB + c),
                                         ALU.mult, ALU.add))
                    for i in range(1, 4):
                        ins = V.scalar_tensor_tensor(LC[:, c, :], LX[:, c, i:i + S], vec(V_CW + 4 * c + i),
                                                     LC[:, c, :], ALU.mult, ALU.add)
                        if (c, i) != (3, 3):
                            link(ins)
                ins.then_inc(s["conv"], 1)
            elif k == "ldecay":
                dve.wait_ge(s["lexp"], 1)
                link(V.tensor_tensor(ST[:, 32:36], ST[:, 32:36], ST[:, 36:40], ALU.add))
                V.tensor_scalar(ST[:, 40:44], ST[:, 32:36], 8.0, None, ALU.mult)
                V.tensor_scalar(ST[:, 44:48], ST[:, 32:36], -8.0, None, ALU.mult).then_inc(s["lgl"], 1)
                dve.wait_ge(s["lt"], 1)
                link(V.tensor_tensor(TMP[:, :, :], LR[:, :, :], LR[:, :, :], ALU.mult))
                V.scalar_tensor_tensor(LTH[:, :, :], TMP[:, :, :], 1.0, LTH[:, :, :],
                                       ALU.add, ALU.mult).then_inc(s["lm2"], 1)
            elif k == "lroot":
                link(V.tensor_tensor(LI[:, :, :], LI[:, :, :], LC[:, :, :], ALU.mult))
                dve.wait_ge(s["lsq"], 2)
                V.tensor_tensor(LI[:, :, :], LI[:, :, :], LTH[:, :, :], ALU.mult).then_inc(s["lin"], 1)
            elif k == "lscan":
                dve.wait_ge(s["lin"], 1)
                for c in range(4):
                    ins = V.tensor_tensor_scan(TMP[:, c, :], LR[:, c, :], LI[:, c, :], 0.0, ALU.mult, ALU.add)
                link(ins)
                V.tensor_tensor(YL_[:, :, :], TMP[:, :, :], LG[:, :, :], ALU.mult).then_inc(s["lrec"], 1)
            elif k == "lnorm":
                dve.wait_ge(s["ysd"], 1)
                link(V.reciprocal(RBC[:, :], RBC[:, :]))
                V.tensor_tensor(YL_[:, :, :], YL_[:, :, :], RBC[:, :].unsqueeze(1).to_broadcast([P, 4, S]),
                                ALU.mult).then_inc(s["yn"], 1)
            elif k == "lsplit":
                dve.wait_ge(s["yn"], 1)
                for c in range(4):
                    dve.wait_ge(s["yhi"], c + 1)
                    V.scalar_tensor_tensor(XL[:, c, :], YL_[:, c, :], vec(V_GLRU + c), XH[:, c, :].bitcast(F32),
                                           ALU.mult, ALU.subtract).then_inc(s["ylo"], 1)
            elif k == "W":
                weights(st.a)
            elif k == "S" and st.att != "stick":
                maxima(st)
            elif k == "C" and st.counts["ptD"]:
                dve.wait_ge(s["tr"], st.a.n + 1)
                if st.a.n:
                    dve.wait_ge(s["pv"], st.a.n)
                for o, i in pieces(st.a, 1):
                    ins = V.tensor_copy(o, i)
                ins.then_inc(s["ptD"], 1)
            elif k == "O":
                output(st.a)
            elif k == "rope":
                rope(st)
            elif k == "msplit":
                for f in range(KT):
                    wait(dve, "ms_hi", st.at, -f - 1)
                    V.tensor_tensor(XL[:, f, :], MG[:, f, :], XH[:, f, :].bitcast(F32),
                                    ALU.subtract).then_inc(s["ms_lo"], 1)
        experts_dve(dve, chain)

    @block.tensor
    def _(pe):
        T = nc.tensor
        pe.wait_ge(consts_in, 32)

        def product(st):
            XHs, XLs = SRC[st.src]
            wh, wl = (w[:, st.u % 2, :st.K * UC].rearrange("p (k c) -> p k c", c=UC) for w in (WH, WL))
            pe.wait_ge(s["w_lo"], st.u + 1)
            if st.src == "a":
                wait(pe, "act_lo", st.at)
            wait(pe, "ylo", st.at)
            i0 = plan.index(st)
            fresh = plan[i0 - 1] if i0 else None
            if fresh is not None and fresh.kind == "msplit":
                step_by = (s["ms_lo"], fresh.at.get("ms_lo", 0) + 1, 0)
            elif fresh is not None and fresh.kind == "tx" and fresh.kw.get("feeds") == st.src:
                step_by = (s["tx_lo"], fresh.at.get("tx_lo", 0) + 1, fresh.kw.get("k0", 0))
            else:
                step_by = None
            if step_by is None:
                wait(pe, "tx_lo", st.at)
                wait(pe, "ms_lo", st.at)
            else:
                wait(pe, "tx_lo", fresh.at)
                wait(pe, "ms_lo", fresh.at)
            waited = set()

            def tile_there(k):
                if step_by and k not in waited and k >= step_by[2]:
                    waited.add(k)
                    pe.wait_ge(step_by[0], step_by[1] + k - step_by[2])

            for r in range(len(st.who)):
                n = st.r0 + r
                bank = LIN[lin_of[n]]
                bank_free(pe, st, n)
                if st.mode == "F":
                    c = slice(P * r, P * r + P)
                    for k in range(st.K):
                        tile_there(k)
                        hi, lo = XHs[:, k, :st.nt], XLs[:, k, :st.nt]
                        T.matmul(bank[:, :st.nt], wh[:, k, c], hi, start=k == 0, stop=False)
                        T.matmul(bank[:, :st.nt], wh[:, k, c], lo, start=False, stop=False)
                        ins = T.matmul(bank[:, :st.nt], wl[:, k, c], hi, start=False, stop=k == st.K - 1)
                else:
                    for i in range(2):
                        t = slice((2 * r + i) * P, (2 * r + i + 1) * P)
                        o = bank[:, i * UC:i * UC + UC]
                        for k in range(st.K):
                            tile_there(k)
                            T.matmul(o, XHs[:, k, t], wh[:, k, :], start=k == 0, stop=False)
                            T.matmul(o, XHs[:, k, t], wl[:, k, :], start=False, stop=False)
                            ins = T.matmul(o, XLs[:, k, t], wh[:, k, :], start=False, stop=k == st.K - 1)
                ins.then_inc(s["res"], 1)

        def banks_idle(st):
            for name in ("ptA", "ptD", "tx_hi", "tx_lo", "sig"):
                wait(pe, name, st.at)

        def qk(a, j):
            b = (a.h % 2) * 64
            h2 = a.h // 2
            qc = slice(a.qt[j] * P, a.qt[j] * P + P)
            if a.att == "stick":
                return QT[b:b + 64, h2, qc], KTT[b:b + 64, h2, 0:a.nkt[j] * P]
            if a.att == "na":
                bs = (0, 8, 24, 32)[a.qt[j]]
                return QT[b:b + 64, h2, qc], KTT[b:b + 64, h2, :].rearrange("p (r c) -> p r c", r=8)[:, :, bs:bs + 32]
            if a.att == "gqa":
                return QG[b:b + 64, h2, qc], KG[b:b + 64, a.h // 4, :]
            return QM[:, a.h, qc], MKT[:, a.h, :]

        later = []

        def scores(a, j):
            q, kk = qk(a, j)
            o = score_bank(a, j)[:, 0:a.nkt[j] * P]
            if a.att == "na":
                o = o.rearrange("p (r c) -> p r c", r=8)
            score_bank_free(pe, a, j)
            T.matmul(o, q, kk, start=True, stop=True).then_inc(s["qk"], 1)

        def flush():
            while later:
                scores(later.pop(), 1)

        def values(a, j, kt):
            if a.att == "stick":
                return VT[:, kt, 64 * a.h:64 * a.h + 64]
            if a.att == "na":
                return VB[:, a.qt[j], kt, 64 * a.h:64 * a.h + 64]
            if a.att == "gqa":
                return KVT[:, kt, 128 + 64 * (a.h // 4):192 + 64 * (a.h // 4)]
            return MV[:, kt, P * a.h:P * a.h + P]

        for st in plan:
            k = st.kind
            if k == "unit":
                flush()
                product(st)
            elif k == "tx":
                if "landed" in st.kw:
                    pe.wait_ge(*st.kw["landed"])
                for name in ("o",) if "norm" in st.kw else ("nrm", "o"):
                    wait(pe, name, st.at)
                if not st.perm:
                    wait(pe, "rope", st.at)
                    wait(pe, "rope_p", st.at)
                banks_idle(st)
                wait(pe, "p", st.at)
                wait(pe, "st_d", st.at)
                for f in range(st.nf):
                    n = st.n0 + f
                    if f >= 4:
                        hi, lo = tx_free[n - 4]
                        pe.wait_ge(s["tx_hi"], hi)
                        if lo:
                            pe.wait_ge(s["tx_lo"], lo)
                    if "norm" in st.kw:
                        t, g = divmod(f, 2)
                        wait(pe, "nrm", st.kw["norm"].at, -t - 1)
                        for i in range(4):
                            c = slice((4 * g + i) * P, (4 * g + i + 1) * P)
                            ins = T.transpose(TXB[n % 4][:, i * P:i * P + P], st.src[:, t, c], ident)
                        ins.then_inc(s["tx_ps"], 1)
                        if st is tx2 and g == 1 and t:
                            pe.wait_ge(wr_in, 16)
                            wait(pe, "o", total)
                            affinities(t - 1)
                        continue
                    for t in range(st.T):
                        ins = T.transpose(TXB[n % 4][:, t * P:t * P + P], st.src[:, t, f * P:f * P + P], ident)
                    ins.then_inc(s["tx_ps"], 1)
            elif k == "lgate":
                pe.wait_ge(bd_in, 64)
                pe.wait_ge(s["conv"], 1)
                banks_idle(st)
                for c in range(4):
                    for w in range(2):
                        if c >= 2:
                            pe.wait_ge(s["sig"], 2 * (c - 2) + w + 1)
                        T.matmul((SB, TR)[c % 2][w][:, :], BD[:, w, c, :], LC[:, c, :],
                                 start=True, stop=True).then_inc(s["gmm"], 1)
            elif k == "lnorm":
                pe.wait_ge(s["ysq"], 1)
                for c in range(4):
                    ins = T.matmul(LIN[0][:, :], ones, YSQ[:, c, :], start=c == 0, stop=c == 3)
                ins.then_inc(s["ysum"], 1)
            elif k == "S":
                wait(pe, "evA", st.after.end)
                wait(pe, "evD", st.after.end)
                wait(pe, "band", st.after.end)
                wait(pe, "tx_hi", st.after.end)
                for name in ("sig", "tx_hi", "tx_lo"):
                    wait(pe, name, st.at)
                flush()
                later.append(st)
                scores(st, 0)
                if st.att in ("stick", "na"):
                    flush()
            elif k == "T":
                flush()
                wait(pe, "p", st.at)
                banks_idle(st)
                for j in range(2):
                    for kt in range(st.a.nkt[j]):
                        c = (kt % 2) * 256 + j * P
                        ins = T.transpose(TR[kt // 2][:, c:c + P], PB[:, st.a.n % 2, j, kt * P:kt * P + P], ident)
                ins.then_inc(s["tr"], 1)
            elif k == "O":
                a = st.a
                wait(pe, "ptA", a.c.end)
                wait(pe, "ptD", a.c.end)
                wait(pe, "o", st.at)
                dv = P if a.att == "mem" else 64
                for j in range(2):
                    for kt in range(a.nkt[j]):
                        ins = T.matmul(PV[:, j * P:j * P + dv], PT[:, kt, j * P:j * P + P], values(a, j, kt),
                                       start=kt == 0, stop=kt == a.nkt[j] - 1)
                ins.then_inc(s["pv"], 1)
                flush()
        experts_pe(pe)
    ctx.close()


def _constants():
    c = np.zeros((P, C_N), np.float32)
    row, col = np.arange(P)[:, None], np.arange(P)[None, :]
    c[:, C_ID:C_ID + P] = row == col
    c[:, C_LT:C_LT + P] = col < row
    c[:, C_NEG:C_NEG + P] = np.where(col < row, 0.0, NEG)
    for i, (cb, bs) in enumerate(((0, 0), (1, 8), (3, 32))):
        q = cb * 16 + np.arange(P)[:, None] // 8
        start = np.clip(q - 8, 0, 48)
        k = bs + np.arange(32)[None, :]
        c[:, C_NAM + 32 * i:C_NAM + 32 * i + 32] = np.where((k >= start) & (k < start + 16), 0.0, NEG)
    c[:, C_ONE:C_ONE + P] = 1.0
    c[:, C_TC:C_TC + 4] = np.arange(P)[:, None] + P * np.arange(4)[None, :]
    c[:, C_EPS6], c[:, C_EPS5] = 1e-6, 1e-5
    t = np.arange(S)
    inv = np.float32(10000.0) ** (-np.arange(0, 32, 2, dtype=np.float32) / np.float32(32))
    ang = np.concatenate([(t // 64).astype(np.float32)[:, None] * inv, (t % 64).astype(np.float32)[:, None] * inv], 1)
    for at, f in ((C_COS, np.cos), (C_SIN, np.sin)):
        c[:, at:at + 128] = f(ang).astype(np.float32).reshape(TT, P, 32).transpose(1, 0, 2).reshape(P, 128)
    c[:, C_IOTA:C_IOTA + S] = t[None, :]
    return c


def kernel(**inputs):
    import concourse.bacc as _bacc
    from concourse.bass_utils import run_bass_kernel_spmd as _run

    a = {k: np.ascontiguousarray(v) for k, v in inputs.items()}

    def cols(v):
        return v.reshape(-1, P).T

    conv = a["conv_w"][0].reshape(4, 4, P).transpose(2, 1, 0).reshape(P, 16)
    vecs = np.concatenate(
        [cols(a["norm_mix"]), cols(a["norm_ffn"]), conv, cols(a["conv_b"]), cols(a["b_rg"]), cols(a["b_ig"]),
         cols(a["lru_lambda"]), cols(a["norm_lru_out"]), cols(a["norm_att_out"]), cols(a["b_gate_2"]),
         np.tile(a["gqa_q_gain_2"], (P, 1)), np.tile(a["gqa_k_gain_2"], (P, 1))], axis=1)
    rows = np.concatenate([a["norm_final"][None], a["ln1_g_2"], a["ln1_b_2"], a["ln2_g_2"], a["ln2_b_2"]])
    rpb = np.concatenate([np.zeros(16, np.float32), a["na_rpb_2"].reshape(-1), np.zeros(64, np.float32)])
    arrays = dict(
        x=a["x"], w_in=a["w_in"], w_out=a["w_out"], w_ffn_in=a["w_ffn_in"], w_ffn_out=a["w_ffn_out"],
        mem=a["mem_2"], w_in2=a["w_in_2"], w_memkv=a["w_mem_kv_2"], w_branch=a["w_branch_2"],
        w_out2=a["w_out_2"], w_router=a["w_router_2"], w_gu=a["w_gate_up_2"], w_down=a["w_down_2"],
        w_rg=a["w_rg"], w_ig=a["w_ig"], rows=rows, rpb=rpb, vecs=vecs, consts=_constants())
    arrays = {k: np.ascontiguousarray(v) for k, v in arrays.items()}
    nc = _bacc.Bacc("TRN2", target_bir_lowering=False, num_devices=1)
    args = {k: nc.dram_tensor(k, v.shape, F32, kind="ExternalInput").ap() for k, v in arrays.items()}
    args["out"] = nc.dram_tensor("out", (1, S, D), F32, kind="ExternalOutput").ap()
    build(nc, **args)
    return _run(nc, [arrays], core_ids=[0]).results[0]["out"]
```
